# Optimizing a Trainium2 kernel written in Bass

```python
import math
import jax, jax.numpy as jnp
from jax import lax
import numpy as np

D_MODEL = 1024
BATCH = 1
SEQ = 1024
DEPTH = 1
DEC_BATCH = 8
DEC_SEQ = 1
PAST_LEN = 8192
PAGE_SIZE = 128

D_MIX = D_MODEL
CONV_CH = D_MIX // 2
GDN_HEADS = 4
GDN_HEAD_DIM = (D_MIX - CONV_CH) // GDN_HEADS
GDN_DIM = GDN_HEADS * GDN_HEAD_DIM
CONV_A_K = 3
CONV_QKV_K = 4
CHUNK = 64
N_META = 16
N_GROUPS = 4
EXPERTS_PER_GROUP = 8
N_EXPERTS = N_GROUPS * EXPERTS_PER_GROUP
TOP_K = 2
D_FF = 256
EPS = 1e-6
IN_SIZES = (CONV_CH, CONV_CH, CONV_CH, GDN_DIM, GDN_DIM, GDN_DIM, GDN_DIM, GDN_HEADS, GDN_HEADS)
N_IN = sum(IN_SIZES)

kernel_name = "hymba_conv_gdn_hmoe_step"

def _rmsnorm(x, w):
    x32 = x.astype(jnp.float32)
    y = x32 * lax.rsqrt(jnp.mean(x32 * x32, axis=-1, keepdims=True) + EPS) * w.astype(jnp.float32)
    return y.astype(x.dtype)

def _l2norm(x):
    return x * lax.rsqrt(jnp.sum(x * x, axis=-1, keepdims=True) + EPS)

def _causal_dwconv(x, buf, w):
    width = w.shape[0]
    length = x.shape[1]
    xp = jnp.concatenate([buf.astype(x.dtype), x], axis=1)
    y = xp[:, 0:length] * w[0]
    for i in range(1, width):
        y = y + xp[:, i:i + length] * w[i]
    return y, xp[:, xp.shape[1] - (width - 1):]

def _gdn_chunks(q, k, v, g, beta, s0, chunk):
    b, length, h, dk = q.shape
    dv = v.shape[-1]
    n = length // chunk

    def to_chunks(t):
        t = t.reshape((b, n, chunk, h) + t.shape[3:])
        return jnp.moveaxis(jnp.moveaxis(t, 1, 0), 3, 2)

    idx = jnp.arange(chunk)
    causal = idx[:, None] >= idx[None, :]
    strict = idx[:, None] > idx[None, :]
    eye = jnp.eye(chunk, dtype=jnp.float32)

    def step(s, inp):
        qc, kc, vc, gc, bc = inp
        gcum = jnp.cumsum(gc, axis=-1)
        decay = jnp.exp(jnp.where(causal, gcum[..., :, None] - gcum[..., None, :], -jnp.inf))
        kb = kc * bc[..., None]
        lmat = jnp.where(strict, jnp.einsum('bhid,bhjd->bhij', kb, kc) * decay, 0.0)
        rhs = jnp.concatenate([vc * bc[..., None], kb * jnp.exp(gcum)[..., None]], axis=-1)
        sol = lax.linalg.triangular_solve(lmat + eye, rhs, left_side=True, lower=True,
                                          unit_diagonal=True)
        u = sol[..., :dv] - jnp.einsum('bhck,bhkv->bhcv', sol[..., dv:], s)
        attn = jnp.where(causal, jnp.einsum('bhik,bhjk->bhij', qc, kc) * decay, 0.0)
        o = (jnp.einsum('bhck,bhkv->bhcv', qc * jnp.exp(gcum)[..., None], s)
             + jnp.einsum('bhij,bhjv->bhiv', attn, u))
        g_last = gcum[..., -1:]
        s_new = (s * jnp.exp(g_last)[..., None]
                 + jnp.einsum('bhck,bhcv->bhkv', kc * jnp.exp(g_last - gcum)[..., None], u))
        return s_new, o

    s, o = lax.scan(step, s0, (to_chunks(q), to_chunks(k), to_chunks(v), to_chunks(g), to_chunks(beta)))
    o = jnp.moveaxis(jnp.moveaxis(o, 2, 3), 0, 1).reshape(b, length, h, dv)
    return o, s

def _moe(h, rg_w, rg_b, re_w, re_b, w_gate, w_up, w_down):
    shp = h.shape
    h2 = h.reshape(-1, shp[-1])
    t = h2.shape[0]
    lg = (h2 @ rg_w).astype(jnp.float32) + rg_b.astype(jnp.float32)
    pg = jax.nn.softmax(lg, axis=-1)
    _, gsel = lax.top_k(lg, 1)
    le = ((h2 @ re_w).astype(jnp.float32) + re_b.astype(jnp.float32)).reshape(t, N_GROUPS, EXPERTS_PER_GROUP)
    le_g = jnp.take_along_axis(le, gsel[:, :, None], axis=1)[:, 0]
    ev, ei = lax.top_k(le_g, TOP_K)
    wts = jnp.take_along_axis(pg, gsel, axis=1) * jax.nn.softmax(ev, axis=-1)
    eid = gsel * EXPERTS_PER_GROUP + ei
    combine = jnp.sum(jax.nn.one_hot(eid, N_EXPERTS, dtype=jnp.float32) * wts[..., None], axis=1)
    combine = combine.astype(h.dtype)
    out = jnp.zeros_like(h2)
    for e in range(N_EXPERTS):
        he = jax.nn.silu(h2 @ w_gate[e]) * (h2 @ w_up[e])
        out = out + combine[:, e:e + 1] * (he @ w_down[e])
    return out.reshape(shp)

def _layer(x, buf_a, buf_qkv, s0, segments, norm_mix, w_in, conv_a_w, conv_qkv_w, a_log, dt_bias,
           o_norm, w_out, norm_ffn, rg_w, rg_b, re_w, re_b, w_gate, w_up, w_down):
    b, length, _ = x.shape
    h = _rmsnorm(x, norm_mix)
    z = h @ w_in
    cuts = [int(c) for c in np.cumsum(IN_SIZES)[:-1]]
    c_b, c_c, c_h, _q, _k, _v, gate, a_raw, b_raw = jnp.split(z, cuts, axis=-1)
    ca, new_buf_a = _causal_dwconv(c_c * c_h, buf_a, conv_a_w)
    y_a = c_b * ca
    qkv_raw = z[..., 3 * CONV_CH:3 * CONV_CH + 3 * GDN_DIM]
    qkv, new_buf_qkv = _causal_dwconv(qkv_raw, buf_qkv, conv_qkv_w)
    qkv = jax.nn.silu(qkv).astype(jnp.float32)
    q, k, v = jnp.split(qkv, 3, axis=-1)
    q = _l2norm(q.reshape(b, length, GDN_HEADS, GDN_HEAD_DIM)) * (GDN_HEAD_DIM ** -0.5)
    k = _l2norm(k.reshape(b, length, GDN_HEADS, GDN_HEAD_DIM))
    v = v.reshape(b, length, GDN_HEADS, GDN_HEAD_DIM)
    g = -jnp.exp(a_log.astype(jnp.float32)) * jax.nn.softplus(
        a_raw.astype(jnp.float32) + dt_bias.astype(jnp.float32))
    beta = jax.nn.sigmoid(b_raw.astype(jnp.float32))
    s = s0.astype(jnp.float32)
    outs = []
    start = 0
    for seg_len, chunk in segments:
        sl = slice(start, start + seg_len)
        o_seg, s = _gdn_chunks(q[:, sl], k[:, sl], v[:, sl], g[:, sl], beta[:, sl], s, chunk)
        outs.append(o_seg)
        start += seg_len
    o = jnp.concatenate(outs, axis=1) if len(outs) > 1 else outs[0]
    o = _rmsnorm(o, o_norm) * jax.nn.silu(
        gate.astype(jnp.float32).reshape(b, length, GDN_HEADS, GDN_HEAD_DIM))
    y_b = o.reshape(b, length, GDN_DIM).astype(x.dtype)
    x = x + jnp.concatenate([y_a, y_b], axis=-1) @ w_out
    x = x + _moe(_rmsnorm(x, norm_ffn), rg_w, rg_b, re_w, re_b, w_gate, w_up, w_down)
    return x, new_buf_a, new_buf_qkv, s

def setup_inputs(seed: int = 0) -> dict:
    key = jax.random.key(seed)
    ks = jax.random.split(key, 24)
    f32 = jnp.float32
    nrm = lambda k, shp, sc: jax.random.normal(k, shp, f32) * sc
    dt = jnp.exp(jax.random.uniform(ks[9], (DEPTH, GDN_HEADS), f32, math.log(1e-3), math.log(1e-1)))
    return {
        "x_prompt": nrm(ks[0], (BATCH, SEQ, D_MODEL), 1.0),
        "x_sample": nrm(ks[1], (DEC_BATCH, DEC_SEQ, D_MODEL), 1.0),
        "state_conv_a": nrm(ks[2], (DEPTH, DEC_BATCH, CONV_A_K - 1, CONV_CH), 1.0),
        "state_conv_qkv": nrm(ks[3], (DEPTH, DEC_BATCH, CONV_QKV_K - 1, 3 * GDN_DIM), 1.0),
        "state_ssm": nrm(ks[4], (DEPTH, DEC_BATCH, GDN_HEADS, GDN_HEAD_DIM, GDN_HEAD_DIM), 0.1),
        "meta_tokens": nrm(ks[5], (N_META, D_MODEL), 1.0),
        "norm_mix": 1.0 + nrm(ks[6], (DEPTH, D_MODEL), 0.02),
        "w_in": nrm(ks[7], (DEPTH, D_MODEL, N_IN), D_MODEL ** -0.5),
        "conv_a_w": nrm(ks[8], (DEPTH, CONV_A_K, CONV_CH), CONV_A_K ** -0.5),
        "conv_qkv_w": nrm(ks[10], (DEPTH, CONV_QKV_K, 3 * GDN_DIM), CONV_QKV_K ** -0.5),
        "a_log": jnp.log(jax.random.uniform(ks[11], (DEPTH, GDN_HEADS), f32, 1.0, 16.0)),
        "dt_bias": dt + jnp.log(-jnp.expm1(-dt)),
        "o_norm": 1.0 + nrm(ks[12], (DEPTH, GDN_HEAD_DIM), 0.02),
        "w_out": nrm(ks[13], (DEPTH, D_MIX, D_MODEL), D_MIX ** -0.5),
        "norm_ffn": 1.0 + nrm(ks[14], (DEPTH, D_MODEL), 0.02),
        "router_group_w": nrm(ks[15], (DEPTH, D_MODEL, N_GROUPS), D_MODEL ** -0.5),
        "router_group_b": nrm(ks[16], (DEPTH, N_GROUPS), 0.01),
        "router_expert_w": nrm(ks[17], (DEPTH, D_MODEL, N_EXPERTS), D_MODEL ** -0.5),
        "router_expert_b": nrm(ks[18], (DEPTH, N_EXPERTS), 0.01),
        "w_gate": nrm(ks[19], (DEPTH, N_EXPERTS, D_MODEL, D_FF), D_MODEL ** -0.5),
        "w_up": nrm(ks[20], (DEPTH, N_EXPERTS, D_MODEL, D_FF), D_MODEL ** -0.5),
        "w_down": nrm(ks[21], (DEPTH, N_EXPERTS, D_FF, D_MODEL), D_FF ** -0.5),
        "norm_final": 1.0 + nrm(ks[22], (D_MODEL,), 0.02),
    }

def reference(x_prompt, x_sample, state_conv_a, state_conv_qkv, state_ssm, meta_tokens, norm_mix, w_in,
              conv_a_w, conv_qkv_w, a_log, dt_bias, o_norm, w_out, norm_ffn, router_group_w,
              router_group_b, router_expert_w, router_expert_b, w_gate, w_up, w_down, norm_final):
    dtype = x_prompt.dtype
    xp = jnp.concatenate([jnp.broadcast_to(meta_tokens.astype(dtype)[None], (BATCH, N_META, D_MODEL)),
                          x_prompt], axis=1)
    xs = x_sample
    prompt_segments = ((N_META, N_META), (SEQ, CHUNK))
    sample_segments = ((DEC_SEQ, DEC_SEQ),)
    pa, pq, ps, sa, sq, ss = [], [], [], [], [], []
    for l in range(DEPTH):
        lw = (norm_mix[l], w_in[l], conv_a_w[l], conv_qkv_w[l], a_log[l], dt_bias[l], o_norm[l], w_out[l],
              norm_ffn[l], router_group_w[l], router_group_b[l], router_expert_w[l], router_expert_b[l],
              w_gate[l], w_up[l], w_down[l])
        xp, ba, bq, s = _layer(xp,
                               jnp.zeros((BATCH, CONV_A_K - 1, CONV_CH), dtype),
                               jnp.zeros((BATCH, CONV_QKV_K - 1, 3 * GDN_DIM), dtype),
                               jnp.zeros((BATCH, GDN_HEADS, GDN_HEAD_DIM, GDN_HEAD_DIM), jnp.float32),
                               prompt_segments, *lw)
        pa.append(ba.astype(state_conv_a.dtype))
        pq.append(bq.astype(state_conv_qkv.dtype))
        ps.append(s.astype(state_ssm.dtype))
        xs, ba, bq, s = _layer(xs, state_conv_a[l], state_conv_qkv[l], state_ssm[l], sample_segments, *lw)
        sa.append(ba.astype(state_conv_a.dtype))
        sq.append(bq.astype(state_conv_qkv.dtype))
        ss.append(s.astype(state_ssm.dtype))
    y_prompt = _rmsnorm(xp, norm_final)[:, N_META:]
    y_sample = _rmsnorm(xs, norm_final)
    return (y_prompt, y_sample, jnp.stack(pa), jnp.stack(pq), jnp.stack(ps),
            jnp.stack(sa), jnp.stack(sq), jnp.stack(ss))


_drawn_inputs = setup_inputs


def setup_inputs(seed=0):
    import zlib

    import numpy as np

    out = dict(_drawn_inputs(seed))
    spreads = {}
    factors = {'o_norm': 3.777,
     'norm_ffn': 3.079,
     'router_group_b': 4.957,
     'router_expert_b': 4.272,
     'norm_final': 2.784}
    for name, (base, spread) in spreads.items():
        noise = np.random.default_rng([zlib.crc32(name.encode()), seed]).standard_normal(out[name].shape)
        drawn = base * np.exp(spread * noise) if base else spread * noise
        out[name] = __import__('jax').numpy.asarray(drawn.astype(out[name].dtype))
    for name, factor in factors.items():
        out[name] = (out[name] * factor).astype(out[name].dtype)
    return out
```

```python
import concourse.bass as bass
from concourse import mybir

F32 = mybir.dt.float32
F32R = mybir.dt.float32r
I32 = mybir.dt.int32
U32 = mybir.dt.uint32
ALU = mybir.AluOpType
ACT = mybir.ActivationFunctionType
AX = mybir.AxisListType

P = 128
D = 1024
KD = D // P
SEQ, META, SAMPLES = 1024, 16, 8
PROMPT = SEQ + META
TOK = PROMPT + SAMPLES
ZC = 350
TP = 3 * ZC
TILES = 9
LAST = TOK - 8 * P
TAIL = PROMPT - 8 * P
CA = 4
H = 4
QK = 2 * H
QKV = 3 * H
KA, KQ = 3, 4
NBLK = 28
GRP, EPG, NE = 4, 8, 32
FF = 256
KF = FF // P
C = 96
OV = 21
PARTS = 11
SLOTS = (NE + OV) * C
NOWHERE = 4 * TOK
EPS = 1e-6
RLEN = 3 + PROMPT + SAMPLES * KQ
QLEN = RLEN - (KQ - 1)
ALEN = 2 + PROMPT + SAMPLES * KA
QS = PROMPT + KQ - 1
AS = PROMPT + KA - 1
(K_G, K_CUM, K_BETA, K_NRK, K_BRK, K_NBRKE, K_E, K_RQ, K_RK) = range(9)
NK = 9
LEVELS = 7
NEG = -1.0e30


class Memory:

    def __init__(self, nc):
        self.nc = nc
        self.base = (nc.sbuf_base + 63) // 64 * 64
        self.end = nc.sbuf_usable_end
        self.at = self.base
        self.count = 0

    def place(self, name, shape, dt=F32, at=None):
        size = 4
        for s in shape[1:]:
            size *= s
        where = self.at if at is None else at
        t = self.nc.alloc_sbuf_tensor_at(name, shape, dt, offset=where)
        assert where + size <= self.end, (name, where + size - self.end)
        self.next = (where + size + 31) // 32 * 32
        if at is None:
            self.at = self.next
        return t


def bc(ap, n):
    return ap.unsqueeze(len(ap.shape)).broadcast_to(list(ap.shape) + [n])


def bc1(ap, n):
    return ap.unsqueeze(1).broadcast_to([ap.shape[0], n] + list(ap.shape[1:]))


def later(i):
    return not isinstance(i, int) or i > 0


class Shared:
    pass


class Sems:

    def __init__(self, nc):
        self.nc, self.made = nc, {}

    def __call__(self, name):
        if name not in self.made:
            self.made[name] = self.nc.alloc_semaphore(name)
        return self.made[name]

    def pair(self, name, n=2):
        return [self(f"{name}{k}") for k in range(n)]

    def begin(self):
        self.before = set(self.made)

    def end(self, keep=()):
        names = [n for n in self.made if n not in self.before and n not in keep]
        self.nc.clear_and_free_semaphores([self.made.pop(n) for n in names])
        self.nc.all_engine_barrier()


def build(nc, x, w_in, w_ab, conv_a, conv_q, hist_a, hist_q, ssm, a_log, dt_bias, o_norm, norm_mix, norm_ffn,
          norm_final, w_out, r_w, r_b, w_gate, w_up, w_down, y, new_hist, new_ssm_prompt, new_ssm_sample,
          dumps=None, stop=9):
    m = Memory(nc)
    s = Sems(nc)
    b = Shared()
    io = Shared()
    io.x, io.w_in, io.w_ab, io.conv_a, io.conv_q, io.hist_a, io.hist_q = x, w_in, w_ab, conv_a, conv_q, hist_a, hist_q
    io.ssm, io.a_log, io.dt_bias, io.o_norm, io.norm_mix, io.norm_ffn = ssm, a_log, dt_bias, o_norm, norm_mix, norm_ffn
    io.norm_final, io.w_out, io.r_w, io.r_b, io.w_gate, io.w_up, io.w_down = (
        norm_final, w_out, r_w, r_b, w_gate, w_up, w_down)
    io.y, io.new_hist, io.new_ssm_prompt, io.new_ssm_sample = y, new_hist, new_ssm_prompt, new_ssm_sample
    b.psum = nc.alloc_psum_tensor("psum", [P, 8, 512], F32)
    b.h2_dram = nc.dram_tensor("h2_rows", (TOK, D), F32, kind="Internal").ap()
    b.table = nc.dram_tensor("slot_table", (SLOTS, 4), I32, kind="Internal").ap()
    b.ye = nc.dram_tensor("expert_rows", (2 * TOK, D), F32, kind="Internal").ap()

    b.ident = m.place("ident", [P, P])
    b.upto = m.place("upto", [P, P])
    b.before = m.place("before", [P, P])
    b.ones = m.place("ones", [P, P])
    b.negmask = m.place("negmask", [P, P])
    b.levels = m.place("levels", [P, LEVELS, 64])
    b.cqw = m.place("cqw", [P, QKV, KQ])
    b.caw = m.place("caw", [P, CA, KA])
    b.hq = m.place("hq", [P, QKV, SAMPLES, KQ - 1])
    b.ha = m.place("ha", [P, CA, SAMPLES, KA - 1])
    b.col = m.place("col", [P, 10, NK, H])
    b.alog = m.place("alog", [P, H])
    b.dtb = m.place("dtb", [P, H])
    b.onw = m.place("onw", [P, 1])
    b.eps = m.place("eps", [P, 1])
    b.stat = m.place("stat", [P, TILES, 4])
    b.rb = m.place("rb", [P, GRP + NE])
    b.rw = m.place("rw", [P, KD, GRP + NE])
    b.valid = m.place("valid", [P, TILES])
    b.state = m.place("state", [P, H, P])
    b.tb = m.place("tb", [C, NE + OV, 4], I32)
    b.ove = m.place("ove", [P, OV + 1], I32)
    m.at = (m.at + 63) // 64 * 64
    b.R1 = m.at
    b.hh = m.place("hh", [P, KD, TP], F32R)
    b.hl = m.place("hl", [P, KD, TP], F32R)
    b.R4 = m.at
    b.wst = [m.place(f"wst{k}", [P, KD, P]) for k in range(2)]
    b.wh = [m.place(f"wh{k}", [P, KD, P], F32R) for k in range(2)]
    b.wl = [m.place(f"wl{k}", [P, KD, P], F32R) for k in range(2)]
    b.tmp = [m.place(f"tmp{k}", [P, RLEN]) for k in range(5)]
    b.R2 = m.at
    b.qkv = m.place("qkv", [P, QKV, QLEN])
    b.R3 = m.at
    b.yt = m.place("yt", [P, KD, TP])
    b.hist = m.place("hist", [P, CA + QKV, RLEN - PROMPT])

    first_stage(nc, m, s, b, io)
    if stop > 2:
        s.begin()
        delta_stage(nc, m, s, b, io)
        s.end()
        sample_stage(nc, m, s, b, io)
    if stop > 3:
        route_stage(nc, m, s, b, io)
    if stop > 4:
        expert_stage(nc, m, s, b, io)
    if stop > 5:
        final_stage(nc, m, s, b, io)
    if dumps:
        dump(nc, s, b, dumps)


def every(ap, first, step):
    return ap[:, first:first + step * (SAMPLES - 1) + 1:step]


def bank4(ps, bank, m, n):
    return ps[0:m, bank, :].rearrange("p (h n) -> p h n", h=4)[:, :, 0:n]


def z_bank(k):
    return 3 * k


def z_in(ps, k):
    return ps[:, 3 * k:3 * k + 3, 0:ZC]


def thirds(ap, off=0):
    return ap[:, off:off + TP].rearrange("p (c n) -> p c n", c=3)


def make_constants(pool, nc, s, b):
    done = s("constants")
    n = 0

    def step(ins):
        nonlocal n
        n += 1
        ins.then_inc(done, 1)
        pool.wait_ge(done, n)

    step(nc.gpsimd.memset(b.ident[:, :], 0.0))
    step(nc.gpsimd.memset(b.upto[:, :], 1.0))
    step(nc.gpsimd.memset(b.before[:, :], 1.0))
    step(nc.gpsimd.memset(b.ones[:, :], 1.0))
    step(nc.gpsimd.memset(b.negmask[:, :], 0.0))
    step(nc.gpsimd.memset(b.levels[:, :, :], 1.0))
    step(nc.gpsimd.memset(b.eps[:, :], EPS))
    step(nc.gpsimd.memset(b.valid[:, :], 1.0))
    sel = nc.gpsimd.affine_select
    step(sel(out=b.ident[:, :], in_=b.ident[:, :], compare_op=ALU.not_equal, fill=1.0, base=0,
             pattern=[[-1, P]], channel_multiplier=1))
    step(sel(out=b.upto[:, :], in_=b.upto[:, :], compare_op=ALU.is_ge, fill=0.0, base=0,
             pattern=[[1, P]], channel_multiplier=-1))
    step(sel(out=b.before[:, :], in_=b.before[:, :], compare_op=ALU.is_gt, fill=0.0, base=0,
             pattern=[[1, P]], channel_multiplier=-1))
    step(sel(out=b.negmask[:, :], in_=b.negmask[:, :], compare_op=ALU.is_ge, fill=NEG, base=0,
             pattern=[[1, P]], channel_multiplier=-1))
    step(sel(out=b.valid[:, 8:9], in_=b.valid[:, 8:9], compare_op=ALU.is_gt, fill=0.0, base=LAST,
             pattern=[[0, 1]], channel_multiplier=-1))
    for lv in range(LEVELS):
        z = 1 << lv
        v = b.levels[:, lv, :].rearrange("p (b r) -> p b r", r=z)
        step(sel(out=v, in_=v, compare_op=ALU.is_ge, fill=0.0, base=0,
                 pattern=[[-2 * z, 64 // z], [0, z]], channel_multiplier=1))
        step(sel(out=v, in_=v, compare_op=ALU.is_gt, fill=0.0, base=z,
                 pattern=[[2 * z, 64 // z], [0, z]], channel_multiplier=-1))
    return n


CONSTANTS = 13 + 2 * LEVELS


def first_stage(nc, m, s, b, io):
    ps = b.psum
    xb = [m.place(f"xb{k}", [P, D], at=b.R2 + 4096 * k) for k in range(2)]
    hb = [m.place(f"hb{k}", [P, D], at=b.R2 + 8192 + 4096 * k) for k in range(2)]
    junk = m.place("junk", [P, D], at=b.R2 + 16384)
    wbc = m.place("wbc", [P, D], at=b.R2 + 20480)
    wab = m.place("wab", [P, KD, 8], at=b.R2 + 24576)
    wabh = m.place("wabh", [P, KD, 8], F32R, at=m.next)
    wabl = m.place("wabl", [P, KD, 8], F32R, at=m.next)
    small = s("small_loaded")
    x_in = s.pair("x_in")
    squared, logged, rstd, normed = s("squared"), s("logged"), s("rstd"), s("normed")
    turned, hi_ok, lo_ok = s("turned"), s("hi_ok"), s("lo_ok")
    w_landed, whi, wlo = s.pair("w_landed"), s("whi"), s("wlo")
    z_done, z_used = s.pair("z_done"), s.pair("z_used")
    wab_hi, wab_lo, ab_ok, zeroed = s("wab_hi"), s("wab_lo"), s("ab_ok"), s("zeroed")
    ch_ok, a_product, acc_ok, ya_main = s("ch_ok"), s("a_product"), s("acc_ok"), s("ya_main")
    raw_main, raw, taps, conv, th_ok, silu = (s("raw_main"), s("raw"), s("taps"), s("conv"), s("th_ok"), s("silu"))
    gth_ok, squares, sums, kept, scaled = s("gth_ok"), s("squares"), s("sums"), s("kept"), s("scaled")

    def rows(t):
        return P if t < 8 else LAST

    with nc.Block() as block:
        @block.sync
        def _(sp):
            for t in range(TILES):
                if t == 2:
                    sp.dma_start(wbc[:, :], io.norm_mix.partition_broadcast(P)).then_inc(small, 16)
                    sp.dma_start(wab[:, :, :], io.w_ab).then_inc(small, 16)
                    sp.dma_start(b.cqw[:, :, :], io.conv_q).then_inc(small, 16)
                    sp.dma_start(b.caw[:, :, :], io.conv_a).then_inc(small, 16)
                    sp.dma_start(b.hq[:, :, :, :], io.hist_q).then_inc(small, 16)
                    sp.dma_start(b.ha[:, :, :, :], io.hist_a).then_inc(small, 16)
                    sp.dma_start(b.alog[:, :], io.a_log.partition_broadcast(P)).then_inc(small, 16)
                    sp.dma_start(b.dtb[:, :], io.dt_bias.partition_broadcast(P)).then_inc(small, 16)
                    sp.dma_start(b.onw[:, :], io.o_norm).then_inc(small, 16)
                    sp.dma_start(b.rw[:, :, :], io.r_w).then_inc(small, 16)
                    sp.dma_start(b.rb[:, :], io.r_b.partition_broadcast(P)).then_inc(small, 16)
                if t >= 2:
                    sp.wait_ge(normed, t - 1)
                sp.dma_start(xb[t % 2][0:rows(t), :], io.x[t * P:t * P + rows(t), :]).then_inc(x_in[t % 2], 16)
            for n in range(2):
                sp.dma_start(b.wst[n][:, :, :], io.w_in[n]).then_inc(w_landed[n], 16)
            with sp.Fori(0, NBLK // 2 - 1) as i:
                for k in range(2):
                    sp.wait_ge(wlo, 2 * i + k + 1)
                    sp.dma_start(b.wst[k][:, :, :], io.w_in[bass.ds(2 * i + 2 + k, 1)]
                                 .rearrange("a p k c -> (a p) k c")).then_inc(w_landed[k], 16)
            sp.wait_ge(kept, CA + QKV)
            sp.dma_start(io.new_hist, b.hist[:, :, :]).then_inc(s("hist_out"), 16)
            sp.wait_ge(s("hist_out"), 16)

        @block.gpsimd
        def _(pool):
            make_constants(pool, nc, s, b)
            def w_low(i):
                for k in range(2):
                    pool.wait_ge(whi, 2 * i + k + 1)
                    if later(i):
                        pool.wait_ge(z_done[k], i)
                    nc.gpsimd.tensor_tensor(b.wl[k][:, :, :], b.wst[k][:, :, :], b.wh[k][:, :, :].bitcast(F32),
                                            ALU.subtract).then_inc(wlo, 1)

            w_low(0)
            with pool.Fori(1, NBLK // 2) as i:
                w_low(i)

        @block.scalar
        def _(act):
            nc.scalar.preload_act_table_set("natural_log_exp_and_others")

            def high(t):
                n = rows(t)
                for g in range(2):
                    act.wait_ge(turned, 2 * t + g + 1)
                    nc.scalar.activation(b.hh[:, 4 * g:4 * g + 4, t * P:t * P + n], bank4(ps, 2 * (t % 2) + g, P, n),
                                         ACT.Copy).then_inc(hi_ok, 1)

            act.wait_ge(s("constants"), CONSTANTS)
            for t in range(TILES):
                n = rows(t)
                act.wait_ge(x_in[t % 2], 16 * (t // 2 + 1))
                nc.scalar.activation(junk[0:n, :], xb[t % 2][0:n, :], ACT.Square,
                                     accum_out=b.stat[0:n, t, 0:1]).then_inc(squared, 1)
                act.wait_ge(squared, t + 1)
                nc.scalar.activation(b.stat[0:n, t, 1:2], b.stat[0:n, t, 0:1], ACT.Ln, scale=1.0 / D,
                                     bias=b.eps[0:n, :]).then_inc(logged, 1)
                act.wait_ge(logged, t + 1)
                nc.scalar.activation(b.stat[0:n, t, 2:3], b.stat[0:n, t, 1:2], ACT.Exp, scale=-0.5).then_inc(rstd, 1)
                if t >= 1:
                    high(t - 1)
            high(TILES - 1)
            act.wait_ge(small, 16 * 11)
            nc.scalar.activation(wabh[:, :, :], wab[:, :, :], ACT.Copy).then_inc(wab_hi, 1)

            def w_high(n):
                i, k = n
                act.wait_ge(w_landed[k], 16 * (i + 1))
                if later(i):
                    act.wait_ge(z_done[k], i)
                nc.scalar.activation(b.wh[k][:, :, :], b.wst[k][:, :, :], ACT.Copy).then_inc(whi, 1)

            w_high((0, 0))
            w_high((0, 1))
            with act.Fori(0, 2) as i:
                for g in range(2):
                    for q in range(3):
                        n = 3 * g + q
                        w_high((3 * i + (n + 2) // 2, n % 2))
                    act.wait_ge(a_product, 2 * i + g + 1)
                    nc.scalar.activation(b.hist[:, bass.ds(2 * i + g, 1), 0:ALEN - PROMPT]
                                         .rearrange("p a n -> p (a n)"),
                                         b.tmp[1][:, PROMPT:ALEN], ACT.Copy).then_inc(kept, 1)

            def q_k_v(i, k, blk, norms):
                w_high((i + 7, k))
                act.wait_ge(raw, blk + 1)
                nc.scalar.activation(b.hist[:, bass.ds(CA + blk, 1), :].rearrange("p a n -> p (a n)"),
                                     b.tmp[0][:, PROMPT:RLEN], ACT.Copy).then_inc(kept, 1)
                act.wait_ge(conv, blk + 1)
                nc.scalar.activation(b.tmp[3][:, 0:QLEN], b.tmp[2][:, 0:QLEN], ACT.Tanh).then_inc(th_ok, 1)
                if norms:
                    act.wait_ge(silu, blk + 1)
                    if later(blk):
                        act.wait_ge(sums, blk)
                    nc.scalar.activation(b.tmp[4][:, 0:QLEN],
                                         b.qkv[:, bass.ds(blk, 1), :].rearrange("p a n -> p (a n)"),
                                         ACT.Square).then_inc(squares, 1)

            for k in range(2):
                q_k_v(0, k, k, True)
            with act.Fori(1, QK // 2) as i:
                for k in range(2):
                    q_k_v(i, k, 2 * i + k, True)
            with act.Fori(QK // 2, QKV // 2) as i:
                for k in range(2):
                    q_k_v(i, k, 2 * i + k, False)
            act.wait_ge(silu, QKV)
            for n in range(24, NBLK):
                if n + 2 < NBLK:
                    w_high(((n + 2) // 2, n % 2))
                act.wait_ge(z_done[n % 2], n // 2 + 1)
                if n > 24:
                    act.wait_ge(z_used[(n - 1) % 2], (n - 1) // 2 + 1)
                nc.scalar.activation(thirds(b.tmp[3]), z_in(ps, n % 2), ACT.Tanh, scale=0.5).then_inc(gth_ok, 1)

        @block.vector
        def _(dve):
            def low(t):
                n = rows(t)
                for g in range(2):
                    dve.wait_ge(hi_ok, 2 * t + g + 1)
                    cols = slice(t * P, t * P + n)
                    nc.vector.tensor_tensor(b.hl[:, 4 * g:4 * g + 4, cols], bank4(ps, 2 * (t % 2) + g, P, n),
                                            b.hh[:, 4 * g:4 * g + 4, cols].bitcast(F32),
                                            ALU.subtract).then_inc(lo_ok, 1)

            for part in (b.hh, b.hl):
                nc.vector.memset(part[:, :, TOK:TP].bitcast(F32), 0.0)
            nc.vector.memset(b.tmp[0][:, 0:3], 0.0)
            nc.vector.memset(b.tmp[1][:, 0:2], 0.0)
            nc.vector.memset(b.hist[:, :, :], 0.0)
            nc.vector.memset(ps[:, 6:8, :], 0.0).then_inc(zeroed, 1)
            dve.wait_ge(small, 16 * 11)
            nc.vector.tensor_scalar(b.cqw[:, :, :], b.cqw[:, :, :], 0.5, None, ALU.mult).then_inc(scaled, 1)
            for t in range(TILES):
                n = rows(t)
                dve.wait_ge(rstd, t + 1)
                if t >= 2:
                    dve.wait_ge(turned, 2 * (t - 1))
                nc.vector.scalar_tensor_tensor(hb[t % 2][0:n, :], xb[t % 2][0:n, :], b.stat[0:n, t, 2:3],
                                               wbc[0:n, :], ALU.mult, ALU.mult).then_inc(normed, 1)
                if t >= 1:
                    low(t - 1)
            low(TILES - 1)
            dve.wait_ge(wab_hi, 1)
            nc.vector.tensor_tensor(wabl[:, :, :], wab[:, :, :], wabh[:, :, :].bitcast(F32),
                                    ALU.subtract).then_inc(wab_lo, 1)
            dve.wait_ge(ab_ok, 1)
            rawb, ch, acc, th = b.tmp[0], b.tmp[1], b.tmp[2], b.tmp[3]
            cc = th

            def mixer_a(i, g, grp):
                (i0, k0), (i1, k1), (i2, k2) = (((3 * g + q) // 2 + 3 * i, (3 * g + q) % 2) for q in range(3))
                dve.wait_ge(z_done[k0], i0 + 1)
                nc.vector.tensor_copy(thirds(cc), z_in(ps, k0)).then_inc(z_used[k0], 1)
                dve.wait_ge(z_done[k1], i1 + 1)
                dve.wait_ge(z_used[k0], i0 + 1)
                if later(grp):
                    dve.wait_ge(kept, grp)
                nc.vector.tensor_tensor(thirds(ch, 2), z_in(ps, k1), thirds(cc), ALU.mult).then_inc(ch_ok, 1)
                dve.wait_ge(ch_ok, grp + 1)
                nc.vector.tensor_tensor(every(ch, PROMPT + 4, KA), ps[:, z_bank(k1) + 2, 340:348],
                                        cc[:, PROMPT:TOK], ALU.mult).then_inc(z_used[k1], 1)
                for r in range(KA - 1):
                    ins = nc.vector.tensor_copy(every(ch, PROMPT + 2 + r, KA),
                                                b.ha[:, bass.ds(grp, 1), :, r].rearrange("p a n -> p (a n)"))
                ins.then_inc(a_product, 1)
                dve.wait_ge(a_product, grp + 1)
                dve.wait_ge(z_used[k1], i1 + 1)
                w = b.caw[:, bass.ds(grp, 1), :].rearrange("p a n -> p (a n)")
                n = ALEN - 2
                nc.vector.tensor_scalar(acc[:, 0:n], ch[:, 0:n], w[:, 0:1], None, ALU.mult).then_inc(acc_ok, 1)
                for r in range(1, KA):
                    dve.wait_ge(acc_ok, 3 * grp + r)
                    nc.vector.scalar_tensor_tensor(acc[:, 0:n], ch[:, r:r + n], w[:, r:r + 1], acc[:, 0:n],
                                                   ALU.mult, ALU.add).then_inc(acc_ok, 1)
                dve.wait_ge(acc_ok, 3 * grp + 3)
                dve.wait_ge(z_done[k2], i2 + 1)
                out = b.yt[:, bass.ds(grp, 1), :].rearrange("p a n -> p (a n)")
                nc.vector.tensor_tensor(thirds(out), z_in(ps, k2), thirds(acc), ALU.mult).then_inc(ya_main, 1)
                dve.wait_ge(ya_main, grp + 1)
                nc.vector.tensor_tensor(out[:, PROMPT:TOK], ps[:, z_bank(k2) + 2, 340:348],
                                        every(acc, AS, KA), ALU.mult).then_inc(z_used[k2], 1)

            def q_k_v(i, k, blk):
                dve.wait_ge(z_done[k], i + 7)
                dve.wait_ge(kept, CA + blk)
                nc.vector.tensor_copy(thirds(rawb, 3), z_in(ps, k)).then_inc(raw_main, 1)
                dve.wait_ge(raw_main, blk + 1)
                nc.vector.tensor_copy(every(rawb, PROMPT + 6, KQ),
                                      ps[:, z_bank(k) + 2, 340:348]).then_inc(z_used[k], 1)
                for r in range(KQ - 1):
                    ins = nc.vector.tensor_copy(every(rawb, PROMPT + 3 + r, KQ),
                                                b.hq[:, bass.ds(blk, 1), :, r].rearrange("p a n -> p (a n)"))
                ins.then_inc(raw, 1)
                dve.wait_ge(raw, blk + 1)
                dve.wait_ge(z_used[k], i + 7)
                w = b.cqw[:, bass.ds(blk, 1), :].rearrange("p a n -> p (a n)")
                nc.vector.tensor_scalar(acc[:, 0:QLEN], rawb[:, 0:QLEN], w[:, 0:1], None,
                                        ALU.mult).then_inc(taps, 1)
                for r in range(1, KQ):
                    dve.wait_ge(taps, 3 * blk + r)
                    nc.vector.scalar_tensor_tensor(acc[:, 0:QLEN], rawb[:, r:r + QLEN], w[:, r:r + 1],
                                                   acc[:, 0:QLEN], ALU.mult, ALU.add
                                                   ).then_inc(taps if r < KQ - 1 else conv, 1)
                dve.wait_ge(conv, blk + 1)
                dve.wait_ge(th_ok, blk + 1)
                nc.vector.scalar_tensor_tensor(b.qkv[:, bass.ds(blk, 1), :].rearrange("p a n -> p (a n)"),
                                               th[:, 0:QLEN], 1.0, acc[:, 0:QLEN], ALU.add,
                                               ALU.mult).then_inc(silu, 1)

            dve.wait_ge(scaled, 1)
            for grp in range(CA):
                mixer_a(grp // 2, grp % 2, grp)
            with dve.Fori(0, QKV // 2) as i:
                for k in range(2):
                    q_k_v(i, k, 2 * i + k)
            for n in range(24, NBLK):
                dve.wait_ge(gth_ok, n - 23)
                nc.vector.scalar_tensor_tensor(thirds(b.yt[:, CA + n - 24, :]), thirds(th), 1.0, z_in(ps, n % 2),
                                               ALU.add, ALU.mult).then_inc(z_used[n % 2], 1)

        @block.tensor
        def _(pe):
            pe.wait_ge(s("constants"), CONSTANTS)
            for t in range(TILES):
                n = rows(t)
                pe.wait_ge(normed, t + 1)
                for g in range(2):
                    if t >= 2:
                        pe.wait_ge(lo_ok, 2 * (t - 2) + g + 1)
                    for k in range(4):
                        kk = 4 * g + k
                        ins = nc.tensor.transpose(ps[:, 2 * (t % 2) + g, k * P:k * P + n],
                                                  hb[t % 2][0:n, kk * P:kk * P + P], b.ident[0:n, 0:n])
                    ins.then_inc(turned, 1)
            pe.wait_ge(lo_ok, 2 * TILES)
            pe.wait_ge(zeroed, 1)
            pe.wait_ge(wab_hi, 1)
            pe.wait_ge(wab_lo, 1)
            for t in range(10):
                lo, n = (t * P, P) if t < 8 else ((8 * P, TAIL) if t == 8 else (PROMPT, SAMPLES))
                for kk in range(KD):
                    for q, (a, w) in enumerate(((b.hh, wabh), (b.hh, wabl), (b.hl, wabh))):
                        ins = nc.tensor.matmul(ps[0:n, 6, 8 * t:8 * t + 8], a[:, kk, lo:lo + n], w[:, kk, :],
                                               start=(kk == 0 and q == 0), stop=(kk == KD - 1 and q == 2))
            ins.then_inc(ab_ok, 1)

            def product(n, i, k):
                pe.wait_ge(whi, n + 1)
                pe.wait_ge(wlo, n + 1)
                if later(i):
                    pe.wait_ge(z_used[k], i)
                for kk in range(KD):
                    for q, (w, a) in enumerate(((b.wh[k], b.hh), (b.wh[k], b.hl), (b.wl[k], b.hh))):
                        for c in range(3):
                            ins = nc.tensor.matmul(ps[:, z_bank(k) + c, 0:ZC], w[:, kk, :],
                                                   a[:, kk, c * ZC:(c + 1) * ZC],
                                                   start=(kk == 0 and q == 0), stop=(kk == KD - 1 and q == 2))
                ins.then_inc(z_done[k], 1)

            def square_sums(blk):
                pe.wait_ge(squares, blk + 1)
                for t in range(10):
                    sq = b.tmp[4][:, t * P:t * P + P] if t < 8 else (
                        b.tmp[4][:, 8 * P:PROMPT] if t == 8 else every(b.tmp[4], QS, KQ))
                    n = sq.shape[1]
                    ins = nc.tensor.matmul(ps[0:n, 7, bass.ds(blk + QK * t, 1)], sq, b.ones[:, 0:1],
                                           start=True, stop=True)
                ins.then_inc(sums, 1)

            product(0, 0, 0)
            product(1, 0, 1)
            with pe.Fori(1, 6) as i:
                for k in range(2):
                    product(2 * i + k, i, k)
            product(12, 6, 0)
            with pe.Fori(0, QK // 2) as i:
                for k in range(2):
                    product(2 * i + 13 + k, i + (13 + k) // 2, (13 + k) % 2)
                    square_sums(2 * i + k)
            with pe.Fori(0, 3) as i:
                for k in range(2):
                    product(2 * i + 21 + k, i + (21 + k) // 2, (21 + k) % 2)
            product(27, 13, 1)


def delta_stage(nc, m, s, b, io):
    ps = b.psum
    m.at = b.R1
    two = range(2)
    ck = [m.place(f"ck{p}", [P, QKV, P]) for p in two]
    cs = [m.place(f"cs{p}", [P, NK, H]) for p in two]
    bt = [[m.place(f"bt{p}_{lv}", [P, H, P]) for lv in range(LEVELS)] for p in two]
    m1 = [[m.place(f"m1{p}_{lv}", [P, H, P]) for lv in range(1, LEVELS)] for p in two]
    tm = [m.place(f"tm{p}", [P, H, P]) for p in two]
    tt = [m.place(f"tt{p}", [P, H, P]) for p in two]
    dt = [m.place(f"dt{p}", [P, H, P]) for p in two]
    at = [m.place(f"at{p}", [P, H, P]) for p in two]
    qa = [m.place(f"qa{p}", [P, H, P]) for p in two]
    kbe = [m.place(f"kbe{p}", [P, H, P]) for p in two]
    kd = [m.place(f"kd{p}", [P, H, P]) for p in two]
    vb = [m.place(f"vb{p}", [P, H, P]) for p in two]
    u = m.place("u", [P, H, P])
    o1 = m.place("o1", [P, H, P])
    oc = m.place("oc", [P, H, P])
    egl = [m.place(f"egl{p}", [P, H]) for p in two]
    gd = [m.place(f"gd{p}", [P, 3, H]) for p in two]
    os_ = m.place("os", [P, 4, H])
    assert m.at <= b.R2, m.at - b.R2
    pre = m.place("pre", [P, 10, 8, H], at=b.R1 + 14336)

    names = ("staged g_bank eg_ok d_ok gl_ok gle_ok dt_ok kk_ok qk_ok kt_ok vt_ok rb_ok at0_ok at_ok qa_ok kds_ok "
             "kbe_ok kd_ok vb_ok bt_ok t1_ok t_ok tt_ok mm_ok mcopy_ok dd_ok tnew_ok ttnew_ok wt_ok wtc_ok u_ok "
             "uc_ok o1_ok o1c_ok ku_ok o2_ok s_ok o_ok osq_ok oln_ok ors_ok ofac_ok on_ok ot_ok y_ok").split()
    q = {n: s.pair("d_" + n) for n in names}
    cols_ready, zero_ok = s("cols_ready"), s("state_zero")
    e_steps, v_steps, g_sum, out_sem = s("pre_act"), s("pre_vec"), s("g_sum"), s("ssm_out")
    M1Z = s("m1_zero")

    def half(buf, lv, n, t):
        return buf[0:n, :, 0:n].rearrange("p h (b t r) -> p h b t r", t=2, r=1 << lv)[:, :, :, t, :]

    def packed(bank, off, lv, n):
        return ps[0:n, bank, off:off + 64 * H].rearrange("p (h q) -> p h q", h=H)[:, :, 0:n // 2].rearrange(
            "p h (b r) -> p h b r", r=1 << lv)

    def last_level(n):
        return 6 if n == P else 3

    def groups(eng, body):
        body(0, [(0, 0, P), (1, 1, P)])
        with eng.Fori(1, 4) as i:
            body(i, [(2 * i, 0, P), (2 * i + 1, 1, P)])
        body(4, [(8, 0, TAIL)])

    def levels_before(i, lv):
        return 6 * i + lv - 1

    with nc.Block() as block:
        @block.sync
        def _(sp):
            sp.wait_ge(q["s_ok"][0], 5)
            sp.dma_start(io.new_ssm_prompt.rearrange("h k v -> k h v"), b.state[:, :, :]).then_inc(out_sem, 16)
            sp.wait_ge(out_sem, 16)

        @block.gpsimd
        def _(pool):
            pool.wait_ge(cols_ready, 1)
            for p in two:
                for lv in range(LEVELS):
                    nc.gpsimd.memset(bt[p][lv][:, :, :], 0.0)
                for lv in range(1, LEVELS):
                    ins = nc.gpsimd.memset(m1[p][lv - 1][:, :, :], 0.0)
            ins.then_inc(M1Z, 1)
            pool.wait_ge(M1Z, 1)

            def body(i, chunks):
                for c, p, n in chunks:
                    if later(i):
                        pool.wait_ge(q["y_ok"][p], i)
                    src = b.qkv[:, :, bass.ds(c * P, n)]
                    nc.gpsimd.tensor_copy(ck[p][:, :, 0:n], src)
                    nc.gpsimd.tensor_copy(cs[p][0:n, :, :].rearrange("p k h -> p (k h)"),
                                          b.col[0:n, bass.ds(c, 1), :, :].rearrange("p a k h -> p (a k h)")
                                          ).then_inc(q["staged"][p], 1)
                for c, p, n in chunks:
                    pool.wait_ge(q["at_ok"][p], i + 1)
                    for lv in range(last_level(n) + 1):
                        z = 1 << lv
                        mask = bc1(b.levels[0:n, lv, 0:n // 2].rearrange("p (b r) -> p b r", r=z), H)
                        nc.gpsimd.tensor_tensor(half(bt[p][lv], lv, n, 1), half(at[p], lv, n, 1), mask,
                                                ALU.mult).then_inc(q["bt_ok"][p], 1)
            groups(pool, body)

        @block.scalar
        def _(act):
            done = 0

            def step(ins):
                nonlocal done
                done += 1
                ins.then_inc(e_steps, 1)

            a_ = nc.scalar.activation
            act.wait_ge(v_steps, 1)
            step(a_(pre[:, :, 1, :], pre[:, :, 0, :], ACT.Abs))
            act.wait_ge(e_steps, 1)
            step(a_(pre[:, :, 2, :], pre[:, :, 1, :], ACT.Exp, scale=-1.0))
            act.wait_ge(e_steps, 2)
            step(a_(pre[:, :, 1, :], pre[:, :, 2, :], ACT.Ln, bias=b.ones[:, 0:1]))
            step(a_(pre[:, :, 3, :], ab_bank(ps, 4), ACT.Exp, scale=-1.0))
            step(a_(pre[:, :, 4:6, :], ss_bank(ps), ACT.Ln, bias=b.eps[:, 0:1]))
            act.wait_ge(e_steps, 5)
            step(a_(pre[:, :, 6:8, :], pre[:, :, 4:6, :], ACT.Exp, scale=-0.5))
            step(a_(b.alog[:, :], b.alog[:, :], ACT.Exp))
            act.wait_ge(g_sum, 1)
            step(a_(b.col[:, :, K_CUM, :], ps[:, 0, 0:40].rearrange("p (t h) -> p t h", h=H), ACT.Copy))
            act.wait_ge(e_steps, 8)
            step(a_(b.col[:, :, K_E, :], b.col[:, :, K_CUM, :], ACT.Exp))

            def body(i, chunks):
                for c, p, n in chunks:
                    act.wait_ge(q["g_bank"][p], i + 1)
                    a_(egl[p][:, :], ps[:, p, n - 1:n - 1 + 3 * P + 1:P], ACT.Exp).then_inc(q["eg_ok"][p], 1)
                for c, p, n in chunks:
                    act.wait_ge(q["gl_ok"][p], i + 1)
                    a_(gd[p][0:n, 1, :], gd[p][0:n, 0, :], ACT.Exp).then_inc(q["gle_ok"][p], 1)
                    a_(dt[p][0:n, :, 0:n], at[p][0:n, :, 0:n], ACT.Exp).then_inc(q["dt_ok"][p], 1)
                    act.wait_ge(q["kt_ok"][p], i + 1)
                    for h in range(H):
                        ins = a_(kbe[p][0:n, h, :], ps[0:n, 4, h * P:h * P + P], ACT.Copy,
                                 scale=cs[p][0:n, K_NBRKE, h:h + 1])
                    ins.then_inc(q["kbe_ok"][p], 1)
                    act.wait_ge(q["kds_ok"][p], i + 1)
                    for h in range(H):
                        ins = a_(kd[p][0:n, h, :], ps[0:n, 4, h * P:h * P + P], ACT.Copy,
                                 scale=gd[p][0:n, 2, h:h + 1])
                    ins.then_inc(q["kd_ok"][p], 1)
                    act.wait_ge(q["vt_ok"][p], i + 1)
                    for h in range(H):
                        ins = a_(vb[p][0:n, h, :], ps[0:n, 5, h * P:h * P + P], ACT.Copy,
                                 scale=cs[p][0:n, K_BETA, h:h + 1])
                    ins.then_inc(q["vb_ok"][p], 1)
                n = chunks[0][2]
                for lv in range(1, last_level(n) + 1):
                    for c, p, n in chunks:
                        act.wait_ge(q["mm_ok"][p], levels_before(i, lv) + 1)
                        a_(half(m1[p][lv - 1], lv, n, 0), packed(p, 0, lv, n), ACT.Copy).then_inc(q["mcopy_ok"][p], 1)
                for c, p, n in chunks:
                    act.wait_ge(q["wt_ok"][p], i + 1)
                    a_(at[p][:, :, 0:n], bank4(ps, p, P, n), ACT.Copy).then_inc(q["wtc_ok"][p], 1)
                for c, p, n in chunks:
                    act.wait_ge(q["u_ok"][p], i + 1)
                    a_(u[0:n, :, :], bank4(ps, 5, n, P), ACT.Copy).then_inc(q["uc_ok"][p], 1)
                    act.wait_ge(q["o1_ok"][p], i + 1)
                    for h in range(H):
                        ins = a_(o1[0:n, h, :], ps[0:n, 6, h * P:h * P + P], ACT.Copy, scale=cs[p][0:n, K_E, h:h + 1])
                    ins.then_inc(q["o1c_ok"][p], 1)
                    act.wait_ge(q["o_ok"][p], i + 1)
                    for h in range(H):
                        ins = a_(o1[0:n, h, :], oc[0:n, h, :], ACT.Square, scale=cs[p][0:n, K_RQ, h:h + 1],
                                 accum_out=os_[0:n, 0, h:h + 1])
                    ins.then_inc(q["osq_ok"][p], 1)
                    act.wait_ge(q["osq_ok"][p], i + 1)
                    a_(os_[0:n, 1, :], os_[0:n, 0, :], ACT.Ln, scale=1.0 / P, bias=b.eps[0:n, :]
                       ).then_inc(q["oln_ok"][p], 1)
                    act.wait_ge(q["oln_ok"][p], i + 1)
                    a_(os_[0:n, 2, :], os_[0:n, 1, :], ACT.Exp, scale=-0.5).then_inc(q["ors_ok"][p], 1)
            groups(act, body)

        @block.vector
        def _(dve):
            done = 0

            def step(ins, wait=True):
                nonlocal done
                done += 1
                ins.then_inc(v_steps, 1)
                if wait:
                    dve.wait_ge(v_steps, done)

            V = nc.vector
            tt_, stt = V.tensor_tensor, V.scalar_tensor_tensor
            kinds = b.col
            step(tt_(pre[:, :, 0, :], ab_bank(ps, 0), bc1(b.dtb[:, :], 10), ALU.add))
            step(V.memset(b.state[:, :, :], 0.0))
            dve.wait_ge(e_steps, 7)
            step(stt(pre[:, :, 2, :], pre[:, :, 0, :], 0.0, pre[:, :, 1, :], ALU.max, ALU.add))
            step(stt(kinds[:, :, K_G, :], pre[:, :, 2, :], -1.0, bc1(b.alog[:, :], 10), ALU.mult, ALU.mult))
            step(V.memset(ps[:, 0, 0:40], 0.0))
            step(V.tensor_scalar(pre[:, :, 1, :], pre[:, :, 3, :], 1.0, None, ALU.add))
            step(V.reciprocal(kinds[:, :, K_BETA, :], pre[:, :, 1, :]))
            step(V.tensor_scalar(kinds[:, :, K_RQ, :], pre[:, :, 6, :], float(P) ** -0.5, None, ALU.mult))
            step(V.tensor_copy(kinds[:, :, K_RK, :], pre[:, :, 7, :]))
            step(V.tensor_scalar(kinds[:, :, K_NRK, :], pre[:, :, 7, :], -1.0, None, ALU.mult))
            step(tt_(kinds[:, :, K_BRK, :], kinds[:, :, K_BETA, :], pre[:, :, 7, :], ALU.mult))
            step(V.tensor_scalar(b.onw[:, :], b.onw[:, :], 0.5, None, ALU.mult))
            dve.wait_ge(e_steps, 9)
            stt(kinds[:, :, K_NBRKE, :], kinds[:, :, K_BRK, :], -1.0, kinds[:, :, K_E, :], ALU.mult,
                ALU.mult).then_inc(cols_ready, 1)

            def body(i, chunks):
                for c, p, n in chunks:
                    dve.wait_ge(q["eg_ok"][p], i + 1)
                    for h in range(H):
                        stt(at[p][0:n, h, 0:n], ps[0:n, p, h * P:h * P + n], cs[p][0:n, K_CUM, h:h + 1],
                            b.negmask[0:n, 0:n], ALU.subtract, ALU.min)
                    tt_(gd[p][0:n, 0, :], ps[0:n, p, n - 1:n - 1 + 3 * P + 1:P], cs[p][0:n, K_CUM, :],
                        ALU.subtract).then_inc(q["gl_ok"][p], 1)
                for c, p, n in chunks:
                    dve.wait_ge(q["gle_ok"][p], i + 1)
                    tt_(gd[p][0:n, 2, :], gd[p][0:n, 1, :], cs[p][0:n, K_RK, :], ALU.mult).then_inc(q["kds_ok"][p], 1)
                    dve.wait_ge(q["dt_ok"][p], i + 1)
                    dve.wait_ge(q["kk_ok"][p], i + 1)
                    for h in range(H):
                        ins = stt(at[p][0:n, h, 0:n], ps[0:n, 2 + p, h * P:h * P + n], cs[p][0:n, K_NRK, h:h + 1],
                                  dt[p][0:n, h, 0:n], ALU.mult, ALU.mult)
                    ins.then_inc(q["at0_ok"][p], 1)
                    dve.wait_ge(q["qk_ok"][p], i + 1)
                    for h in range(H):
                        ins = stt(qa[p][0:n, h, 0:n], ps[0:n, 6, h * P:h * P + n], cs[p][0:n, K_RK, h:h + 1],
                                  dt[p][0:n, h, 0:n], ALU.mult, ALU.mult)
                    ins.then_inc(q["qa_ok"][p], 1)
                    dve.wait_ge(q["at0_ok"][p], i + 1)
                    dve.wait_ge(q["rb_ok"][p], i + 1)
                    tt_(at[p][0:n, :, 0:n], at[p][0:n, :, 0:n], bank4(ps, p, n, n), ALU.mult
                        ).then_inc(q["at_ok"][p], 1)
                for c, p, n in chunks:
                    dve.wait_ge(q["t1_ok"][p], i + 1)
                    eye = bc1(b.ident[0:n, 0:n], H)
                    tt_(tt[p][0:n, :, 0:n], bt[p][0][0:n, :, 0:n], eye, ALU.add)
                    tt_(tm[p][0:n, :, 0:n], bank4(ps, 2 + p, n, n), eye, ALU.add).then_inc(q["t_ok"][p], 1)
                n = chunks[0][2]
                for lv in range(1, last_level(n) + 1):
                    for c, p, n in chunks:
                        dve.wait_ge(q["dd_ok"][p], levels_before(i, lv) + 1)
                        x = half(tt[p], lv, n, 1)
                        ins = tt_(x, x, packed(2 + p, 256, lv, n), ALU.add)
                        if lv < last_level(n):
                            x = half(tm[p], lv, n, 0)
                            ins = tt_(x, x, packed(2 + p, 0, lv, n), ALU.add)
                        ins.then_inc(q["tnew_ok"][p], 1)
                for c, p, n in chunks:
                    dve.wait_ge(q["ku_ok"][p], i + 1)
                    for h in range(H):
                        ins = stt(b.state[:, h, :], b.state[:, h, :], egl[p][:, h:h + 1], ps[:, 4, h * P:h * P + P],
                                  ALU.mult, ALU.add)
                    ins.then_inc(q["s_ok"][p], 1)
                    dve.wait_ge(q["o2_ok"][p], i + 1)
                    dve.wait_ge(q["o1c_ok"][p], i + 1)
                    tt_(oc[0:n, :, :], bank4(ps, 7, n, P), o1[0:n, :, :], ALU.add).then_inc(q["o_ok"][p], 1)
                    dve.wait_ge(q["ors_ok"][p], i + 1)
                    tt_(os_[0:n, 3, :], os_[0:n, 2, :], cs[p][0:n, K_RQ, :], ALU.mult).then_inc(q["ofac_ok"][p], 1)
                    dve.wait_ge(q["ofac_ok"][p], i + 1)
                    tt_(oc[0:n, :, :], oc[0:n, :, :], bc(os_[0:n, 3, :], P), ALU.mult).then_inc(q["on_ok"][p], 1)
                    dve.wait_ge(q["ot_ok"][p], i + 1)
                    out = b.yt[:, CA:, bass.ds(c * P, n)]
                    stt(out, bank4(ps, 2 + p, P, n), b.onw[:, 0:1], out, ALU.mult, ALU.mult).then_inc(q["y_ok"][p], 1)
            groups(dve, body)

        @block.tensor
        def _(pe):
            mm, tp = nc.tensor.matmul, nc.tensor.transpose
            pe.wait_ge(v_steps, 5)
            g = b.col
            mm(ps[:, 0, 0:32], b.upto[:, :], g[:, 0:8, K_G, :], start=True, stop=True)
            mm(ps[0:TAIL, 0, 32:36], b.upto[0:TAIL, 0:TAIL], g[0:TAIL, 8, K_G, :], start=True, stop=True)
            mm(ps[0:SAMPLES, 0, 36:40], b.ident[0:SAMPLES, 0:SAMPLES], g[0:SAMPLES, 9, K_G, :], start=True,
               stop=True).then_inc(g_sum, 1)

            def body(i, chunks):
                for p in two if later(i) else ():
                    pe.wait_ge(q["y_ok"][p], i)
                for c, p, n in chunks:
                    pe.wait_ge(q["staged"][p], i + 1)
                    for h in range(H):
                        ins = mm(ps[:, p, h * P:h * P + n], cs[p][0:n, K_G, h:h + 1].to_broadcast([n, P]),
                                 b.upto[0:n, 0:n], start=True, stop=True)
                    ins.then_inc(q["g_bank"][p], 1)
                for c, p, n in chunks:
                    for h in range(H):
                        kt = ck[p][:, H + h, 0:n]
                        ins = mm(ps[0:n, 2 + p, h * P:h * P + n], kt, kt, start=True, stop=True)
                    ins.then_inc(q["kk_ok"][p], 1)
                for c, p, n in chunks:
                    if p == 1:
                        pe.wait_ge(q["kd_ok"][0], i + 1)
                        pe.wait_ge(q["vb_ok"][0], i + 1)
                        pe.wait_ge(q["qa_ok"][0], i + 1)
                    for h in range(H):
                        ins = tp(ps[0:n, 4, h * P:h * P + P], ck[p][:, H + h, 0:n], b.ident[:, :])
                    ins.then_inc(q["kt_ok"][p], 1)
                    for h in range(H):
                        ins = tp(ps[0:n, 5, h * P:h * P + P], ck[p][:, 2 * H + h, 0:n], b.ident[:, :])
                    ins.then_inc(q["vt_ok"][p], 1)
                    for h in range(H):
                        ins = mm(ps[0:n, 6, h * P:h * P + n], ck[p][:, H + h, 0:n], ck[p][:, h, 0:n],
                                 start=True, stop=True)
                    ins.then_inc(q["qk_ok"][p], 1)
                    pe.wait_ge(q["gl_ok"][p], i + 1)
                    for h in range(H):
                        ins = mm(ps[0:n, p, h * P:h * P + n], cs[p][0:n, K_BRK, h:h + 1].to_broadcast([n, n]),
                                 b.ident[0:n, 0:n], start=True, stop=True)
                    ins.then_inc(q["rb_ok"][p], 1)
                for c, p, n in chunks:
                    pe.wait_ge(q["bt_ok"][p], 7 * i + 1)
                    pe.wait_ge(q["at0_ok"][p], i + 1)
                    for h in range(H):
                        ins = tp(ps[0:n, 2 + p, h * P:h * P + n], bt[p][0][0:n, h, 0:n], b.ident[0:n, 0:n])
                    ins.then_inc(q["t1_ok"][p], 1)
                n = chunks[0][2]
                top = last_level(n)
                for lv in range(1, top + 1):
                    for c, p, n in chunks:
                        if lv == 1:
                            pe.wait_ge(q["t_ok"][p], i + 1)
                            pe.wait_ge(q["at_ok"][p], i + 1)
                        else:
                            pe.wait_ge(q["tnew_ok"][p], levels_before(i, lv))
                        pe.wait_ge(q["bt_ok"][p], 7 * i + lv + 1)
                        for h in range(H):
                            ins = mm(ps[0:n, p, h * 64:h * 64 + n // 2], bt[p][lv][0:n, h, 0:n],
                                     half(tm[p], lv, n, 0)[:, h], start=True, stop=True)
                        ins.then_inc(q["mm_ok"][p], 1)
                    for c, p, n in chunks:
                        pe.wait_ge(q["mcopy_ok"][p], levels_before(i, lv) + 1)
                        for h in range(H):
                            if lv < top:
                                mm(ps[0:n, 2 + p, h * 64:h * 64 + n // 2], tt[p][0:n, h, 0:n],
                                   half(m1[p][lv - 1], lv, n, 0)[:, h], start=True, stop=True)
                            ins = mm(ps[0:n, 2 + p, 256 + h * 64:256 + h * 64 + n // 2], m1[p][lv - 1][0:n, h, 0:n],
                                     half(tt[p], lv, n, 1)[:, h], start=True, stop=True)
                        ins.then_inc(q["dd_ok"][p], 1)
                for c, p, n in chunks:
                    pe.wait_ge(q["tnew_ok"][p], levels_before(i, top) + 1)
                    pe.wait_ge(q["kbe_ok"][p], i + 1)
                    for h in range(H):
                        ins = mm(ps[:, p, h * P:h * P + n], kbe[p][0:n, h, :], tt[p][0:n, h, 0:n],
                                 start=True, stop=True)
                    ins.then_inc(q["wt_ok"][p], 1)
                for c, p, n in chunks:
                    before = (1 - p, i if p == 0 else i + 1)
                    pe.wait_ge(q["wtc_ok"][p], i + 1)
                    pe.wait_ge(q["vb_ok"][chunks[-1][1]], i + 1)
                    if later(before[1]):
                        pe.wait_ge(q["s_ok"][before[0]], before[1])
                        pe.wait_ge(q["uc_ok"][before[0]], before[1])
                    for h in range(H):
                        mm(ps[0:n, 5, h * P:h * P + P], tt[p][0:n, h, 0:n], vb[p][0:n, h, :], start=True, stop=False)
                        ins = mm(ps[0:n, 5, h * P:h * P + P], at[p][:, h, 0:n], b.state[:, h, :],
                                 start=False, stop=True)
                    ins.then_inc(q["u_ok"][p], 1)
                    pe.wait_ge(q["qa_ok"][chunks[-1][1]], i + 1)
                    if later(before[1]):
                        pe.wait_ge(q["o1c_ok"][before[0]], before[1])
                    for h in range(H):
                        ins = mm(ps[0:n, 6, h * P:h * P + P], ck[p][:, h, 0:n], b.state[:, h, :],
                                 start=True, stop=True)
                    ins.then_inc(q["o1_ok"][p], 1)
                    pe.wait_ge(q["uc_ok"][p], i + 1)
                    pe.wait_ge(q["kd_ok"][chunks[-1][1]], i + 1)
                    for h in range(H):
                        ins = mm(ps[:, 4, h * P:h * P + P], kd[p][0:n, h, :], u[0:n, h, :], start=True, stop=True)
                    ins.then_inc(q["ku_ok"][p], 1)
                    if later(before[1]):
                        pe.wait_ge(q["o_ok"][before[0]], before[1])
                    for h in range(H):
                        ins = mm(ps[0:n, 7, h * P:h * P + P], qa[p][0:n, h, 0:n], u[0:n, h, :], start=True, stop=True)
                    ins.then_inc(q["o2_ok"][p], 1)
                    pe.wait_ge(q["on_ok"][p], i + 1)
                    for h in range(H):
                        ins = tp(ps[:, 2 + p, h * P:h * P + n], oc[0:n, h, :], b.ident[0:n, 0:n])
                    ins.then_inc(q["ot_ok"][p], 1)
            groups(pe, body)


def ab_bank(ps, first):
    return ps[:, 6, 0:80].rearrange("p (t k) -> p t k", k=8)[:, :, first:first + H]


def ss_bank(ps):
    return ps[:, 7, 0:80].rearrange("p (t a h) -> p t a h", a=2, h=H)


def sample_stage(nc, m, s, b, io):
    ps = b.psum
    m.at = b.R1
    SH = SAMPLES * H
    s_in = m.place("s_in", [P, SH, P])
    s_new = m.place("s_new", [P, SH, P])
    spread = m.place("spread", [SAMPLES, 4, SAMPLES, H])
    vals = m.place("vals", [P, 4, SAMPLES, H])
    kh = m.place("kh", [P, SAMPLES, H])
    qh = m.place("qh", [P, SAMPLES, H])
    kq = m.place("kq", [P, SH, 2])
    qk = m.place("qk", [P, SAMPLES, H])
    vu = m.place("vu", [P, SAMPLES, H])
    uu = m.place("uu", [P, SAMPLES, H])
    oo = m.place("oo", [P, SAMPLES, H])
    osq = m.place("osq_s", [P, SAMPLES, H])
    rs = m.place("rs", [P, 2, SAMPLES, H])
    outer = [m.place(f"outer{p}", [P, H, P]) for p in range(2)]
    v, a, in_, out = s("s_vec"), s("s_act"), s("s_state_in"), s("s_state_out")
    pe1, pe2, pe3, pe4, scaled, added, mult = (s("s_vals"), s("s_products"), s("s_norms"), s("s_rows"), s("s_scaled"),
                                               s("s_added"), s("s_outer"))

    def flat(ap):
        return ap.rearrange("p b h -> p (b h)")

    def mine(first):
        return every3(b.qkv[:, first:first + H, :]).rearrange("p h b -> p b h")

    with nc.Block() as block:
        @block.sync
        def _(sp):
            sp.dma_start(s_in[:, :, :], io.ssm.rearrange("b h k v -> k (b h) v")).then_inc(in_, 16)
            sp.wait_ge(added, SAMPLES)
            sp.dma_start(io.new_ssm_sample.rearrange("b h k v -> k (b h) v"), s_new[:, :, :]).then_inc(out, 16)
            sp.wait_ge(out, 16)

        @block.gpsimd
        def _(pool):
            pool.wait_ge(in_, 16)
            pool.wait_ge(v, 3)
            for k in range(SAMPLES):
                nc.gpsimd.tensor_tensor(s_new[:, H * k:H * k + H, :], s_in[:, H * k:H * k + H, :],
                                        bc(vals[:, 1, k, :], P), ALU.mult).then_inc(scaled, 1)

        @block.scalar
        def _(act):
            act.wait_ge(pe3, 1)
            nc.scalar.activation(rs[:, 0, :, :].rearrange("p b h -> p (b h)"), ps[:, 2, 0:SH], ACT.Ln, scale=1.0 / P,
                                 bias=b.eps[:, :]).then_inc(a, 1)
            act.wait_ge(a, 1)
            nc.scalar.activation(rs[:, 1, :, :], rs[:, 0, :, :], ACT.Exp, scale=-0.5).then_inc(a, 1)

        @block.vector
        def _(dve):
            n = 0

            def step(ins):
                nonlocal n
                n += 1
                ins.then_inc(v, 1)
                dve.wait_ge(v, n)

            tt = nc.vector.tensor_tensor
            eye = b.ident[0:SAMPLES, 0:SAMPLES]
            step(tt(spread[:, 0, :, :], bc1(b.col[0:SAMPLES, 9, K_BETA, :], SAMPLES), bc(eye, H), ALU.mult))
            shape = [SAMPLES, 3, SAMPLES, H]
            step(tt(spread[:, 1:4, :, :], b.col[0:SAMPLES, 9, K_E:K_RK + 1, :].unsqueeze(2).broadcast_to(shape),
                    bc1(bc(eye, H), 3), ALU.mult))
            dve.wait_ge(pe1, 1)
            step(nc.vector.tensor_copy(vals[:, :, :, :].rearrange("p k b h -> p (k b h)"), ps[:, 0, 0:4 * SH]))
            step(tt(kh[:, :, :], mine(H), vals[:, 3, :, :], ALU.mult))
            step(tt(qh[:, :, :], mine(0), vals[:, 2, :, :], ALU.mult))
            step(tt(qk[:, :, :], kh[:, :, :], qh[:, :, :], ALU.mult))
            step(tt(vu[:, :, :], kh[:, :, :], vals[:, 1, :, :], ALU.mult))
            step(tt(kq[:, :, 0], flat(vu[:, :, :]), flat(vals[:, 0, :, :]), ALU.mult))
            step(tt(kq[:, :, 1], flat(qh[:, :, :]), flat(vals[:, 1, :, :]), ALU.mult))
            step(tt(vu[:, :, :], mine(2 * H), vals[:, 0, :, :], ALU.mult))
            dve.wait_ge(pe2, 1)
            got = ps[:, 1, 0:2 * SH].rearrange("p (n k) -> p n k", k=2)
            step(tt(flat(uu[:, :, :]), flat(vu[:, :, :]), got[:, :, 0], ALU.subtract))
            step(tt(flat(oo[:, :, :]), flat(uu[:, :, :]), ps[:, 3, 0:SH], ALU.mult))
            step(tt(flat(oo[:, :, :]), flat(oo[:, :, :]), got[:, :, 1], ALU.add))
            step(tt(osq[:, :, :], oo[:, :, :], oo[:, :, :], ALU.mult))
            dve.wait_ge(a, 2)
            step(tt(oo[:, :, :], oo[:, :, :], rs[:, 1, :, :], ALU.mult))
            y = b.yt[:, CA:, PROMPT:TOK].rearrange("p h b -> p b h")
            step(nc.vector.scalar_tensor_tensor(y, oo[:, :, :], b.onw[:, 0:1], y, ALU.mult, ALU.mult))
            for k in range(SAMPLES):
                dve.wait_ge(pe4, k + 1)
                tt(outer[k % 2][:, :, :], bank4(ps, 4 + k % 4, P, P), bc(kh[:, k, :], P), ALU.mult).then_inc(mult, 1)
                dve.wait_ge(mult, k + 1)
                dve.wait_ge(scaled, k + 1)
                rows = s_new[:, H * k:H * k + H, :]
                tt(rows, rows, outer[k % 2][:, :, :], ALU.add).then_inc(added, 1)

        @block.tensor
        def _(pe):
            mm = nc.tensor.matmul
            pe.wait_ge(v, 2)
            mm(ps[:, 0, 0:4 * SH], b.ones[0:SAMPLES, :], spread[:, :, :, :].rearrange("p k b h -> p (k b h)"),
               start=True, stop=True).then_inc(pe1, 1)
            pe.wait_ge(in_, 16)
            pe.wait_ge(v, 9)
            for n in range(SH):
                mm(ps[:, 1, 2 * n:2 * n + 2], s_in[:, n, :], kq[:, n, :], start=True, stop=True)
            mm(ps[:, 3, 0:SH], b.ones[:, :], flat(qk[:, :, :]), start=True, stop=True).then_inc(pe2, 1)
            pe.wait_ge(v, 14)
            mm(ps[:, 2, 0:SH], b.ones[:, :], flat(osq[:, :, :]), start=True, stop=True).then_inc(pe3, 1)
            for k in range(SAMPLES):
                if k >= 4:
                    pe.wait_ge(mult, k - 3)
                for h in range(H):
                    ins = mm(ps[:, 4 + k % 4, h * P:h * P + P], uu[:, k, h:h + 1].to_broadcast([P, P]),
                             b.ident[:, :], start=True, stop=True)
                ins.then_inc(pe4, 1)


def every3(ap):
    return ap[:, :, QS:QS + KQ * (SAMPLES - 1) + 1:KQ]


def route_stage(nc, m, s, b, io):
    ps = b.psum
    wo = m.place("wo", [P, KD, D], at=b.R1)
    b.x1 = m.place("x1", [P, TILES, D], at=b.R1 + 49152)
    b.R5 = m.next
    m.at = b.R5
    xt = [m.place(f"xt{k}", [P, D]) for k in range(2)]
    h2 = [m.place(f"h2{k}", [P, D]) for k in range(2)]
    wf = m.place("wf", [P, D])
    h2t = m.place("h2t", [P, KD, P])
    assert m.at <= b.R2
    lg = m.place("lg", [P, TILES, GRP + NE], at=b.R1 + 32768)
    m.at = b.R5
    T = TILES
    r = {}
    for name, shape in (
            ("mg", [T]), ("eg", [T, 4]), ("eq", [T, 4]), ("sc", [T, 4]), ("ms", [T]), ("og", [T, 4]), ("sg", [T]),
            ("pg", [T]), ("lx", [T, 4, 8]), ("les", [T, 8]), ("m1", [T]), ("eq1", [T, 8]), ("oh1", [T, 8]),
            ("le2", [T, 8]), ("m2", [T]), ("oh2", [T, 8]), ("d", [T]), ("ed", [T]), ("den", [T]), ("w", [2, T]),
            ("o1", [T, 4, 8]), ("o2", [T, 4, 8]), ("os", [T, 4, 8]), ("cr", [T + 1, NE]), ("pos", [T, NE]),
            ("tmp", [T, NE]), ("rank", [2, T]), ("thr", [PARTS - 1]), ("cmp", [NE, PARTS - 1]), ("nov", [NE]),
            ("incl", [NE]), ("zero", [NE]), ("slotb", [NE]), ("slotm", [NE]), ("ov", [2, T]), ("ma", [2, T]),
            ("isov", [2, T]), ("slot", [2, T]), ("bad", [T]), ("le_", [OV, NE]), ("ovf", [OV + 1]), ("ib", [OV]),
            ("iw", [8]), ("ie", [NE]), ("tok", [T])):
        r[name] = m.place("r_" + name, [P] + shape)
    slot_i = m.place("slot_i", [P, 2, T], I32)
    pay = m.place("pay", [P, 2, T, 4], I32)
    assert m.at <= b.R2
    w_in, x_in, x1_ok, sq, ln, rs, h2_ok = (s("wo_in"), s.pair("x2_in"), s("x1_ok"), s("h2_sq"), s("h2_ln"),
                                            s("h2_rs"), s("h2_ok"))
    prod, turned, turned_c, logits, lg_ok, h2_out = (s("out_prod"), s("h2_turned"), s("h2_copied"), s("logits"),
                                                     s("lg_ok"), s.pair("h2_out"))
    iota, filled, vr, ar, counted = s("r_iota"), s("table_filled"), s("r_vec"), s("r_act"), s("r_counts")
    scattered, b.table_in = s("scattered"), s("table_in")
    b.w_landed = [s(f"expert_w{k}") for k in range(4)]
    b.slots = expert_slots(m, b)

    def rows(t):
        return P if t < 8 else LAST

    with nc.Block() as block:
        @block.sync
        def _(sp):
            sp.dma_start(wo[:, :, :], io.w_out).then_inc(w_in, 16)
            sp.dma_start(wf[:, :], io.norm_ffn.partition_broadcast(P)).then_inc(w_in, 16)
            for t in range(TILES):
                n = rows(t)
                if t >= 2:
                    sp.wait_ge(x1_ok, t - 1)
                sp.dma_start(xt[t % 2][0:n, :], io.x[t * P:t * P + n, :]).then_inc(x_in[t % 2], 16)
                if t == 1:
                    for e in range(2):
                        load_expert(sp, b, io, e, e)
                if t >= 1:
                    k = rows(t - 1)
                    sp.wait_ge(h2_ok, t)
                    sp.dma_start(b.h2_dram[(t - 1) * P:(t - 1) * P + k, :], h2[(t - 1) % 2][0:k, :]
                                 ).then_inc(h2_out[(t - 1) % 2], 16)
            sp.wait_ge(h2_ok, TILES)
            sp.dma_start(b.h2_dram[8 * P:TOK, :], h2[0][0:LAST, :]).then_inc(h2_out[0], 16)
            sp.wait_ge(h2_out[0], 16 * 5)
            sp.wait_ge(h2_out[1], 16 * 4)
            sp.wait_ge(scattered, 16 * 2 * TILES)
            sp.dma_start(b.tb[:, :, :], b.table.rearrange("(k r) c -> r k c", r=C)).then_inc(b.table_in, 16)
            sp.wait_ge(b.table_in, 16)

        @block.gpsimd
        def _(pool):
            nc.gpsimd.memset(b.tb[:, :, :], 0).then_inc(iota, 1)
            pool.wait_ge(iota, 1)
            nc.gpsimd.memset(b.tb[:, :, 1:2], NOWHERE).then_inc(iota, 1)
            pool.wait_ge(iota, 2)
            pool.dma_start(b.table.rearrange("(k r) c -> r k c", r=C), b.tb[:, :, :]).then_inc(filled, 16)
            pool.wait_ge(lg_ok, TILES)
            pool.wait_ge(h2_out[0], 16 * 5)
            pool.wait_ge(h2_out[1], 16 * 4)
            it = nc.gpsimd.iota
            kw = dict(allow_small_or_imprecise_dtypes=True)
            it(r["iw"][:, :], pattern=[[-1, 8]], base=8, channel_multiplier=0, **kw)
            it(r["ie"][:, :], pattern=[[C, NE]], base=0, channel_multiplier=0, **kw)
            it(r["ib"][:, :], pattern=[[1, OV]], base=0, channel_multiplier=0, **kw)
            it(r["thr"][:, :], pattern=[[C, PARTS - 1]], base=C, channel_multiplier=0, **kw)
            nc.gpsimd.memset(r["zero"][:, :], 0.0)
            nc.gpsimd.memset(pay[:, :, :, :], 0).then_inc(iota, 1)
            pool.wait_ge(iota, 3)
            for k in range(2):
                it(pay[:, k, :, 0], pattern=[[P, TILES]], base=0, channel_multiplier=1)
                ins = it(pay[:, k, :, 1], pattern=[[P, TILES]], base=k * TOK, channel_multiplier=1)
            ins.then_inc(iota, 1)
            pool.wait_ge(vr, ROUTE_STEPS)
            pool.wait_ge(filled, 16)
            pool.wait_ge(iota, 4)
            for k in range(2):
                for t in range(TILES):
                    pool.indirect_dma_start(
                        b.table, bass.IndirectOffsetOnAxis(ap=slot_i[:, k, t:t + 1].bitcast(U32), axis=0),
                        pay[:, k, t, :], None, bounds_check=SLOTS - 1, oob_is_err=False).then_inc(scattered, 16)

        @block.scalar
        def _(act):
            a_ = nc.scalar.activation

            def copy_turned(t):
                n = rows(t)
                for g in range(2):
                    act.wait_ge(turned, 2 * t + g + 1)
                    if t >= 1:
                        act.wait_ge(logits, t)
                    a_(h2t[:, 4 * g:4 * g + 4, 0:n], bank4(ps, 4 + g, P, n), ACT.Copy).then_inc(turned_c, 1)

            for t in range(TILES):
                n = rows(t)
                act.wait_ge(x1_ok, t + 1)
                if t >= 2:
                    act.wait_ge(turned, 2 * t - 2)
                    act.wait_ge(h2_out[t % 2], 16 * (t // 2))
                a_(h2[t % 2][0:n, :], b.x1[0:n, t, :], ACT.Square, accum_out=b.stat[0:n, t, 0:1]).then_inc(sq, 1)
                act.wait_ge(sq, t + 1)
                a_(b.stat[0:n, t, 1:2], b.stat[0:n, t, 0:1], ACT.Ln, scale=1.0 / D, bias=b.eps[0:n, :]
                   ).then_inc(ln, 1)
                act.wait_ge(ln, t + 1)
                a_(b.stat[0:n, t, 2:3], b.stat[0:n, t, 1:2], ACT.Exp, scale=-0.5).then_inc(rs, 1)
                copy_turned(t)
            act.wait_ge(vr, 7)
            a_(r["eg"][:, :, :], r["eq"][:, :, :], ACT.Exp).then_inc(ar, 1)
            act.wait_ge(vr, 18)
            a_(r["ed"][:, :], r["d"][:, :], ACT.Exp).then_inc(ar, 1)

        @block.vector
        def _(dve):
            V = nc.vector
            V.memset(lg[:, :, :], 0.0).then_inc(s("lg_zero"), 1)
            dve.wait_ge(w_in, 32)
            dve.wait_ge(s("lg_zero"), 1)

            def tail(t):
                dve.wait_ge(logits, t + 1)
                n = rows(t)
                V.tensor_tensor(lg[0:n, t, :], ps[0:n, 6, 0:GRP + NE], b.rb[0:n, :], ALU.add).then_inc(lg_ok, 1)

            for t in range(TILES):
                n = rows(t)
                dve.wait_ge(x_in[t % 2], 16 * (t // 2 + 1))
                dve.wait_ge(prod, t + 1)
                V.tensor_tensor(b.x1[0:n, t, :].rearrange("p (c n) -> p c n", c=2),
                                ps[0:n, 2 * (t % 2):2 * (t % 2) + 2, :],
                                xt[t % 2][0:n, :].rearrange("p (c n) -> p c n", c=2), ALU.add).then_inc(x1_ok, 1)
                dve.wait_ge(rs, t + 1)
                V.scalar_tensor_tensor(h2[t % 2][0:n, :], b.x1[0:n, t, :], b.stat[0:n, t, 2:3], wf[0:n, :],
                                       ALU.mult, ALU.mult).then_inc(h2_ok, 1)
                tail(t)
            dve.wait_ge(iota, 4)
            dve.wait_ge(lg_ok, TILES)
            n = 0

            def step(ins):
                nonlocal n
                n += 1
                ins.then_inc(vr, 1)
                dve.wait_ge(vr, n)

            tt, ts, stt, red = V.tensor_tensor, V.tensor_scalar, V.scalar_tensor_tensor, V.tensor_reduce
            l4 = lg[:, :, 0:GRP]
            l32 = lg[:, :, GRP:].rearrange("p t (g e) -> p t g e", g=GRP)

            def top(vals, eq, sel, best, first, k):
                step(red(best, vals, AX.X, ALU.max))
                step(tt(eq, vals, bc(best, k), ALU.is_equal))
                step(tt(eq, eq, bc1(r["iw"][:, 8 - k:8], T), ALU.mult))
                step(red(first, eq, AX.X, ALU.max))
                step(tt(sel, eq, bc(first, k), ALU.is_equal))

            top(l4, r["sc"][:, :, :], r["og"][:, :, :], r["mg"][:, :], r["ms"][:, :], GRP)
            step(tt(r["og"][:, :, :], r["og"][:, :, :], bc(b.valid[:, :], GRP), ALU.mult))
            step(tt(r["eq"][:, :, :], l4, bc(r["mg"][:, :], GRP), ALU.subtract))
            step(tt(r["lx"][:, :, :, :], l32, bc(r["og"][:, :, :], EPG), ALU.mult))
            step(red(r["les"][:, :, :], r["lx"][:, :, :, :].rearrange("p t g e -> p t e g"), AX.X, ALU.add))
            top(r["les"][:, :, :], r["eq1"][:, :, :], r["oh1"][:, :, :], r["m1"][:, :], r["ms"][:, :], EPG)
            step(stt(r["le2"][:, :, :], r["oh1"][:, :, :], 2 * NEG, r["les"][:, :, :], ALU.mult, ALU.add))
            step(red(r["m2"][:, :], r["le2"][:, :, :], AX.X, ALU.max))
            dve.wait_ge(ar, 1)
            step(red(r["sg"][:, :], r["eg"][:, :, :], AX.X, ALU.add))
            step(tt(r["d"][:, :], r["m2"][:, :], r["m1"][:, :], ALU.subtract))
            step(tt(r["eq1"][:, :, :], r["le2"][:, :, :], bc(r["m2"][:, :], EPG), ALU.is_equal))
            step(tt(r["eq1"][:, :, :], r["eq1"][:, :, :], bc1(r["iw"][:, :], T), ALU.mult))
            step(red(r["ms"][:, :], r["eq1"][:, :, :], AX.X, ALU.max))
            step(tt(r["oh2"][:, :, :], r["eq1"][:, :, :], bc(r["ms"][:, :], EPG), ALU.is_equal))
            step(V.reciprocal(r["pg"][:, :], r["sg"][:, :]))
            dve.wait_ge(ar, 2)
            step(ts(r["den"][:, :], r["ed"][:, :], 1.0, None, ALU.add))
            step(V.reciprocal(r["den"][:, :], r["den"][:, :]))
            step(tt(r["w"][:, 0, :], r["pg"][:, :], r["den"][:, :], ALU.mult))
            step(tt(r["w"][:, 1, :], r["w"][:, 0, :], r["ed"][:, :], ALU.mult))
            shape = [P, T, GRP, EPG]
            for o, oh in ((r["o1"], r["oh1"]), (r["o2"], r["oh2"])):
                step(tt(o[:, :, :, :], bc(r["og"][:, :, :], EPG), oh[:, :, :].unsqueeze(2).broadcast_to(shape), ALU.mult))
            step(tt(r["os"][:, :, :, :], r["o1"][:, :, :, :], r["o2"][:, :, :, :], ALU.add))
            step(V.memset(r["cr"][:, 0, :], 0.0))
            dve.wait_ge(counted, 1)
            for t in range(T):
                step(tt(r["cr"][:, t + 1, :], r["cr"][:, t, :], ps[:, 1, NE * t:NE * t + NE], ALU.add))
            step(tt(r["pos"][:, :, :], r["cr"][:, 0:T, :], ps[:, 0, 0:NE * T].rearrange("p (t e) -> p t e", e=NE), ALU.add))
            total = r["cr"][:, T, :]
            step(tt(r["cmp"][:, :, :], bc(total, PARTS - 1), bc1(r["thr"][:, :], NE), ALU.is_gt))
            step(red(r["nov"][:, :], r["cmp"][:, :, :], AX.X, ALU.add))
            step(V.tensor_tensor_scan(r["incl"][:, :], r["nov"][:, :], r["zero"][:, :], 0.0, ALU.add, ALU.add))
            step(tt(r["slotb"][:, :], r["incl"][:, :], r["nov"][:, :], ALU.subtract))
            step(ts(r["slotb"][:, :], r["slotb"][:, :], float(C), float((NE - 1) * C), ALU.mult, ALU.add))
            for k, o in enumerate((r["o1"], r["o2"])):
                oe = o[:, :, :, :].rearrange("p t g e -> p t (g e)")
                for vals, dst in ((r["pos"][:, :, :], r["rank"]), (bc1(r["ie"][:, :], T), r["ma"]), (bc1(r["slotb"][:, :], T), r["ov"])):
                    step(tt(r["tmp"][:, :, :], oe, vals, ALU.mult))
                    step(red(dst[:, k, :], r["tmp"][:, :, :], AX.X, ALU.add))
            step(ts(r["isov"][:, :, :], r["rank"][:, :, :], float(C), None, ALU.is_ge))
            step(tt(r["ov"][:, :, :], r["ov"][:, :, :], r["ma"][:, :, :], ALU.subtract))
            step(tt(r["ov"][:, :, :], r["ov"][:, :, :], r["isov"][:, :, :], ALU.mult))
            step(tt(r["slot"][:, :, :], r["rank"][:, :, :], r["ma"][:, :, :], ALU.add))
            step(tt(r["slot"][:, :, :], r["slot"][:, :, :], r["ov"][:, :, :], ALU.add))
            step(ts(r["bad"][:, :], b.valid[:, :], -1.0e5, 1.0e5, ALU.mult, ALU.add))
            step(tt(r["slot"][:, :, :], r["slot"][:, :, :], bc1(r["bad"][:, :], 2), ALU.add))
            step(V.tensor_copy(slot_i[:, :, :], r["slot"][:, :, :]))
            step(V.tensor_copy(pay[:, :, :, 2].bitcast(F32), r["w"][:, :, :]))
            step(tt(r["le_"][:, :, :], bc1(r["incl"][:, :], OV), bc(r["ib"][:, :], NE), ALU.is_le))
            step(red(r["ovf"][:, 0:OV], r["le_"][:, :, :], AX.X, ALU.add))
            step(V.tensor_copy(r["ovf"][:, OV:OV + 1], r["incl"][:, NE - 1:NE]))
            step(V.tensor_copy(b.ove[:, :], r["ovf"][:, :]))
            assert n == ROUTE_STEPS, n

        @block.tensor
        def _(pe):
            mm = nc.tensor.matmul

            def turn_and_route(t):
                n = rows(t)
                pe.wait_ge(h2_ok, t + 1)
                if t >= 1:
                    pe.wait_ge(turned_c, 2 * t)
                for g in range(2):
                    for k in range(4):
                        kk = 4 * g + k
                        ins = nc.tensor.transpose(ps[:, 4 + g, k * P:k * P + n],
                                                  h2[t % 2][0:n, kk * P:kk * P + P], b.ident[0:n, 0:n])
                    ins.then_inc(turned, 1)
                pe.wait_ge(turned_c, 2 * t + 2)
                if t >= 1:
                    pe.wait_ge(lg_ok, t)
                for kk in range(KD):
                    ins = mm(ps[0:n, 6, 0:GRP + NE], h2t[:, kk, 0:n], b.rw[:, kk, :], start=(kk == 0),
                             stop=(kk == KD - 1))
                ins.then_inc(logits, 1)

            pe.wait_ge(w_in, 32)
            for t in range(TILES):
                n = rows(t)
                if t >= 2:
                    pe.wait_ge(x1_ok, t - 1)
                for c in range(2):
                    for kk in range(KD):
                        ins = mm(ps[0:n, 2 * (t % 2) + c, :], b.yt[:, kk, t * P:t * P + n],
                                 wo[:, kk, c * 512:c * 512 + 512], start=(kk == 0), stop=(kk == KD - 1))
                ins.then_inc(prod, 1)
                if t >= 1:
                    turn_and_route(t - 1)
            turn_and_route(TILES - 1)
            pe.wait_ge(vr, 30)
            rhs = r["os"][:, :, :, :].rearrange("p t g e -> p (t g e)")
            pe.wait_ge(x1_ok, TILES)
            mm(ps[:, 0, 0:NE * TILES], b.before[:, :], rhs, start=True, stop=True)
            mm(ps[:, 1, 0:NE * TILES], b.ones[:, :], rhs, start=True, stop=True).then_inc(counted, 1)


ROUTE_STEPS = 71


def expert_slots(m, b):
    slots = []
    for k, at in enumerate((b.R2, b.R2 + 24576, b.R1, b.R1 + 24576)):
        slots.append((m.place(f"wg{k}", [P, KD, FF], at=at), m.place(f"wu{k}", [P, KD, FF], at=at + 8192),
                      m.place(f"wd{k}", [P, KF, D], at=at + 16384)))
    return slots


def load_expert(eng, b, io, e, k, sem=None):
    wg, wu, wd = b.slots[k]
    sem = b.w_landed[k] if sem is None else sem
    e1 = bass.ds(e, 1)
    eng.dma_start(wg[:, :, :], io.w_gate[e1].rearrange("a (p k) f -> (a p) k f", k=KD)).then_inc(sem, 16)
    eng.dma_start(wu[:, :, :], io.w_up[e1].rearrange("a (p k) f -> (a p) k f", k=KD)).then_inc(sem, 16)
    eng.dma_start(wd[:, :, :], io.w_down[e1].rearrange("a (f p) d -> (a p) f d", p=P)).then_inc(sem, 16)


class StepSems:

    def __init__(self, q):
        self.turned, self.xt_ok, self.gu_ok, self.tanh_ok = q["turned"], q["xt_ok"], q["gu_ok"], q["tanh_ok"]
        self.ge_ok, self.he_ok, self.down_ok = q["ge_ok"], q["he_ok"], q["down_ok"]
        self.outa_ok, self.outb_ok, self.scattered = q["outa_ok"], q["outb_ok"], q["scattered"]


def expert_stage(nc, m, s, b, io):
    ps = b.psum
    m.at = b.R3
    xg = [m.place(f"xg{k}", [C, D]) for k in range(4)]
    xt = [m.place(f"xgt{k}", [P, KD, C]) for k in range(2)]
    th = [m.place(f"thx{k}", [P, KF, C]) for k in range(2)]
    ge = [m.place(f"ge{k}", [P, KF, C]) for k in range(2)]
    he = [m.place(f"he{k}", [P, KF, C]) for k in range(2)]
    m.at = b.R5
    out = [m.place(f"out{k}", [C, D]) for k in range(2)]
    assert m.at <= b.R2
    tb32 = b.tb[:, :, :].bitcast(F32)
    names = "turned xt_ok gu_ok tanh_ok ge_ok he_ok down_ok outa_ok outb_ok scattered".split()
    q = {n: s.pair("e_" + n) for n in names}
    gathered = s.pair("e_gathered", 4)
    main = [StepSems({n: q[n][p] for n in names}) for p in range(2)]
    more = StepSems({n: s("v_" + n) for n in names})
    more_w, more_gathered = s("v_w"), s("v_gathered")



    def gather(pool, k, e, done):
        pool.indirect_dma_start(xg[k][:, :], None, b.h2_dram,
                                bass.IndirectOffsetOnAxis(ap=b.tb[:, e, 0:1].bitcast(U32), axis=0),
                                bounds_check=TOK - 1, oob_is_err=False).then_inc(done, 16)

    def scatter(pool, q, p, n, e):
        pool.wait_ge(q.outa_ok, n + 1)
        pool.wait_ge(q.outb_ok, n + 1)
        pool.indirect_dma_start(b.ye, bass.IndirectOffsetOnAxis(ap=b.tb[:, e, 1:2].bitcast(U32), axis=0),
                                out[p][:, :], None, bounds_check=2 * TOK - 1, oob_is_err=False
                                ).then_inc(q.scattered, 16)

    def turn(pe, q, k):
        for g in range(2):
            for j in range(4):
                kk = 4 * g + j
                ins = nc.tensor.transpose(ps[:, 2 + g, j * P:j * P + C], xg[k][:, kk:kk + KD * (P - 1) + 1:KD],
                                          b.ident[0:C, 0:C])
        ins.then_inc(q.turned, 1)

    def copy_turned(act, q, p, n):
        act.wait_ge(q.turned, n + 1)
        if later(n):
            act.wait_ge(q.gu_ok, n)
        for g in range(2):
            nc.scalar.activation(xt[p][:, 4 * g:4 * g + 4, :], bank4(ps, 2 + g, P, C), ACT.Copy
                                 ).then_inc(q.xt_ok, 1)

    def gate_up(pe, q, p, n, k):
        pe.wait_ge(q.xt_ok, 2 * n + 2)
        for g in range(2):
            for f in range(KF):
                o = (g * KF + f) * P
                for kk in range(KD):
                    ins = nc.tensor.matmul(ps[:, p, o:o + C], b.slots[k][g][:, kk, f * P:f * P + P],
                                           xt[p][:, kk, :], start=(kk == 0), stop=(kk == KD - 1))
        ins.then_inc(q.gu_ok, 1)

    def tanh(act, q, p, n):
        act.wait_ge(q.gu_ok, n + 1)
        nc.scalar.activation(th[p][:, :, :], bank4(ps, p, P, C)[:, 0:KF], ACT.Tanh, scale=0.5).then_inc(q.tanh_ok, 1)

    def swiglu(dve, q, p, n):
        dve.wait_ge(q.tanh_ok, n + 1)
        g = bank4(ps, p, P, C)
        nc.vector.scalar_tensor_tensor(ge[p][:, :, :], th[p][:, :, :], 1.0, g[:, 0:KF], ALU.add, ALU.mult
                                       ).then_inc(q.ge_ok, 1)
        dve.wait_ge(q.ge_ok, n + 1)
        nc.vector.scalar_tensor_tensor(he[p][:, :, :], ge[p][:, :, :], 0.5, g[:, KF:2 * KF], ALU.mult, ALU.mult
                                       ).then_inc(q.he_ok, 1)

    def down(pe, q, p, n, k):
        pe.wait_ge(q.he_ok, n + 1)
        if later(n):
            pe.wait_ge(q.outa_ok, n)
            pe.wait_ge(q.outb_ok, n)
        for c in range(2):
            for f in range(KF):
                ins = nc.tensor.matmul(ps[0:C, 4 + 2 * p + c, :], he[p][:, f, :],
                                       b.slots[k][2][:, f, c * 512:c * 512 + 512], start=(f == 0), stop=(f == KF - 1))
        ins.then_inc(q.down_ok, 1)

    def weight(e):
        return tb32[:, bass.ds(e, 1), 2:3].rearrange("p a c -> p (a c)")

    def weigh_a(act, q, p, n, e):
        act.wait_ge(q.down_ok, n + 1)
        if later(n):
            act.wait_ge(q.scattered, 16 * n)
        nc.scalar.activation(out[p][:, 0:512], ps[0:C, 4 + 2 * p, :], ACT.Copy, scale=weight(e)
                             ).then_inc(q.outa_ok, 1)

    def weigh_b(dve, q, p, n, e):
        dve.wait_ge(q.down_ok, n + 1)
        if later(n):
            dve.wait_ge(q.scattered, 16 * n)
        nc.vector.tensor_scalar(out[p][:, 512:D], ps[0:C, 5 + 2 * p, :], weight(e), None, ALU.mult
                                ).then_inc(q.outb_ok, 1)

    def block_of(j, i=0):
        x = Shared()
        x.e, x.p, x.n, x.k, x.r, x.q = 4 * i + j, j % 2, 2 * i + j // 2, j % 4, i + j // 4, main[j % 2]
        x.last, x.last_n = main[1 - j % 2], 2 * i + (j + 1) // 2
        return x

    def staggered(eng, front, mid, back):
        front(block_of(0))
        front(block_of(1))
        mid(block_of(0))
        for j in range(4):
            front(block_of(j + 2))
            mid(block_of(j + 1))
            back(block_of(j))
        with eng.Fori(1, 7) as i:
            for j in range(4):
                front(block_of(j + 2, i))
                mid(block_of(j + 1, i))
                back(block_of(j, i))
        for e in (30, 31):
            front(block_of(e))
            mid(block_of(e - 1))
            back(block_of(e - 2))
        mid(block_of(31))
        back(block_of(30))
        back(block_of(31))

    def further(eng, body):
        count = eng.value_load(b.ove[0:1, OV:OV + 1], min_val=0, max_val=OV)
        with eng.If_lt(eng.to_reg(0), eng.to_reg(count)):
            body(0)
        with eng.Fori(1, OV) as v:
            with eng.If_lt(eng.to_reg(v), eng.to_reg(count)):
                body(v)

    def nothing(x):
        pass

    with nc.Block() as block:
        @block.sync
        def _(sp):
            for e in (2, 3):
                load_expert(sp, b, io, e, e)
            with sp.Fori(0, 7) as i:
                for k in range(4):
                    sp.wait_ge(main[k % 2].down_ok, 2 * i + k // 2 + 1)
                    load_expert(sp, b, io, 4 * i + 4 + k, k)
            sp.wait_ge(main[0].down_ok, NE // 2)

            def body(v):
                if later(v):
                    sp.wait_ge(more.down_ok, v)
                e = sp.value_load(b.ove[0:1, bass.ds(v, 1)], min_val=0, max_val=NE - 1)
                load_expert(sp, b, io, e, 0, more_w)
            further(sp, body)

        @block.gpsimd
        def _(pool):
            for k in range(4):
                gather(pool, k, k, gathered[k])
            for e in range(NE):
                x = block_of(e)
                if e + 4 < NE:
                    pool.wait_ge(x.q.turned, x.n + 1)
                    gather(pool, x.k, e + 4, gathered[x.k])
                scatter(pool, x.q, x.p, x.n, e)
            for p in range(2):
                pool.wait_ge(main[p].scattered, 16 * (NE // 2))
            count = pool.value_load(b.ove[0:1, OV:OV + 1], min_val=0, max_val=OV)
            for v in range(OV):
                with pool.If_lt(pool.to_reg(v), pool.to_reg(count)):
                    gather(pool, 0, NE + v, more_gathered)
                    scatter(pool, more, 0, v, NE + v)
                    pool.wait_ge(more.scattered, 16 * (v + 1))

        @block.scalar
        def _(act):
            def back(x):
                weigh_a(act, x.q, x.p, x.n, x.e)
            staggered(act, lambda x: copy_turned(act, x.q, x.p, x.n), lambda x: tanh(act, x.q, x.p, x.n), back)

            def body(v):
                copy_turned(act, more, 0, v)
                tanh(act, more, 0, v)
                weigh_a(act, more, 0, v, NE + v)
            further(act, body)

        @block.vector
        def _(dve):
            staggered(dve, nothing, lambda x: swiglu(dve, x.q, x.p, x.n),
                      lambda x: weigh_b(dve, x.q, x.p, x.n, x.e))

            def body(v):
                swiglu(dve, more, 0, v)
                weigh_b(dve, more, 0, v, NE + v)
            further(dve, body)

        @block.tensor
        def _(pe):
            def front(x):
                if later(x.last_n):
                    pe.wait_ge(x.last.xt_ok, 2 * x.last_n)
                pe.wait_ge(gathered[x.k], 16 * (x.r + 1))
                turn(pe, x.q, x.k)

            def mid(x):
                pe.wait_ge(b.w_landed[x.k], 48 * (x.r + 1))
                gate_up(pe, x.q, x.p, x.n, x.k)

            staggered(pe, front, mid, lambda x: down(pe, x.q, x.p, x.n, x.k))
            for p in range(2):
                pe.wait_ge(main[p].outa_ok, NE // 2)
                pe.wait_ge(main[p].outb_ok, NE // 2)

            def body(v):
                pe.wait_ge(more_gathered, 16 * (v + 1))
                turn(pe, more, 0)
                pe.wait_ge(more_w, 48 * (v + 1))
                gate_up(pe, more, 0, v, 0)
                down(pe, more, 0, v, 0)
            further(pe, body)


def final_stage(nc, m, s, b, io):
    m.at = b.R2
    y0 = [m.place(f"y0{k}", [P, D]) for k in range(2)]
    y1 = [m.place(f"y1{k}", [P, D]) for k in range(2)]
    o = [m.place(f"fo{k}", [P, D]) for k in range(2)]
    wn = m.place("wn", [P, D])
    w_in, e_in, add0, x2_ok, sq, ln, rs, o_ok, left = (
        s("wn_in"), s.pair("ye_in"), s("f_add"), s("x2_ok"), s("f_sq"), s("f_ln"), s("f_rs"), s("f_ok"),
        s.pair("y_out"))

    def rows(t):
        return P if t < 8 else LAST

    with nc.Block() as block:
        @block.sync
        def _(sp):
            sp.dma_start(wn[:, :], io.norm_final.partition_broadcast(P)).then_inc(w_in, 16)
            for t in range(TILES):
                n, p = rows(t), t % 2
                if t >= 2:
                    sp.wait_ge(x2_ok, t - 1)
                sp.dma_start(y0[p][0:n, :], b.ye[t * P:t * P + n, :]).then_inc(e_in[p], 16)
                sp.dma_start(y1[p][0:n, :], b.ye[TOK + t * P:TOK + t * P + n, :]).then_inc(e_in[p], 16)

        @block.gpsimd
        def _(pool):
            for t in range(TILES):
                n, p = rows(t), t % 2
                pool.wait_ge(e_in[p], 32 * (t // 2 + 1))
                nc.gpsimd.tensor_tensor(y0[p][0:n, :], y0[p][0:n, :], y1[p][0:n, :], ALU.add).then_inc(add0, 1)

        @block.scalar
        def _(act):
            def send(t):
                n, p = rows(t), t % 2
                act.wait_ge(o_ok, t + 1)
                act.dma_start(io.y[t * P:t * P + n, :], o[p][0:n, :]).then_inc(left[p], 16)

            for t in range(TILES):
                n, p = rows(t), t % 2
                act.wait_ge(x2_ok, t + 1)
                if t >= 2:
                    act.wait_ge(left[p], 16 * (t // 2))
                nc.scalar.activation(o[p][0:n, :], b.x1[0:n, t, :], ACT.Square, accum_out=b.stat[0:n, t, 0:1]
                                     ).then_inc(sq, 1)
                act.wait_ge(sq, t + 1)
                nc.scalar.activation(b.stat[0:n, t, 1:2], b.stat[0:n, t, 0:1], ACT.Ln, scale=1.0 / D,
                                     bias=b.eps[0:n, :]).then_inc(ln, 1)
                act.wait_ge(ln, t + 1)
                nc.scalar.activation(b.stat[0:n, t, 2:3], b.stat[0:n, t, 1:2], ACT.Exp, scale=-0.5).then_inc(rs, 1)
                if t >= 1:
                    send(t - 1)
            send(TILES - 1)
            act.wait_ge(left[0], 16 * 5)
            act.wait_ge(left[1], 16 * 4)

        @block.vector
        def _(dve):
            dve.wait_ge(w_in, 16)

            def scale(t):
                n, p = rows(t), t % 2
                dve.wait_ge(rs, t + 1)
                nc.vector.scalar_tensor_tensor(o[p][0:n, :], b.x1[0:n, t, :], b.stat[0:n, t, 2:3], wn[0:n, :],
                                               ALU.mult, ALU.mult).then_inc(o_ok, 1)

            for t in range(TILES):
                n, p = rows(t), t % 2
                dve.wait_ge(add0, t + 1)
                nc.vector.tensor_tensor(b.x1[0:n, t, :], b.x1[0:n, t, :], y0[p][0:n, :], ALU.add).then_inc(x2_ok, 1)
                if t >= 1:
                    scale(t - 1)
            scale(TILES - 1)


def dump(nc, s, b, dumps):
    with nc.Block() as block:
        @block.sync
        def _(sp):
            for out, src in dumps(b):
                sp.dma_start(out, src).then_inc(s("dumped"), 16)
                sp.wait_ge(s("dumped"), 16)


def laid_out(inputs):
    import numpy as np

    a = {k: np.asarray(v) for k, v in inputs.items()}
    f = np.ascontiguousarray
    w_in = a["w_in"][0]
    blocks = w_in[:, :NBLK * P].reshape(KD, P, NBLK, P)
    order = [q for g in range(CA) for q in (CA + g, 2 * CA + g, g)] + list(range(3 * CA, NBLK))
    return {
        "x": f(np.concatenate([a["meta_tokens"], a["x_prompt"][0], a["x_sample"][:, 0]], axis=0)),
        "w_in": f(blocks[:, :, order].transpose(2, 1, 0, 3)),
        "w_ab": f(w_in[:, NBLK * P:].reshape(KD, P, 8).transpose(1, 0, 2)),
        "conv_a": f(a["conv_a_w"][0].reshape(KA, CA, P).transpose(2, 1, 0)),
        "conv_q": f(a["conv_qkv_w"][0].reshape(KQ, QKV, P).transpose(2, 1, 0)),
        "hist_a": f(a["state_conv_a"][0].reshape(SAMPLES, KA - 1, CA, P).transpose(3, 2, 0, 1)),
        "hist_q": f(a["state_conv_qkv"][0].reshape(SAMPLES, KQ - 1, QKV, P).transpose(3, 2, 0, 1)),
        "ssm": f(a["state_ssm"][0]),
        "a_log": f(a["a_log"][0]),
        "dt_bias": f(a["dt_bias"][0]),
        "o_norm": f(a["o_norm"][0].reshape(P, 1)),
        "norm_mix": f(a["norm_mix"][0]),
        "norm_ffn": f(a["norm_ffn"][0]),
        "norm_final": f(a["norm_final"]),
        "w_out": f(a["w_out"][0].reshape(KD, P, D).transpose(1, 0, 2)),
        "r_w": f(np.concatenate([a["router_group_w"][0], a["router_expert_w"][0]], axis=1)
                 .reshape(KD, P, GRP + NE).transpose(1, 0, 2)),
        "r_b": f(np.concatenate([a["router_group_b"][0], a["router_expert_b"][0]])),
        "w_gate": f(a["w_gate"][0]),
        "w_up": f(a["w_up"][0]),
        "w_down": f(a["w_down"][0]),
    }


OUTPUTS = {
    "y": (TOK, D),
    "new_hist": (P, CA + QKV, RLEN - PROMPT),
    "new_ssm_prompt": (H, P, P),
    "new_ssm_sample": (SAMPLES, H, P, P),
}


def kernel(**inputs):
    import concourse.bacc as bacc
    import numpy as np
    from concourse.bass_utils import run_bass_kernel_spmd

    arrays = laid_out(inputs)
    nc = bacc.Bacc("TRN2", target_bir_lowering=False, num_devices=1)
    args = {}
    for name, a in arrays.items():
        args[name] = nc.dram_tensor(name, a.shape, mybir.dt.from_np(a.dtype), kind="ExternalInput").ap()
    for name, shape in OUTPUTS.items():
        args[name] = nc.dram_tensor(name, shape, F32, kind="ExternalOutput").ap()
    build(nc, **args)
    r = run_bass_kernel_spmd(nc, [arrays], core_ids=[0]).results[0]
    y, hist = r["y"], r["new_hist"]
    ch = hist.transpose(2, 1, 0)
    ha = ch[:, :CA].reshape(-1, CA * P)
    hq = ch[:, CA:].reshape(-1, QKV * P)
    conv_a_sample = np.stack([ha[2 + KA * k + 1:2 + KA * k + KA] for k in range(SAMPLES)])
    conv_q_sample = np.stack([hq[3 + KQ * k + 1:3 + KQ * k + KQ] for k in range(SAMPLES)])
    return (y[None, META:PROMPT], y[PROMPT:, None], ha[None, None, 0:KA - 1], hq[None, None, 0:KQ - 1],
            r["new_ssm_prompt"][None, None], conv_a_sample[None], conv_q_sample[None], r["new_ssm_sample"][None])
```

```python
import concourse.bass as bass
from concourse import mybir

F32 = mybir.dt.float32
F32R = mybir.dt.float32r
I32 = mybir.dt.int32
U32 = mybir.dt.uint32
ALU = mybir.AluOpType
ACT = mybir.ActivationFunctionType
AX = mybir.AxisListType

P = 128
D = 1024
KD = D // P
SEQ, META, SAMPLES = 1024, 16, 8
PROMPT = SEQ + META
TOK = PROMPT + SAMPLES
ZC = 350
TP = 3 * ZC
TILES = 9
LAST = TOK - 8 * P
TAIL = PROMPT - 8 * P
CA = 4
H = 4
QK = 2 * H
QKV = 3 * H
KA, KQ = 3, 4
NBLK = 28
GRP, EPG, NE = 4, 8, 32
FF = 256
KF = FF // P
C = 96
OV = 21
PARTS = 11
NB = NE + OV
NOWHERE = 4 * TOK
EPS = 1e-6
RLEN = 3 + PROMPT + SAMPLES * KQ
QLEN = RLEN - (KQ - 1)
ALEN = 2 + PROMPT + SAMPLES * KA
QS = PROMPT + KQ - 1
AS = PROMPT + KA - 1
(K_G, K_CUM, K_BETA, K_NRK, K_BRK, K_NBRKE, K_E, K_RQ, K_RK) = range(9)
NK = 9
LEVELS = 7
NEG = -1.0e30


class Memory:

    def __init__(self, nc):
        self.nc = nc
        self.base = (nc.sbuf_base + 63) // 64 * 64
        self.end = nc.sbuf_usable_end
        self.at = self.base
        self.count = 0

    def place(self, name, shape, dt=F32, at=None):
        size = 4
        for s in shape[1:]:
            size *= s
        where = self.at if at is None else at
        t = self.nc.alloc_sbuf_tensor_at(name, shape, dt, offset=where)
        assert where + size <= self.end, (name, where + size - self.end)
        self.next = (where + size + 31) // 32 * 32
        if at is None:
            self.at = self.next
        return t


def bc(ap, n):
    return ap.unsqueeze(len(ap.shape)).broadcast_to(list(ap.shape) + [n])


def bc1(ap, n):
    return ap.unsqueeze(1).broadcast_to([ap.shape[0], n] + list(ap.shape[1:]))


def later(i):
    return not isinstance(i, int) or i > 0


class Shared:
    pass


class Sems:

    def __init__(self, nc):
        self.nc, self.made = nc, {}

    def __call__(self, name):
        if name not in self.made:
            self.made[name] = self.nc.alloc_semaphore(name)
        return self.made[name]

    def pair(self, name, n=2):
        return [self(f"{name}{k}") for k in range(n)]

    def begin(self):
        self.before = set(self.made)

    def end(self, keep=()):
        names = [n for n in self.made if n not in self.before and n not in keep]
        self.nc.clear_and_free_semaphores([self.made.pop(n) for n in names])
        self.nc.all_engine_barrier()


def build(nc, x, w_in, w_ab, conv_a, conv_q, hist_a, hist_q, ssm, a_log, dt_bias, o_norm, norm_mix, norm_ffn,
          norm_final, w_out, r_w, r_b, w_gate, w_up, w_down, y, new_hist, new_ssm_prompt, new_ssm_sample):
    m = Memory(nc)
    s = Sems(nc)
    b = Shared()
    io = Shared()
    io.x, io.w_in, io.w_ab, io.conv_a, io.conv_q, io.hist_a, io.hist_q = x, w_in, w_ab, conv_a, conv_q, hist_a, hist_q
    io.ssm, io.a_log, io.dt_bias, io.o_norm, io.norm_mix, io.norm_ffn = ssm, a_log, dt_bias, o_norm, norm_mix, norm_ffn
    io.norm_final, io.w_out, io.r_w, io.r_b, io.w_gate, io.w_up, io.w_down = (
        norm_final, w_out, r_w, r_b, w_gate, w_up, w_down)
    io.y, io.new_hist, io.new_ssm_prompt, io.new_ssm_sample = y, new_hist, new_ssm_prompt, new_ssm_sample
    b.psum = nc.alloc_psum_tensor("psum", [P, 8, 512], F32)
    b.h2_dram = nc.dram_tensor("h2_rows", (TOK, D), F32, kind="Internal").ap()
    b.ye = nc.dram_tensor("expert_rows", (2 * TOK, D), F32, kind="Internal").ap()

    b.ident = m.place("ident", [P, P])
    b.upto = m.place("upto", [P, P])
    b.before = m.place("before", [P, P])
    b.ones = m.place("ones", [P, P])
    b.negmask = m.place("negmask", [P, P])
    b.levels = m.place("levels", [P, LEVELS, 64])
    b.cqw = m.place("cqw", [P, QKV, KQ])
    b.caw = m.place("caw", [P, CA, KA])
    b.hq = m.place("hq", [P, QKV, SAMPLES, KQ - 1])
    b.ha = m.place("ha", [P, CA, SAMPLES, KA - 1])
    b.col = m.place("col", [P, 10, NK, H])
    b.alog = m.place("alog", [P, H])
    b.dtb = m.place("dtb", [P, H])
    b.onw = m.place("onw", [P, 1])
    b.eps = m.place("eps", [P, 1])
    b.stat = m.place("stat", [P, TILES, 4])
    b.rb = m.place("rb", [P, GRP + NE])
    b.rw = m.place("rw", [P, KD, GRP + NE])
    b.valid = m.place("valid", [P, TILES])
    b.state = m.place("state", [P, H, P])
    b.slot_rows = m.place("slot_rows", [C, 2, NE + OV], I32)
    b.slot_w = m.place("slot_w", [C, NE + OV])
    b.ove = m.place("ove", [P, OV + 1], I32)
    m.at = (m.at + 63) // 64 * 64
    b.R1 = m.at
    b.hh = m.place("hh", [P, KD, TP], F32R)
    b.hl = m.place("hl", [P, KD, TP], F32R)
    b.R4 = m.at
    b.wst = [m.place(f"wst{k}", [P, KD, P]) for k in range(2)]
    b.wh = [m.place(f"wh{k}", [P, KD, P], F32R) for k in range(2)]
    b.wl = [m.place(f"wl{k}", [P, KD, P], F32R) for k in range(2)]
    b.tmp = [m.place(f"tmp{k}", [P, RLEN]) for k in range(5)]
    b.R2 = m.at
    b.qkv = m.place("qkv", [P, QKV, QLEN])
    b.R3 = m.at
    b.yt = m.place("yt", [P, KD, TP])
    b.hist = m.place("hist", [P, CA + QKV, RLEN - PROMPT])

    first_stage(nc, m, s, b, io)
    s.begin()
    delta_stage(nc, m, s, b, io)
    s.end()
    sample_stage(nc, m, s, b, io)
    route_stage(nc, m, s, b, io)
    expert_stage(nc, m, s, b, io)
    final_stage(nc, m, s, b, io)


def every(ap, first, step):
    return ap[:, first:first + step * (SAMPLES - 1) + 1:step]


def bank4(ps, bank, m, n):
    return ps[0:m, bank, :].rearrange("p (h n) -> p h n", h=4)[:, :, 0:n]


def z_bank(k):
    return 3 * k


def z_in(ps, k):
    return ps[:, 3 * k:3 * k + 3, 0:ZC]


def thirds(ap, off=0):
    return ap[:, off:off + TP].rearrange("p (c n) -> p c n", c=3)


def make_constants(pool, nc, s, b):
    done = s("constants")
    n = 0

    def step(ins):
        nonlocal n
        n += 1
        ins.then_inc(done, 1)
        pool.wait_ge(done, n)

    step(nc.gpsimd.memset(b.ident[:, :], 0.0))
    step(nc.gpsimd.memset(b.upto[:, :], 1.0))
    step(nc.gpsimd.memset(b.before[:, :], 1.0))
    step(nc.gpsimd.memset(b.ones[:, :], 1.0))
    step(nc.gpsimd.memset(b.negmask[:, :], 0.0))
    step(nc.gpsimd.memset(b.levels[:, :, :], 1.0))
    step(nc.gpsimd.memset(b.eps[:, :], EPS))
    step(nc.gpsimd.memset(b.valid[:, :], 1.0))
    sel = nc.gpsimd.affine_select
    step(sel(out=b.ident[:, :], in_=b.ident[:, :], compare_op=ALU.not_equal, fill=1.0, base=0,
             pattern=[[-1, P]], channel_multiplier=1))
    step(sel(out=b.upto[:, :], in_=b.upto[:, :], compare_op=ALU.is_ge, fill=0.0, base=0,
             pattern=[[1, P]], channel_multiplier=-1))
    step(sel(out=b.before[:, :], in_=b.before[:, :], compare_op=ALU.is_gt, fill=0.0, base=0,
             pattern=[[1, P]], channel_multiplier=-1))
    step(sel(out=b.negmask[:, :], in_=b.negmask[:, :], compare_op=ALU.is_ge, fill=NEG, base=0,
             pattern=[[1, P]], channel_multiplier=-1))
    step(sel(out=b.valid[:, 8:9], in_=b.valid[:, 8:9], compare_op=ALU.is_gt, fill=0.0, base=LAST,
             pattern=[[0, 1]], channel_multiplier=-1))
    for lv in range(LEVELS):
        z = 1 << lv
        v = b.levels[:, lv, :].rearrange("p (b r) -> p b r", r=z)
        step(sel(out=v, in_=v, compare_op=ALU.is_ge, fill=0.0, base=0,
                 pattern=[[-2 * z, 64 // z], [0, z]], channel_multiplier=1))
        step(sel(out=v, in_=v, compare_op=ALU.is_gt, fill=0.0, base=z,
                 pattern=[[2 * z, 64 // z], [0, z]], channel_multiplier=-1))
    return n


CONSTANTS = 13 + 2 * LEVELS


def first_stage(nc, m, s, b, io):
    ps = b.psum
    xb = [m.place(f"xb{k}", [P, D], at=b.R2 + 4096 * k) for k in range(2)]
    hb = [m.place(f"hb{k}", [P, D], at=b.R2 + 8192 + 4096 * k) for k in range(2)]
    junk = m.place("junk", [P, D], at=b.R2 + 16384)
    wbc = m.place("wbc", [P, D], at=b.R2 + 20480)
    wab = m.place("wab", [P, KD, 8], at=b.R2 + 24576)
    wabh = m.place("wabh", [P, KD, 8], F32R, at=m.next)
    wabl = m.place("wabl", [P, KD, 8], F32R, at=m.next)
    ab = b.tmp[4][0:8, 0:TP]
    small, ab_copied = s("small_loaded"), s("ab_copied")
    x_in = s.pair("x_in")
    squared, logged, rstd, normed = s("squared"), s("logged"), s("rstd"), s("normed")
    turned, hi_ok, lo_ok = s("turned"), s("hi_ok"), s("lo_ok")
    w_landed, whi, wlo = s.pair("w_landed"), s("whi"), s("wlo")
    z_done, z_used = s.pair("z_done"), s.pair("z_used")
    wab_hi, wab_lo, ab_ok, zeroed = s("wab_hi"), s("wab_lo"), s("ab_ok"), s("zeroed")
    ch_ok, a_product, acc_ok, ya_main = s("ch_ok"), s("a_product"), s("acc_ok"), s("ya_main")
    raw_main, raw, taps, conv, th_ok, silu = (s("raw_main"), s("raw"), s("taps"), s("conv"), s("th_ok"), s("silu"))
    gth_ok, squares, sums, kept, scaled = s("gth_ok"), s("squares"), s("sums"), s("kept"), s("scaled")

    def rows(t):
        return P if t < 8 else LAST

    with nc.Block() as block:
        @block.sync
        def _(sp):
            for t in range(TILES):
                if t == 2:
                    sp.dma_start(wbc[:, :], io.norm_mix.partition_broadcast(P)).then_inc(small, 16)
                    sp.dma_start(wab[:, :, :], io.w_ab).then_inc(small, 16)
                    sp.dma_start(b.cqw[:, :, :], io.conv_q).then_inc(small, 16)
                    sp.dma_start(b.caw[:, :, :], io.conv_a).then_inc(small, 16)
                    sp.dma_start(b.hq[:, :, :, :], io.hist_q).then_inc(small, 16)
                    sp.dma_start(b.ha[:, :, :, :], io.hist_a).then_inc(small, 16)
                    sp.dma_start(b.alog[:, :], io.a_log.partition_broadcast(P)).then_inc(small, 16)
                    sp.dma_start(b.dtb[:, :], io.dt_bias.partition_broadcast(P)).then_inc(small, 16)
                    sp.dma_start(b.onw[:, :], io.o_norm).then_inc(small, 16)
                    sp.dma_start(b.rw[:, :, :], io.r_w).then_inc(small, 16)
                    sp.dma_start(b.rb[:, :], io.r_b.partition_broadcast(P)).then_inc(small, 16)
                if t >= 2:
                    sp.wait_ge(normed, t - 1)
                sp.dma_start(xb[t % 2][0:rows(t), :], io.x[t * P:t * P + rows(t), :]).then_inc(x_in[t % 2], 16)
            for n in range(2):
                sp.dma_start(b.wst[n][:, :, :], io.w_in[n]).then_inc(w_landed[n], 16)
            with sp.Fori(0, NBLK // 2 - 1) as i:
                for k in range(2):
                    sp.wait_ge(wlo, 2 * i + k + 1)
                    sp.dma_start(b.wst[k][:, :, :], io.w_in[bass.ds(2 * i + 2 + k, 1)]
                                 .rearrange("a p k c -> (a p) k c")).then_inc(w_landed[k], 16)
            sp.wait_ge(kept, CA + QKV)
            sp.dma_start(io.new_hist, b.hist[:, :, :]).then_inc(s("hist_out"), 16)
            sp.wait_ge(s("hist_out"), 16)

        @block.gpsimd
        def _(pool):
            make_constants(pool, nc, s, b)
            def w_low(i):
                for k in range(2):
                    pool.wait_ge(whi, 2 * i + k + 1)
                    if later(i):
                        pool.wait_ge(z_done[k], i)
                    nc.gpsimd.tensor_tensor(b.wl[k][:, :, :], b.wst[k][:, :, :], b.wh[k][:, :, :].bitcast(F32),
                                            ALU.subtract).then_inc(wlo, 1)

            w_low(0)
            with pool.Fori(1, NBLK // 2) as i:
                w_low(i)

        @block.scalar
        def _(act):
            nc.scalar.preload_act_table_set("natural_log_exp_and_others")

            def high(t):
                n = rows(t)
                for g in range(2):
                    act.wait_ge(turned, 2 * t + g + 1)
                    nc.scalar.activation(b.hh[:, 4 * g:4 * g + 4, t * P:t * P + n], bank4(ps, 2 * (t % 2) + g, P, n),
                                         ACT.Copy).then_inc(hi_ok, 1)

            act.wait_ge(s("constants"), CONSTANTS)
            for t in range(TILES):
                n = rows(t)
                act.wait_ge(x_in[t % 2], 16 * (t // 2 + 1))
                nc.scalar.activation(junk[0:n, :], xb[t % 2][0:n, :], ACT.Square,
                                     accum_out=b.stat[0:n, t, 0:1]).then_inc(squared, 1)
                act.wait_ge(squared, t + 1)
                nc.scalar.activation(b.stat[0:n, t, 1:2], b.stat[0:n, t, 0:1], ACT.Ln, scale=1.0 / D,
                                     bias=b.eps[0:n, :]).then_inc(logged, 1)
                act.wait_ge(logged, t + 1)
                nc.scalar.activation(b.stat[0:n, t, 2:3], b.stat[0:n, t, 1:2], ACT.Exp, scale=-0.5).then_inc(rstd, 1)
                if t >= 1:
                    high(t - 1)
            high(TILES - 1)
            act.wait_ge(small, 16 * 11)
            nc.scalar.activation(wabh[:, :, :], wab[:, :, :], ACT.Copy).then_inc(wab_hi, 1)

            def w_high(n):
                i, k = n
                act.wait_ge(w_landed[k], 16 * (i + 1))
                if later(i):
                    act.wait_ge(z_done[k], i)
                nc.scalar.activation(b.wh[k][:, :, :], b.wst[k][:, :, :], ACT.Copy).then_inc(whi, 1)

            w_high((0, 0))
            w_high((0, 1))
            act.wait_ge(ab_ok, 1)
            nc.scalar.activation(thirds(ab), ps[0:8, 0:3, 0:ZC], ACT.Copy).then_inc(ab_copied, 1)
            with act.Fori(0, 2) as i:
                for g in range(2):
                    for q in range(3):
                        n = 3 * g + q
                        w_high((3 * i + (n + 2) // 2, n % 2))
                    act.wait_ge(a_product, 2 * i + g + 1)
                    nc.scalar.activation(b.hist[:, bass.ds(2 * i + g, 1), 0:ALEN - PROMPT]
                                         .rearrange("p a n -> p (a n)"),
                                         b.tmp[1][:, PROMPT:ALEN], ACT.Copy).then_inc(kept, 1)

            def q_k_v(i, k, blk, norms):
                w_high((i + 7, k))
                act.wait_ge(raw, blk + 1)
                nc.scalar.activation(b.hist[:, bass.ds(CA + blk, 1), :].rearrange("p a n -> p (a n)"),
                                     b.tmp[0][:, PROMPT:RLEN], ACT.Copy).then_inc(kept, 1)
                act.wait_ge(conv, blk + 1)
                nc.scalar.activation(b.tmp[3][:, 0:QLEN], b.tmp[2][:, 0:QLEN], ACT.Tanh).then_inc(th_ok, 1)
                if norms:
                    act.wait_ge(silu, blk + 1)
                    if later(blk):
                        act.wait_ge(sums, blk)
                    nc.scalar.activation(b.tmp[4][:, 0:QLEN],
                                         b.qkv[:, bass.ds(blk, 1), :].rearrange("p a n -> p (a n)"),
                                         ACT.Square).then_inc(squares, 1)

            for k in range(2):
                q_k_v(0, k, k, True)
            with act.Fori(1, QK // 2) as i:
                for k in range(2):
                    q_k_v(i, k, 2 * i + k, True)
            with act.Fori(QK // 2, QKV // 2) as i:
                for k in range(2):
                    q_k_v(i, k, 2 * i + k, False)
            act.wait_ge(silu, QKV)
            for n in range(24, NBLK):
                if n + 2 < NBLK:
                    w_high(((n + 2) // 2, n % 2))
                act.wait_ge(z_done[n % 2], n // 2 + 1)
                if n > 24:
                    act.wait_ge(z_used[(n - 1) % 2], (n - 1) // 2 + 1)
                nc.scalar.activation(thirds(b.tmp[3]), z_in(ps, n % 2), ACT.Tanh, scale=0.5).then_inc(gth_ok, 1)

        @block.vector
        def _(dve):
            def low(t):
                n = rows(t)
                for g in range(2):
                    dve.wait_ge(hi_ok, 2 * t + g + 1)
                    cols = slice(t * P, t * P + n)
                    nc.vector.tensor_tensor(b.hl[:, 4 * g:4 * g + 4, cols], bank4(ps, 2 * (t % 2) + g, P, n),
                                            b.hh[:, 4 * g:4 * g + 4, cols].bitcast(F32),
                                            ALU.subtract).then_inc(lo_ok, 1)

            for part in (b.hh, b.hl):
                nc.vector.memset(part[:, :, TOK:TP].bitcast(F32), 0.0)
            nc.vector.memset(b.tmp[0][:, 0:3], 0.0)
            nc.vector.memset(b.tmp[1][:, 0:2], 0.0)
            nc.vector.memset(b.hist[:, :, :], 0.0)
            nc.vector.memset(ps[:, 6:8, :], 0.0).then_inc(zeroed, 1)
            dve.wait_ge(small, 16 * 11)
            nc.vector.tensor_scalar(b.cqw[:, :, :], b.cqw[:, :, :], 0.5, None, ALU.mult).then_inc(scaled, 1)
            for t in range(TILES):
                n = rows(t)
                dve.wait_ge(rstd, t + 1)
                if t >= 2:
                    dve.wait_ge(turned, 2 * (t - 1))
                nc.vector.scalar_tensor_tensor(hb[t % 2][0:n, :], xb[t % 2][0:n, :], b.stat[0:n, t, 2:3],
                                               wbc[0:n, :], ALU.mult, ALU.mult).then_inc(normed, 1)
                if t >= 1:
                    low(t - 1)
            low(TILES - 1)
            dve.wait_ge(wab_hi, 1)
            nc.vector.tensor_tensor(wabl[:, :, :], wab[:, :, :], wabh[:, :, :].bitcast(F32),
                                    ALU.subtract).then_inc(wab_lo, 1)
            dve.wait_ge(ab_ok, 1)
            rawb, ch, acc, th = b.tmp[0], b.tmp[1], b.tmp[2], b.tmp[3]
            cc = th

            def mixer_a(i, g, grp):
                (i0, k0), (i1, k1), (i2, k2) = (((3 * g + q) // 2 + 3 * i, (3 * g + q) % 2) for q in range(3))
                dve.wait_ge(z_done[k0], i0 + 1)
                nc.vector.tensor_copy(thirds(cc), z_in(ps, k0)).then_inc(z_used[k0], 1)
                dve.wait_ge(z_done[k1], i1 + 1)
                dve.wait_ge(z_used[k0], i0 + 1)
                if later(grp):
                    dve.wait_ge(kept, grp)
                nc.vector.tensor_tensor(thirds(ch, 2), z_in(ps, k1), thirds(cc), ALU.mult).then_inc(ch_ok, 1)
                dve.wait_ge(ch_ok, grp + 1)
                nc.vector.tensor_tensor(every(ch, PROMPT + 4, KA), ps[:, z_bank(k1) + 2, 340:348],
                                        cc[:, PROMPT:TOK], ALU.mult).then_inc(z_used[k1], 1)
                for r in range(KA - 1):
                    ins = nc.vector.tensor_copy(every(ch, PROMPT + 2 + r, KA),
                                                b.ha[:, bass.ds(grp, 1), :, r].rearrange("p a n -> p (a n)"))
                ins.then_inc(a_product, 1)
                dve.wait_ge(a_product, grp + 1)
                dve.wait_ge(z_used[k1], i1 + 1)
                w = b.caw[:, bass.ds(grp, 1), :].rearrange("p a n -> p (a n)")
                n = ALEN - 2
                nc.vector.tensor_scalar(acc[:, 0:n], ch[:, 0:n], w[:, 0:1], None, ALU.mult).then_inc(acc_ok, 1)
                for r in range(1, KA):
                    dve.wait_ge(acc_ok, 3 * grp + r)
                    nc.vector.scalar_tensor_tensor(acc[:, 0:n], ch[:, r:r + n], w[:, r:r + 1], acc[:, 0:n],
                                                   ALU.mult, ALU.add).then_inc(acc_ok, 1)
                dve.wait_ge(acc_ok, 3 * grp + 3)
                dve.wait_ge(z_done[k2], i2 + 1)
                out = b.yt[:, bass.ds(grp, 1), :].rearrange("p a n -> p (a n)")
                nc.vector.tensor_tensor(thirds(out), z_in(ps, k2), thirds(acc), ALU.mult).then_inc(ya_main, 1)
                dve.wait_ge(ya_main, grp + 1)
                nc.vector.tensor_tensor(out[:, PROMPT:TOK], ps[:, z_bank(k2) + 2, 340:348],
                                        every(acc, AS, KA), ALU.mult).then_inc(z_used[k2], 1)

            def q_k_v(i, k, blk):
                dve.wait_ge(z_done[k], i + 7)
                dve.wait_ge(kept, CA + blk)
                nc.vector.tensor_copy(thirds(rawb, 3), z_in(ps, k)).then_inc(raw_main, 1)
                dve.wait_ge(raw_main, blk + 1)
                nc.vector.tensor_copy(every(rawb, PROMPT + 6, KQ),
                                      ps[:, z_bank(k) + 2, 340:348]).then_inc(z_used[k], 1)
                for r in range(KQ - 1):
                    ins = nc.vector.tensor_copy(every(rawb, PROMPT + 3 + r, KQ),
                                                b.hq[:, bass.ds(blk, 1), :, r].rearrange("p a n -> p (a n)"))
                ins.then_inc(raw, 1)
                dve.wait_ge(raw, blk + 1)
                dve.wait_ge(z_used[k], i + 7)
                w = b.cqw[:, bass.ds(blk, 1), :].rearrange("p a n -> p (a n)")
                nc.vector.tensor_scalar(acc[:, 0:QLEN], rawb[:, 0:QLEN], w[:, 0:1], None,
                                        ALU.mult).then_inc(taps, 1)
                for r in range(1, KQ):
                    dve.wait_ge(taps, 3 * blk + r)
                    nc.vector.scalar_tensor_tensor(acc[:, 0:QLEN], rawb[:, r:r + QLEN], w[:, r:r + 1],
                                                   acc[:, 0:QLEN], ALU.mult, ALU.add
                                                   ).then_inc(taps if r < KQ - 1 else conv, 1)
                dve.wait_ge(conv, blk + 1)
                dve.wait_ge(th_ok, blk + 1)
                nc.vector.scalar_tensor_tensor(b.qkv[:, bass.ds(blk, 1), :].rearrange("p a n -> p (a n)"),
                                               th[:, 0:QLEN], 1.0, acc[:, 0:QLEN], ALU.add,
                                               ALU.mult).then_inc(silu, 1)

            dve.wait_ge(scaled, 1)
            for grp in range(CA):
                mixer_a(grp // 2, grp % 2, grp)
            with dve.Fori(0, QKV // 2) as i:
                for k in range(2):
                    q_k_v(i, k, 2 * i + k)
            for n in range(24, NBLK):
                dve.wait_ge(gth_ok, n - 23)
                nc.vector.scalar_tensor_tensor(thirds(b.yt[:, CA + n - 24, :]), thirds(th), 1.0, z_in(ps, n % 2),
                                               ALU.add, ALU.mult).then_inc(z_used[n % 2], 1)

        @block.tensor
        def _(pe):
            pe.wait_ge(s("constants"), CONSTANTS)
            for t in range(TILES):
                n = rows(t)
                pe.wait_ge(normed, t + 1)
                for g in range(2):
                    if t >= 2:
                        pe.wait_ge(lo_ok, 2 * (t - 2) + g + 1)
                    for k in range(4):
                        kk = 4 * g + k
                        ins = nc.tensor.transpose(ps[:, 2 * (t % 2) + g, k * P:k * P + n],
                                                  hb[t % 2][0:n, kk * P:kk * P + P], b.ident[0:n, 0:n])
                    ins.then_inc(turned, 1)
            pe.wait_ge(lo_ok, 2 * TILES)
            pe.wait_ge(zeroed, 1)
            pe.wait_ge(wab_hi, 1)
            pe.wait_ge(wab_lo, 1)
            for kk in range(KD):
                for q, (w, a) in enumerate(((wabh, b.hh), (wabl, b.hh), (wabh, b.hl))):
                    for c in range(3):
                        ins = nc.tensor.matmul(ps[0:8, c, 0:ZC], w[:, kk, :], a[:, kk, c * ZC:(c + 1) * ZC],
                                               start=(kk == 0 and q == 0), stop=(kk == KD - 1 and q == 2))
            ins.then_inc(ab_ok, 1)
            pe.wait_ge(ab_copied, 1)
            for t in range(10):
                lo, n = (t * P, P) if t < 8 else ((8 * P, TAIL) if t == 8 else (PROMPT, SAMPLES))
                nc.tensor.transpose(ps[0:n, 6, 8 * t:8 * t + 8], ab[:, lo:lo + n], b.ident[0:8, 0:8])

            def product(n, i, k):
                pe.wait_ge(whi, n + 1)
                pe.wait_ge(wlo, n + 1)
                if later(i):
                    pe.wait_ge(z_used[k], i)
                for kk in range(KD):
                    for q, (w, a) in enumerate(((b.wh[k], b.hh), (b.wh[k], b.hl), (b.wl[k], b.hh))):
                        for c in range(3):
                            ins = nc.tensor.matmul(ps[:, z_bank(k) + c, 0:ZC], w[:, kk, :],
                                                   a[:, kk, c * ZC:(c + 1) * ZC],
                                                   start=(kk == 0 and q == 0), stop=(kk == KD - 1 and q == 2))
                ins.then_inc(z_done[k], 1)

            def square_sums(blk):
                pe.wait_ge(squares, blk + 1)
                for t in range(10):
                    sq = b.tmp[4][:, t * P:t * P + P] if t < 8 else (
                        b.tmp[4][:, 8 * P:PROMPT] if t == 8 else every(b.tmp[4], QS, KQ))
                    n = sq.shape[1]
                    ins = nc.tensor.matmul(ps[0:n, 7, bass.ds(blk + QK * t, 1)], sq, b.ones[:, 0:1],
                                           start=True, stop=True)
                ins.then_inc(sums, 1)

            product(0, 0, 0)
            product(1, 0, 1)
            with pe.Fori(1, 6) as i:
                for k in range(2):
                    product(2 * i + k, i, k)
            product(12, 6, 0)
            with pe.Fori(0, QK // 2) as i:
                for k in range(2):
                    product(2 * i + 13 + k, i + (13 + k) // 2, (13 + k) % 2)
                    square_sums(2 * i + k)
            with pe.Fori(0, 3) as i:
                for k in range(2):
                    product(2 * i + 21 + k, i + (21 + k) // 2, (21 + k) % 2)
            product(27, 13, 1)


def delta_stage(nc, m, s, b, io):
    ps = b.psum
    m.at = b.R1
    two = range(2)
    ck = [m.place(f"ck{p}", [P, QKV, P]) for p in two]
    cs = [m.place(f"cs{p}", [P, NK, H]) for p in two]
    bt = [[m.place(f"bt{p}_{lv}", [P, H, P]) for lv in range(LEVELS)] for p in two]
    m1 = [[m.place(f"m1{p}_{lv}", [P, H, P]) for lv in range(1, LEVELS)] for p in two]
    tm = [m.place(f"tm{p}", [P, H, P]) for p in two]
    tt = [m.place(f"tt{p}", [P, H, P]) for p in two]
    dt = [m.place(f"dt{p}", [P, H, P]) for p in two]
    at = [m.place(f"at{p}", [P, H, P]) for p in two]
    qa = [m.place(f"qa{p}", [P, H, P]) for p in two]
    kbe = [m.place(f"kbe{p}", [P, H, P]) for p in two]
    kd = [m.place(f"kd{p}", [P, H, P]) for p in two]
    vb = [m.place(f"vb{p}", [P, H, P]) for p in two]
    u = m.place("u", [P, H, P])
    o1 = m.place("o1", [P, H, P])
    oc = [m.place(f"oc{p}", [P, H, P]) for p in two]
    egl = [m.place(f"egl{p}", [P, H]) for p in two]
    gd = [m.place(f"gd{p}", [P, 3, H]) for p in two]
    os_ = [m.place(f"os{p}", [P, 4, H]) for p in two]
    pre = m.place("pre", [P, 10, 8, H])
    assert m.at <= b.R2, m.at - b.R2

    names = ("staged g_bank eg_ok d_ok gl_ok gle_ok dt_ok kk_ok qk_ok kt_ok vt_ok rb_ok at0_ok at_ok qa_ok kds_ok "
             "kbe_ok kd_ok vb_ok bt_ok t1_ok t_ok tt_ok mm_ok mcopy_ok dd_ok tnew_ok ttnew_ok wt_ok wtc_ok u_ok "
             "uc_ok o1_ok o1c_ok ku_ok o2_ok s_ok o_ok osq_ok oln_ok ors_ok ofac_ok on_ok ot_ok y_ok").split()
    q = {n: s.pair("d_" + n) for n in names}
    cols_ready, zero_ok = s("cols_ready"), s("state_zero")
    e_steps, v_steps, g_sum, out_sem = s("pre_act"), s("pre_vec"), s("g_sum"), s("ssm_out")
    M1Z = s("m1_zero")

    def half(buf, lv, n, t):
        return buf[0:n, :, 0:n].rearrange("p h (b t r) -> p h b t r", t=2, r=1 << lv)[:, :, :, t, :]

    def packed(bank, off, lv, n):
        return ps[0:n, bank, off:off + 64 * H].rearrange("p (h q) -> p h q", h=H)[:, :, 0:n // 2].rearrange(
            "p h (b r) -> p h b r", r=1 << lv)

    def last_level(n):
        return 6 if n == P else 3

    def groups(eng, body):
        body(0, [(0, 0, P), (1, 1, P)])
        with eng.Fori(1, 4) as i:
            body(i, [(2 * i, 0, P), (2 * i + 1, 1, P)])
        body(4, [(8, 0, TAIL)])

    def levels_before(i, lv):
        return 6 * i + lv - 1

    with nc.Block() as block:
        @block.sync
        def _(sp):
            sp.wait_ge(q["s_ok"][0], 5)
            sp.dma_start(io.new_ssm_prompt.rearrange("h k v -> k h v"), b.state[:, :, :]).then_inc(out_sem, 16)
            sp.wait_ge(out_sem, 16)

        @block.gpsimd
        def _(pool):
            for lv in range(LEVELS):
                nc.gpsimd.memset(bt[0][lv][:, :, :], 0.0)
            for lv in range(1, LEVELS):
                ins = nc.gpsimd.memset(m1[0][lv - 1][:, :, :], 0.0)
            ins.then_inc(M1Z, 1)
            pool.wait_ge(M1Z, 1)
            pool.wait_ge(cols_ready, 1)

            def body(i, chunks):
                for c, p, n in chunks:
                    if later(i):
                        pool.wait_ge(q["o1_ok"][p], i)
                    src = b.qkv[:, :, bass.ds(c * P, n)]
                    nc.gpsimd.tensor_copy(ck[p][:, :, 0:n], src)
                    if later(i):
                        pool.wait_ge(q["y_ok"][p], i)
                    nc.gpsimd.tensor_copy(cs[p][0:n, :, :].rearrange("p k h -> p (k h)"),
                                          b.col[0:n, bass.ds(c, 1), :, :].rearrange("p a k h -> p (a k h)")
                                          ).then_inc(q["staged"][p], 1)
                for c, p, n in chunks:
                    pool.wait_ge(q["at_ok"][p], i + 1)
                    for lv in range(last_level(n) + 1):
                        z = 1 << lv
                        mask = bc1(b.levels[0:n, lv, 0:n // 2].rearrange("p (b r) -> p b r", r=z), H)
                        nc.gpsimd.tensor_tensor(half(bt[p][lv], lv, n, 1), half(at[p], lv, n, 1), mask,
                                                ALU.mult).then_inc(q["bt_ok"][p], 1)
            groups(pool, body)

        @block.scalar
        def _(act):
            done = 0

            def step(ins):
                nonlocal done
                done += 1
                ins.then_inc(e_steps, 1)

            a_ = nc.scalar.activation
            nc.scalar.preload_act_table_set("natural_log_exp_and_others")
            act.wait_ge(v_steps, 1)
            step(a_(pre[:, :, 1, :], pre[:, :, 0, :], ACT.Abs))
            act.wait_ge(e_steps, 1)
            step(a_(pre[:, :, 2, :], pre[:, :, 1, :], ACT.Exp, scale=-1.0))
            act.wait_ge(e_steps, 2)
            step(a_(pre[:, :, 1, :], pre[:, :, 2, :], ACT.Ln, bias=b.ones[:, 0:1]))
            step(a_(pre[:, :, 3, :], ab_bank(ps, 4), ACT.Exp, scale=-1.0))
            step(a_(pre[:, :, 4:6, :], ss_bank(ps), ACT.Ln, bias=b.eps[:, 0:1]))
            act.wait_ge(e_steps, 5)
            step(a_(pre[:, :, 6:8, :], pre[:, :, 4:6, :], ACT.Exp, scale=-0.5))
            step(a_(b.alog[:, :], b.alog[:, :], ACT.Exp))
            act.wait_ge(g_sum, 1)
            step(a_(b.col[:, :, K_CUM, :], ps[:, 0, 0:40].rearrange("p (t h) -> p t h", h=H), ACT.Copy))
            act.wait_ge(e_steps, 8)
            step(a_(b.col[:, :, K_E, :], b.col[:, :, K_CUM, :], ACT.Exp))

            def body(i, chunks):
                nc.scalar.preload_act_table_set("natural_log_exp_and_others")
                for c, p, n in chunks:
                    act.wait_ge(q["g_bank"][p], i + 1)
                    a_(egl[p][:, :], ps[:, p, n - 1:n - 1 + 3 * P + 1:P], ACT.Exp).then_inc(q["eg_ok"][p], 1)
                for c, p, n in chunks:
                    act.wait_ge(q["gl_ok"][p], i + 1)
                    a_(gd[p][0:n, 1, :], gd[p][0:n, 0, :], ACT.Exp).then_inc(q["gle_ok"][p], 1)
                    a_(dt[p][0:n, :, 0:n], at[p][0:n, :, 0:n], ACT.Exp).then_inc(q["dt_ok"][p], 1)
                    act.wait_ge(q["kt_ok"][p], i + 1)
                    for h in range(H):
                        ins = a_(kbe[p][0:n, h, :], ps[0:n, 4, h * P:h * P + P], ACT.Copy,
                                 scale=cs[p][0:n, K_NBRKE, h:h + 1])
                    ins.then_inc(q["kbe_ok"][p], 1)
                    act.wait_ge(q["kds_ok"][p], i + 1)
                    for h in range(H):
                        ins = a_(kd[p][0:n, h, :], ps[0:n, 4, h * P:h * P + P], ACT.Copy,
                                 scale=gd[p][0:n, 2, h:h + 1])
                    ins.then_inc(q["kd_ok"][p], 1)
                    act.wait_ge(q["vt_ok"][p], i + 1)
                    for h in range(H):
                        ins = a_(vb[p][0:n, h, :], ps[0:n, 5, h * P:h * P + P], ACT.Copy,
                                 scale=cs[p][0:n, K_BETA, h:h + 1])
                    ins.then_inc(q["vb_ok"][p], 1)
                n = chunks[0][2]
                for lv in range(1, last_level(n) + 1):
                    for c, p, n in chunks:
                        act.wait_ge(q["mm_ok"][p], levels_before(i, lv) + 1)
                        a_(half(m1[p][lv - 1], lv, n, 0), packed(p, 0, lv, n), ACT.Copy).then_inc(q["mcopy_ok"][p], 1)
                for c, p, n in chunks:
                    act.wait_ge(q["wt_ok"][p], i + 1)
                    a_(at[p][:, :, 0:n], bank4(ps, p, P, n), ACT.Copy).then_inc(q["wtc_ok"][p], 1)
                for c, p, n in chunks:
                    act.wait_ge(q["u_ok"][p], i + 1)
                    a_(u[0:n, :, :], bank4(ps, 5, n, P), ACT.Copy).then_inc(q["uc_ok"][p], 1)
                    act.wait_ge(q["o1_ok"][p], i + 1)
                    for h in range(H):
                        ins = a_(o1[0:n, h, :], ps[0:n, 6, h * P:h * P + P], ACT.Copy, scale=cs[p][0:n, K_E, h:h + 1])
                    ins.then_inc(q["o1c_ok"][p], 1)
                    act.wait_ge(q["o_ok"][p], i + 1)
                    for h in range(H):
                        ins = a_(o1[0:n, h, :], oc[p][0:n, h, :], ACT.Square, scale=cs[p][0:n, K_RQ, h:h + 1],
                                 accum_out=os_[p][0:n, 0, h:h + 1])
                    ins.then_inc(q["osq_ok"][p], 1)
                    act.wait_ge(q["osq_ok"][p], i + 1)
                    a_(os_[p][0:n, 1, :], os_[p][0:n, 0, :], ACT.Ln, scale=1.0 / P, bias=b.eps[0:n, :]
                       ).then_inc(q["oln_ok"][p], 1)
                    act.wait_ge(q["oln_ok"][p], i + 1)
                    a_(os_[p][0:n, 2, :], os_[p][0:n, 1, :], ACT.Exp, scale=-0.5).then_inc(q["ors_ok"][p], 1)
            groups(act, body)

        @block.vector
        def _(dve):
            done = 0

            def step(ins, wait=True):
                nonlocal done
                done += 1
                ins.then_inc(v_steps, 1)
                if wait:
                    dve.wait_ge(v_steps, done)

            V = nc.vector
            tt_, stt = V.tensor_tensor, V.scalar_tensor_tensor
            kinds = b.col
            step(tt_(pre[:, :, 0, :], ab_bank(ps, 0), bc1(b.dtb[:, :], 10), ALU.add))
            step(V.memset(b.state[:, :, :], 0.0))
            for lv in range(LEVELS):
                V.memset(bt[1][lv][:, :, :], 0.0)
            for lv in range(1, LEVELS):
                V.memset(m1[1][lv - 1][:, :, :], 0.0)
            dve.wait_ge(e_steps, 7)
            step(stt(pre[:, :, 2, :], pre[:, :, 0, :], 0.0, pre[:, :, 1, :], ALU.max, ALU.add))
            step(stt(kinds[:, :, K_G, :], pre[:, :, 2, :], -1.0, bc1(b.alog[:, :], 10), ALU.mult, ALU.mult))
            step(V.memset(ps[:, 0, 0:40], 0.0))
            step(V.tensor_scalar(pre[:, :, 1, :], pre[:, :, 3, :], 1.0, None, ALU.add))
            step(V.reciprocal(kinds[:, :, K_BETA, :], pre[:, :, 1, :]))
            step(V.tensor_scalar(kinds[:, :, K_RQ, :], pre[:, :, 6, :], float(P) ** -0.5, None, ALU.mult))
            step(V.tensor_copy(kinds[:, :, K_RK, :], pre[:, :, 7, :]))
            step(V.tensor_scalar(kinds[:, :, K_NRK, :], pre[:, :, 7, :], -1.0, None, ALU.mult))
            step(tt_(kinds[:, :, K_BRK, :], kinds[:, :, K_BETA, :], pre[:, :, 7, :], ALU.mult))
            step(V.tensor_scalar(b.onw[:, :], b.onw[:, :], 0.5, None, ALU.mult))
            dve.wait_ge(e_steps, 9)
            stt(kinds[:, :, K_NBRKE, :], kinds[:, :, K_BRK, :], -1.0, kinds[:, :, K_E, :], ALU.mult,
                ALU.mult).then_inc(cols_ready, 1)

            def body(i, chunks):
                for c, p, n in chunks:
                    dve.wait_ge(q["eg_ok"][p], i + 1)
                    for h in range(H):
                        stt(at[p][0:n, h, 0:n], ps[0:n, p, h * P:h * P + n], cs[p][0:n, K_CUM, h:h + 1],
                            b.negmask[0:n, 0:n], ALU.subtract, ALU.min)
                    tt_(gd[p][0:n, 0, :], ps[0:n, p, n - 1:n - 1 + 3 * P + 1:P], cs[p][0:n, K_CUM, :],
                        ALU.subtract).then_inc(q["gl_ok"][p], 1)
                for c, p, n in chunks:
                    dve.wait_ge(q["gle_ok"][p], i + 1)
                    tt_(gd[p][0:n, 2, :], gd[p][0:n, 1, :], cs[p][0:n, K_RK, :], ALU.mult).then_inc(q["kds_ok"][p], 1)
                    dve.wait_ge(q["dt_ok"][p], i + 1)
                    dve.wait_ge(q["kk_ok"][p], i + 1)
                    for h in range(H):
                        ins = stt(at[p][0:n, h, 0:n], ps[0:n, 2 + p, h * P:h * P + n], cs[p][0:n, K_NRK, h:h + 1],
                                  dt[p][0:n, h, 0:n], ALU.mult, ALU.mult)
                    ins.then_inc(q["at0_ok"][p], 1)
                    dve.wait_ge(q["qk_ok"][p], i + 1)
                    for h in range(H):
                        ins = stt(qa[p][0:n, h, 0:n], ps[0:n, 6, h * P:h * P + n], cs[p][0:n, K_RK, h:h + 1],
                                  dt[p][0:n, h, 0:n], ALU.mult, ALU.mult)
                    ins.then_inc(q["qa_ok"][p], 1)
                    dve.wait_ge(q["at0_ok"][p], i + 1)
                    dve.wait_ge(q["rb_ok"][p], i + 1)
                    tt_(at[p][0:n, :, 0:n], at[p][0:n, :, 0:n], bank4(ps, p, n, n), ALU.mult
                        ).then_inc(q["at_ok"][p], 1)
                for c, p, n in chunks:
                    dve.wait_ge(q["t1_ok"][p], i + 1)
                    eye = bc1(b.ident[0:n, 0:n], H)
                    tt_(tt[p][0:n, :, 0:n], bt[p][0][0:n, :, 0:n], eye, ALU.add)
                    tt_(tm[p][0:n, :, 0:n], bank4(ps, 2 + p, n, n), eye, ALU.add).then_inc(q["t_ok"][p], 1)
                n = chunks[0][2]
                for lv in range(1, last_level(n) + 1):
                    for c, p, n in chunks:
                        dve.wait_ge(q["dd_ok"][p], levels_before(i, lv) + 1)
                        x = half(tt[p], lv, n, 1)
                        ins = tt_(x, x, packed(2 + p, 256, lv, n), ALU.add)
                        if lv < last_level(n):
                            x = half(tm[p], lv, n, 0)
                            ins = tt_(x, x, packed(2 + p, 0, lv, n), ALU.add)
                        ins.then_inc(q["tnew_ok"][p], 1)
                def state(c, p, n):
                    dve.wait_ge(q["ku_ok"][p], i + 1)
                    for h in range(H):
                        ins = stt(b.state[:, h, :], b.state[:, h, :], egl[p][:, h:h + 1], ps[:, 4, h * P:h * P + P],
                                  ALU.mult, ALU.add)
                    ins.then_inc(q["s_ok"][p], 1)
                    dve.wait_ge(q["o2_ok"][p], i + 1)
                    dve.wait_ge(q["o1c_ok"][p], i + 1)
                    tt_(oc[p][0:n, :, :], bank4(ps, 7, n, P), o1[0:n, :, :], ALU.add).then_inc(q["o_ok"][p], 1)

                def norm(c, p, n):
                    dve.wait_ge(q["ors_ok"][p], i + 1)
                    tt_(os_[p][0:n, 3, :], os_[p][0:n, 2, :], cs[p][0:n, K_RQ, :], ALU.mult
                        ).then_inc(q["ofac_ok"][p], 1)
                    dve.wait_ge(q["ofac_ok"][p], i + 1)
                    tt_(oc[p][0:n, :, :], oc[p][0:n, :, :], bc(os_[p][0:n, 3, :], P), ALU.mult
                        ).then_inc(q["on_ok"][p], 1)

                def gated(c, p, n):
                    dve.wait_ge(q["ot_ok"][p], i + 1)
                    out = b.yt[:, CA:, bass.ds(c * P, n)]
                    stt(out, bank4(ps, 2 + p, P, n), b.onw[:, 0:1], out, ALU.mult, ALU.mult).then_inc(q["y_ok"][p], 1)

                state(*chunks[0])
                norm(*chunks[0])
                if len(chunks) == 2:
                    state(*chunks[1])
                    gated(*chunks[0])
                    norm(*chunks[1])
                gated(*chunks[-1])
            groups(dve, body)

        @block.tensor
        def _(pe):
            mm, tp = nc.tensor.matmul, nc.tensor.transpose
            pe.wait_ge(v_steps, 5)
            g = b.col
            mm(ps[:, 0, 0:32], b.upto[:, :], g[:, 0:8, K_G, :], start=True, stop=True)
            mm(ps[0:TAIL, 0, 32:36], b.upto[0:TAIL, 0:TAIL], g[0:TAIL, 8, K_G, :], start=True, stop=True)
            mm(ps[0:SAMPLES, 0, 36:40], b.ident[0:SAMPLES, 0:SAMPLES], g[0:SAMPLES, 9, K_G, :], start=True,
               stop=True).then_inc(g_sum, 1)

            def output(i, p, n):
                pe.wait_ge(q["on_ok"][p], i + 1)
                for h in range(H):
                    ins = tp(ps[:, 2 + p, h * P:h * P + n], oc[p][0:n, h, :], b.ident[0:n, 0:n])
                ins.then_inc(q["ot_ok"][p], 1)

            def body(i, chunks):
                for c, p, n in chunks:
                    if later(i):
                        if p == 1 or len(chunks) == 1:
                            output(i - 1, 1, P)
                        pe.wait_ge(q["y_ok"][p], i)
                    pe.wait_ge(q["staged"][p], i + 1)
                    for h in range(H):
                        ins = mm(ps[:, p, h * P:h * P + n], cs[p][0:n, K_G, h:h + 1].to_broadcast([n, P]),
                                 b.upto[0:n, 0:n], start=True, stop=True)
                    ins.then_inc(q["g_bank"][p], 1)
                    for h in range(H):
                        kt = ck[p][:, H + h, 0:n]
                        ins = mm(ps[0:n, 2 + p, h * P:h * P + n], kt, kt, start=True, stop=True)
                    ins.then_inc(q["kk_ok"][p], 1)
                for c, p, n in chunks:
                    if p == 1:
                        pe.wait_ge(q["kd_ok"][0], i + 1)
                        pe.wait_ge(q["vb_ok"][0], i + 1)
                        pe.wait_ge(q["qa_ok"][0], i + 1)
                    for h in range(H):
                        ins = tp(ps[0:n, 4, h * P:h * P + P], ck[p][:, H + h, 0:n], b.ident[:, :])
                    ins.then_inc(q["kt_ok"][p], 1)
                    for h in range(H):
                        ins = tp(ps[0:n, 5, h * P:h * P + P], ck[p][:, 2 * H + h, 0:n], b.ident[:, :])
                    ins.then_inc(q["vt_ok"][p], 1)
                    for h in range(H):
                        ins = mm(ps[0:n, 6, h * P:h * P + n], ck[p][:, H + h, 0:n], ck[p][:, h, 0:n],
                                 start=True, stop=True)
                    ins.then_inc(q["qk_ok"][p], 1)
                    pe.wait_ge(q["gl_ok"][p], i + 1)
                    for h in range(H):
                        ins = mm(ps[0:n, p, h * P:h * P + n], cs[p][0:n, K_BRK, h:h + 1].to_broadcast([n, n]),
                                 b.ident[0:n, 0:n], start=True, stop=True)
                    ins.then_inc(q["rb_ok"][p], 1)
                for c, p, n in chunks:
                    pe.wait_ge(q["bt_ok"][p], 7 * i + 1)
                    pe.wait_ge(q["at0_ok"][p], i + 1)
                    for h in range(H):
                        ins = tp(ps[0:n, 2 + p, h * P:h * P + n], bt[p][0][0:n, h, 0:n], b.ident[0:n, 0:n])
                    ins.then_inc(q["t1_ok"][p], 1)
                n = chunks[0][2]
                top = last_level(n)
                for lv in range(1, top + 1):
                    for c, p, n in chunks:
                        if lv == 1:
                            pe.wait_ge(q["t_ok"][p], i + 1)
                            pe.wait_ge(q["at_ok"][p], i + 1)
                        else:
                            pe.wait_ge(q["tnew_ok"][p], levels_before(i, lv))
                        pe.wait_ge(q["bt_ok"][p], 7 * i + lv + 1)
                        for h in range(H):
                            ins = mm(ps[0:n, p, h * 64:h * 64 + n // 2], bt[p][lv][0:n, h, 0:n],
                                     half(tm[p], lv, n, 0)[:, h], start=True, stop=True)
                        ins.then_inc(q["mm_ok"][p], 1)
                    for c, p, n in chunks:
                        pe.wait_ge(q["mcopy_ok"][p], levels_before(i, lv) + 1)
                        for h in range(H):
                            if lv < top:
                                mm(ps[0:n, 2 + p, h * 64:h * 64 + n // 2], tt[p][0:n, h, 0:n],
                                   half(m1[p][lv - 1], lv, n, 0)[:, h], start=True, stop=True)
                            ins = mm(ps[0:n, 2 + p, 256 + h * 64:256 + h * 64 + n // 2], m1[p][lv - 1][0:n, h, 0:n],
                                     half(tt[p], lv, n, 1)[:, h], start=True, stop=True)
                        ins.then_inc(q["dd_ok"][p], 1)
                for c, p, n in chunks:
                    pe.wait_ge(q["tnew_ok"][p], levels_before(i, top) + 1)
                    pe.wait_ge(q["kbe_ok"][p], i + 1)
                    for h in range(H):
                        ins = mm(ps[:, p, h * P:h * P + n], kbe[p][0:n, h, :], tt[p][0:n, h, 0:n],
                                 start=True, stop=True)
                    ins.then_inc(q["wt_ok"][p], 1)
                for c, p, n in chunks:
                    before = (1 - p, i if p == 0 else i + 1)
                    pe.wait_ge(q["wtc_ok"][p], i + 1)
                    pe.wait_ge(q["vb_ok"][chunks[-1][1]], i + 1)
                    if later(before[1]):
                        pe.wait_ge(q["s_ok"][before[0]], before[1])
                        pe.wait_ge(q["uc_ok"][before[0]], before[1])
                    for h in range(H):
                        mm(ps[0:n, 5, h * P:h * P + P], tt[p][0:n, h, 0:n], vb[p][0:n, h, :], start=True, stop=False)
                        ins = mm(ps[0:n, 5, h * P:h * P + P], at[p][:, h, 0:n], b.state[:, h, :],
                                 start=False, stop=True)
                    ins.then_inc(q["u_ok"][p], 1)
                    pe.wait_ge(q["qa_ok"][chunks[-1][1]], i + 1)
                    if later(before[1]):
                        pe.wait_ge(q["o1c_ok"][before[0]], before[1])
                    for h in range(H):
                        ins = mm(ps[0:n, 6, h * P:h * P + P], ck[p][:, h, 0:n], b.state[:, h, :],
                                 start=True, stop=True)
                    ins.then_inc(q["o1_ok"][p], 1)
                    pe.wait_ge(q["uc_ok"][p], i + 1)
                    pe.wait_ge(q["kd_ok"][chunks[-1][1]], i + 1)
                    for h in range(H):
                        ins = mm(ps[:, 4, h * P:h * P + P], kd[p][0:n, h, :], u[0:n, h, :], start=True, stop=True)
                    ins.then_inc(q["ku_ok"][p], 1)
                    if later(before[1]):
                        pe.wait_ge(q["o_ok"][before[0]], before[1])
                    for h in range(H):
                        ins = mm(ps[0:n, 7, h * P:h * P + P], qa[p][0:n, h, 0:n], u[0:n, h, :], start=True, stop=True)
                    ins.then_inc(q["o2_ok"][p], 1)
                if len(chunks) == 2:
                    output(i, 0, P)
                else:
                    output(i, 0, TAIL)
            groups(pe, body)


def ab_bank(ps, first):
    return ps[:, 6, 0:80].rearrange("p (t k) -> p t k", k=8)[:, :, first:first + H]


def ss_bank(ps):
    return ps[:, 7, 0:80].rearrange("p (t a h) -> p t a h", a=2, h=H)


def sample_stage(nc, m, s, b, io):
    ps = b.psum
    b.wo = m.place("wo", [P, KD, D], at=b.R1)
    m.at = b.R1 + 49152
    SH = SAMPLES * H
    s_in = m.place("s_in", [P, SH, P])
    s_new = m.place("s_new", [P, SH, P])
    spread = m.place("spread", [SAMPLES, 4, SAMPLES, H])
    vals = m.place("vals", [P, 4, SAMPLES, H])
    kh = m.place("kh", [P, SAMPLES, H])
    qh = m.place("qh", [P, SAMPLES, H])
    kq = m.place("kq", [P, SH, 2])
    qk = m.place("qk", [P, SAMPLES, H])
    vu = m.place("vu", [P, SAMPLES, H])
    uu = m.place("uu", [P, SAMPLES, H])
    oo = m.place("oo", [P, SAMPLES, H])
    osq = m.place("osq_s", [P, SAMPLES, H])
    rs = m.place("rs", [P, 2, SAMPLES, H])
    outer = [m.place(f"outer{p}", [P, H, P]) for p in range(2)]
    b.wo_in = s("wo_in")
    v, a, in_, out = s("s_vec"), s("s_act"), s("s_state_in"), s("s_state_out")
    pe1, pe2, pe3, pe4, scaled, added, mult = (s("s_vals"), s("s_products"), s("s_norms"), s("s_rows"), s("s_scaled"),
                                               s("s_added"), s("s_outer"))

    def flat(ap):
        return ap.rearrange("p b h -> p (b h)")

    def mine(first):
        return every3(b.qkv[:, first:first + H, :]).rearrange("p h b -> p b h")

    with nc.Block() as block:
        @block.sync
        def _(sp):
            sp.dma_start(s_in[:, :, :], io.ssm.rearrange("b h k v -> k (b h) v")).then_inc(in_, 16)
            sp.dma_start(b.wo[:, :, :], io.w_out).then_inc(b.wo_in, 16)
            sp.wait_ge(added, SAMPLES)
            sp.dma_start(io.new_ssm_sample.rearrange("b h k v -> k (b h) v"), s_new[:, :, :]).then_inc(out, 16)
            sp.wait_ge(out, 16)

        @block.gpsimd
        def _(pool):
            pool.wait_ge(in_, 16)
            pool.wait_ge(v, 3)
            for k in range(SAMPLES):
                nc.gpsimd.tensor_tensor(s_new[:, H * k:H * k + H, :], s_in[:, H * k:H * k + H, :],
                                        bc(vals[:, 1, k, :], P), ALU.mult).then_inc(scaled, 1)

        @block.scalar
        def _(act):
            nc.scalar.preload_act_table_set("natural_log_exp_and_others")
            act.wait_ge(pe3, 1)
            nc.scalar.activation(rs[:, 0, :, :].rearrange("p b h -> p (b h)"), ps[:, 2, 0:SH], ACT.Ln, scale=1.0 / P,
                                 bias=b.eps[:, :]).then_inc(a, 1)
            act.wait_ge(a, 1)
            nc.scalar.activation(rs[:, 1, :, :], rs[:, 0, :, :], ACT.Exp, scale=-0.5).then_inc(a, 1)

        @block.vector
        def _(dve):
            n = 0

            def step(ins):
                nonlocal n
                n += 1
                ins.then_inc(v, 1)
                dve.wait_ge(v, n)

            tt = nc.vector.tensor_tensor
            eye = b.ident[0:SAMPLES, 0:SAMPLES]
            step(tt(spread[:, 0, :, :], bc1(b.col[0:SAMPLES, 9, K_BETA, :], SAMPLES), bc(eye, H), ALU.mult))
            shape = [SAMPLES, 3, SAMPLES, H]
            step(tt(spread[:, 1:4, :, :], b.col[0:SAMPLES, 9, K_E:K_RK + 1, :].unsqueeze(2).broadcast_to(shape),
                    bc1(bc(eye, H), 3), ALU.mult))
            dve.wait_ge(pe1, 1)
            step(nc.vector.tensor_copy(vals[:, :, :, :].rearrange("p k b h -> p (k b h)"), ps[:, 0, 0:4 * SH]))
            step(tt(kh[:, :, :], mine(H), vals[:, 3, :, :], ALU.mult))
            step(tt(qh[:, :, :], mine(0), vals[:, 2, :, :], ALU.mult))
            step(tt(qk[:, :, :], kh[:, :, :], qh[:, :, :], ALU.mult))
            step(tt(vu[:, :, :], kh[:, :, :], vals[:, 1, :, :], ALU.mult))
            step(tt(kq[:, :, 0], flat(vu[:, :, :]), flat(vals[:, 0, :, :]), ALU.mult))
            step(tt(kq[:, :, 1], flat(qh[:, :, :]), flat(vals[:, 1, :, :]), ALU.mult))
            step(tt(vu[:, :, :], mine(2 * H), vals[:, 0, :, :], ALU.mult))
            dve.wait_ge(pe2, 1)
            got = ps[:, 1, 0:2 * SH].rearrange("p (n k) -> p n k", k=2)
            step(tt(flat(uu[:, :, :]), flat(vu[:, :, :]), got[:, :, 0], ALU.subtract))
            step(tt(flat(oo[:, :, :]), flat(uu[:, :, :]), ps[:, 3, 0:SH], ALU.mult))
            step(tt(flat(oo[:, :, :]), flat(oo[:, :, :]), got[:, :, 1], ALU.add))
            step(tt(osq[:, :, :], oo[:, :, :], oo[:, :, :], ALU.mult))
            dve.wait_ge(a, 2)
            step(tt(oo[:, :, :], oo[:, :, :], rs[:, 1, :, :], ALU.mult))
            y = b.yt[:, CA:, PROMPT:TOK].rearrange("p h b -> p b h")
            step(nc.vector.scalar_tensor_tensor(y, oo[:, :, :], b.onw[:, 0:1], y, ALU.mult, ALU.mult))
            for k in range(SAMPLES):
                dve.wait_ge(pe4, k + 1)
                tt(outer[k % 2][:, :, :], bank4(ps, 4 + k % 4, P, P), bc(kh[:, k, :], P), ALU.mult).then_inc(mult, 1)
                dve.wait_ge(mult, k + 1)
                dve.wait_ge(scaled, k + 1)
                rows = s_new[:, H * k:H * k + H, :]
                tt(rows, rows, outer[k % 2][:, :, :], ALU.add).then_inc(added, 1)

        @block.tensor
        def _(pe):
            mm = nc.tensor.matmul
            pe.wait_ge(v, 2)
            mm(ps[:, 0, 0:4 * SH], b.ones[0:SAMPLES, :], spread[:, :, :, :].rearrange("p k b h -> p (k b h)"),
               start=True, stop=True).then_inc(pe1, 1)
            pe.wait_ge(in_, 16)
            pe.wait_ge(v, 9)
            for n in range(SH):
                mm(ps[:, 1, 2 * n:2 * n + 2], s_in[:, n, :], kq[:, n, :], start=True, stop=True)
            mm(ps[:, 3, 0:SH], b.ones[:, :], flat(qk[:, :, :]), start=True, stop=True).then_inc(pe2, 1)
            pe.wait_ge(v, 14)
            mm(ps[:, 2, 0:SH], b.ones[:, :], flat(osq[:, :, :]), start=True, stop=True).then_inc(pe3, 1)
            for k in range(SAMPLES):
                if k >= 4:
                    pe.wait_ge(mult, k - 3)
                for h in range(H):
                    ins = mm(ps[:, 4 + k % 4, h * P:h * P + P], uu[:, k, h:h + 1].to_broadcast([P, P]),
                             b.ident[:, :], start=True, stop=True)
                ins.then_inc(pe4, 1)


def every3(ap):
    return ap[:, :, QS:QS + KQ * (SAMPLES - 1) + 1:KQ]


def route_stage(nc, m, s, b, io):
    ps = b.psum
    wo = b.wo
    half = KD // 2
    wo_hi = [m.place("wo_hi0", [P, half, D], F32R, at=b.R1 + 32768),
             m.place("wo_hi1", [P, half, D], F32R, at=b.R2 + 4 * KD * TP)]
    yt_hi = m.place("yt_hi", [P, KD, TP], F32R, at=b.R2)
    wo_lo = m.place("wo_lo", [P, KD, D], F32R, at=b.R1)
    yt_lo = m.place("yt_lo", [P, KD, TP], F32R, at=b.R3)
    assert 4 * KD * TP + 4 * half * D <= b.R3 - b.R2

    def w_hi(kk):
        return wo_hi[kk // half][:, kk % half, :]

    b.x1 = m.place("x1", [P, TILES, D], at=b.R1 + 49152)
    b.R5 = m.next
    m.at = b.R5
    xt = [m.place(f"xt{k}", [P, D]) for k in range(2)]
    h2 = [m.place(f"h2{k}", [P, D]) for k in range(2)]
    wf = m.place("wf", [P, D])
    h2t = m.place("h2t", [P, KD, P])
    assert m.at <= b.R2
    lg = m.place("lg", [P, TILES, GRP + NE], at=b.R3 + 4 * KD * TP)
    m.at = b.R5
    T = TILES
    r = {}
    for name, shape in (
            ("mg", [T]), ("sc", [T, 4]), ("eg", [T, 4]), ("eq", [T, 4]), ("ms", [T]), ("og", [T, 4]), ("sg", [T]),
            ("pg", [T]), ("lx", [T, 4, 8]), ("les", [T, 8]), ("m1", [T]), ("eq1", [T, 8]), ("oh1", [T, 8]),
            ("le2", [T, 8]), ("m2", [T]), ("oh2", [T, 8]), ("d", [T]), ("ed", [T]), ("den", [T]),
            ("o1", [T, 4, 8]), ("o2", [T, 4, 8]), ("os", [T, 4, 8]), ("cr", [T + 1, NE]), ("pos", [T, NE]),
            ("tmp", [T, NE]), ("rank", [2, T]), ("thr", [PARTS - 1]), ("cmp", [NE, PARTS - 1]), ("nov", [NE]),
            ("incl", [NE]), ("zero", [NE]), ("first", [NE]), ("base", [2, T]), ("eid", [2, T]), ("isov", [2, T]),
            ("part", [2, T]), ("part_cmp", [2, T, PARTS - 1]), ("cpos", [2, T]), ("bad", [T]),
            ("le_", [OV, NE]), ("ovf", [OV + 1]), ("ib", [NB]), ("ic", [C]), ("iw", [8]), ("ie", [NE]),
            ("vals", [3, 2, T]), ("in_slot", [2 * T, C])):
        r[name] = m.place("r_" + name, [P] + shape)
    assert m.at <= b.R2, m.at - b.R2
    b.xg = [m.place(f"xg{k}", [C, D], at=b.R3 + 4096 * k) for k in range(4)]
    m.at = b.R3 + 4 * 4096
    spread = m.place("r_spread", [P, 2 * T, 3, NB])
    rows_f = m.place("r_rows_f", [C, 2, NB])
    r["in_block"] = m.place("r_in_block", [P, 2 * T, NB])
    assert m.at <= b.R3 + 4 * KD * TP
    w_in, x_in, x1_ok, sq, ln, rs, h2_ok = (s("wf_in"), s.pair("x2_in"), s("x1_ok"), s("h2_sq"), s("h2_ln"),
                                            s("h2_rs"), s("h2_ok"))
    prod, turned, turned_c, logits, lg_ok, h2_out = (s("out_prod"), s("h2_turned"), s("h2_copied"), s("logits"),
                                                     s("lg_ok"), s.pair("h2_out"))
    y_hi_ok, y_lo_ok, w_hi_ok, w_lo_ok = s("y_hi_ok"), s("y_lo_ok"), s("wo_hi_ok"), s("wo_lo_ok")
    spread_1 = s("r_spread_1")
    iota, vr, ar, counted, tabled = s("r_iota"), s("r_vec"), s("r_act"), s("r_counts"), s("r_tabled")
    b.w_landed = [s(f"expert_w{k}") for k in range(4)]
    b.slots = expert_slots(m, b)

    def rows(t):
        return P if t < 8 else LAST

    with nc.Block() as block:
        @block.sync
        def _(sp):
            sp.dma_start(wf[:, :], io.norm_ffn.partition_broadcast(P)).then_inc(w_in, 16)
            for t in range(TILES):
                n = rows(t)
                if t >= 2:
                    sp.wait_ge(x1_ok, t - 1)
                sp.dma_start(xt[t % 2][0:n, :], io.x[t * P:t * P + n, :]).then_inc(x_in[t % 2], 16)
                if t >= 1:
                    k = rows(t - 1)
                    sp.wait_ge(h2_ok, t)
                    sp.dma_start(b.h2_dram[(t - 1) * P:(t - 1) * P + k, :], h2[(t - 1) % 2][0:k, :]
                                 ).then_inc(h2_out[(t - 1) % 2], 16)
            sp.wait_ge(h2_ok, TILES)
            sp.dma_start(b.h2_dram[8 * P:TOK, :], h2[0][0:LAST, :]).then_inc(h2_out[0], 16)
            sp.wait_ge(h2_out[0], 16 * 5)
            sp.wait_ge(h2_out[1], 16 * 4)
            sp.wait_ge(prod, TILES)
            for e in range(4):
                load_expert(sp, b, io, e, e)

        @block.gpsimd
        def _(pool):
            pool.wait_ge(lg_ok, TILES)
            pool.wait_ge(h2_out[0], 16 * 5)
            pool.wait_ge(h2_out[1], 16 * 4)
            it = nc.gpsimd.iota
            kw = dict(allow_small_or_imprecise_dtypes=True)
            it(r["iw"][:, :], pattern=[[-1, 8]], base=8, channel_multiplier=0, **kw)
            it(r["ie"][:, :], pattern=[[1, NE]], base=0, channel_multiplier=0, **kw)
            it(r["ib"][:, :], pattern=[[1, NB]], base=0, channel_multiplier=0, **kw)
            it(r["ic"][:, :], pattern=[[1, C]], base=0, channel_multiplier=0, **kw)
            it(r["thr"][:, :], pattern=[[C, PARTS - 1]], base=C, channel_multiplier=0, **kw)
            for k in range(2):
                it(r["vals"][:, 0, k, :], pattern=[[-P, TILES]], base=NOWHERE, channel_multiplier=-1, **kw)
                it(r["vals"][:, 1, k, :], pattern=[[-P, TILES]], base=NOWHERE - k * TOK, channel_multiplier=-1, **kw)
            nc.gpsimd.memset(r["zero"][:, :], 0.0).then_inc(iota, 1)
            pool.wait_ge(prod, TILES)
            for k in range(4):
                nc.gpsimd.memset(b.xg[k][:, :], 0.0)
            pool.wait_ge(vr, BLOCK_STEP)
            pool.wait_ge(iota, 1)
            nc.gpsimd.tensor_tensor(spread[:, :, 1, :], r["in_block"][:, :, :],
                                    bc(r["vals"][:, 1, :, :].rearrange("p k t -> p (k t)"), NB), ALU.mult
                                    ).then_inc(spread_1, 1)

        @block.scalar
        def _(act):
            a_ = nc.scalar.activation
            nc.scalar.preload_act_table_set("natural_log_exp_and_others")

            def copy_turned(t):
                n = rows(t)
                for g in range(2):
                    act.wait_ge(turned, 2 * t + g + 1)
                    if t >= 1:
                        act.wait_ge(logits, t)
                    a_(h2t[:, 4 * g:4 * g + 4, 0:n], bank4(ps, 4 + g, P, n), ACT.Copy).then_inc(turned_c, 1)

            def y_high(t):
                cols = slice(t * P, t * P + rows(t))
                a_(yt_hi[:, :, cols], b.yt[:, :, cols], ACT.Copy).then_inc(y_hi_ok, 1)

            act.wait_ge(b.wo_in, 16)
            y_high(0)
            for kk in range(KD):
                a_(w_hi(kk), wo[:, kk, :], ACT.Copy).then_inc(w_hi_ok, 1)
            y_high(1)
            for t in range(TILES):
                n = rows(t)
                if t + 2 < TILES:
                    y_high(t + 2)
                act.wait_ge(x1_ok, t + 1)
                if t >= 2:
                    act.wait_ge(turned, 2 * t - 2)
                    act.wait_ge(h2_out[t % 2], 16 * (t // 2))
                a_(h2[t % 2][0:n, :], b.x1[0:n, t, :], ACT.Square, accum_out=b.stat[0:n, t, 0:1]).then_inc(sq, 1)
                act.wait_ge(sq, t + 1)
                a_(b.stat[0:n, t, 1:2], b.stat[0:n, t, 0:1], ACT.Ln, scale=1.0 / D, bias=b.eps[0:n, :]
                   ).then_inc(ln, 1)
                act.wait_ge(ln, t + 1)
                a_(b.stat[0:n, t, 2:3], b.stat[0:n, t, 1:2], ACT.Exp, scale=-0.5).then_inc(rs, 1)
                copy_turned(t)
            act.wait_ge(vr, 7)
            a_(r["eg"][:, :, :], r["eq"][:, :, :], ACT.Exp).then_inc(ar, 1)
            act.wait_ge(vr, 18)
            a_(r["ed"][:, :], r["d"][:, :], ACT.Exp).then_inc(ar, 1)

        @block.vector
        def _(dve):
            V = nc.vector
            V.memset(lg[:, :, :], 0.0).then_inc(s("lg_zero"), 1)
            dve.wait_ge(w_in, 16)
            dve.wait_ge(s("lg_zero"), 1)

            def tail(t):
                dve.wait_ge(logits, t + 1)
                n = rows(t)
                V.tensor_tensor(lg[0:n, t, :], ps[0:n, 6, 0:GRP + NE], b.rb[0:n, :], ALU.add).then_inc(lg_ok, 1)

            def y_low(t):
                cols = slice(t * P, t * P + rows(t))
                dve.wait_ge(y_hi_ok, t + 1)
                V.tensor_tensor(yt_lo[:, :, cols], b.yt[:, :, cols], yt_hi[:, :, cols].bitcast(F32),
                                ALU.subtract).then_inc(y_lo_ok, 1)

            y_low(0)
            for kk in range(KD):
                dve.wait_ge(w_hi_ok, kk + 1)
                V.tensor_tensor(wo_lo[:, kk, :], wo[:, kk, :], w_hi(kk).bitcast(F32),
                                ALU.subtract).then_inc(w_lo_ok, 1)
            y_low(1)
            for t in range(TILES):
                n = rows(t)
                if t + 2 < TILES:
                    y_low(t + 2)
                dve.wait_ge(x_in[t % 2], 16 * (t // 2 + 1))
                dve.wait_ge(prod, t + 1)
                V.tensor_tensor(b.x1[0:n, t, :].rearrange("p (c n) -> p c n", c=2),
                                ps[0:n, 2 * (t % 2):2 * (t % 2) + 2, :],
                                xt[t % 2][0:n, :].rearrange("p (c n) -> p c n", c=2), ALU.add).then_inc(x1_ok, 1)
                dve.wait_ge(rs, t + 1)
                V.scalar_tensor_tensor(h2[t % 2][0:n, :], b.x1[0:n, t, :], b.stat[0:n, t, 2:3], wf[0:n, :],
                                       ALU.mult, ALU.mult).then_inc(h2_ok, 1)
                tail(t)
            dve.wait_ge(iota, 1)
            dve.wait_ge(lg_ok, TILES)
            n = 0

            def step(ins):
                nonlocal n
                n += 1
                ins.then_inc(vr, 1)
                dve.wait_ge(vr, n)

            tt, ts, stt, red = V.tensor_tensor, V.tensor_scalar, V.scalar_tensor_tensor, V.tensor_reduce
            l4 = lg[:, :, 0:GRP]
            l32 = lg[:, :, GRP:].rearrange("p t (g e) -> p t g e", g=GRP)

            def top(vals, eq, sel, best, first, k):
                step(red(best, vals, AX.X, ALU.max))
                step(tt(eq, vals, bc(best, k), ALU.is_equal))
                step(tt(eq, eq, bc1(r["iw"][:, 8 - k:8], T), ALU.mult))
                step(red(first, eq, AX.X, ALU.max))
                step(tt(sel, eq, bc(first, k), ALU.is_equal))

            top(l4, r["sc"][:, :, :], r["og"][:, :, :], r["mg"][:, :], r["ms"][:, :], GRP)
            step(tt(r["og"][:, :, :], r["og"][:, :, :], bc(b.valid[:, :], GRP), ALU.mult))
            step(tt(r["eq"][:, :, :], l4, bc(r["mg"][:, :], GRP), ALU.subtract))
            step(tt(r["lx"][:, :, :, :], l32, bc(r["og"][:, :, :], EPG), ALU.mult))
            step(red(r["les"][:, :, :], r["lx"][:, :, :, :].rearrange("p t g e -> p t e g"), AX.X, ALU.add))
            top(r["les"][:, :, :], r["eq1"][:, :, :], r["oh1"][:, :, :], r["m1"][:, :], r["ms"][:, :], EPG)
            step(stt(r["le2"][:, :, :], r["oh1"][:, :, :], 2 * NEG, r["les"][:, :, :], ALU.mult, ALU.add))
            step(red(r["m2"][:, :], r["le2"][:, :, :], AX.X, ALU.max))
            dve.wait_ge(ar, 1)
            step(red(r["sg"][:, :], r["eg"][:, :, :], AX.X, ALU.add))
            step(tt(r["d"][:, :], r["m2"][:, :], r["m1"][:, :], ALU.subtract))
            step(tt(r["eq1"][:, :, :], r["le2"][:, :, :], bc(r["m2"][:, :], EPG), ALU.is_equal))
            step(tt(r["eq1"][:, :, :], r["eq1"][:, :, :], bc1(r["iw"][:, :], T), ALU.mult))
            step(red(r["ms"][:, :], r["eq1"][:, :, :], AX.X, ALU.max))
            step(tt(r["oh2"][:, :, :], r["eq1"][:, :, :], bc(r["ms"][:, :], EPG), ALU.is_equal))
            step(V.reciprocal(r["pg"][:, :], r["sg"][:, :]))
            dve.wait_ge(ar, 2)
            step(ts(r["den"][:, :], r["ed"][:, :], 1.0, None, ALU.add))
            step(V.reciprocal(r["den"][:, :], r["den"][:, :]))
            step(tt(r["vals"][:, 2, 0, :], r["pg"][:, :], r["den"][:, :], ALU.mult))
            step(tt(r["vals"][:, 2, 1, :], r["vals"][:, 2, 0, :], r["ed"][:, :], ALU.mult))
            shape = [P, T, GRP, EPG]
            for o, oh in ((r["o1"], r["oh1"]), (r["o2"], r["oh2"])):
                step(tt(o[:, :, :, :], bc(r["og"][:, :, :], EPG), oh[:, :, :].unsqueeze(2).broadcast_to(shape), ALU.mult))
            step(tt(r["os"][:, :, :, :], r["o1"][:, :, :, :], r["o2"][:, :, :, :], ALU.add))
            step(V.memset(r["cr"][:, 0, :], 0.0))
            dve.wait_ge(counted, 1)
            for t in range(T):
                step(tt(r["cr"][:, t + 1, :], r["cr"][:, t, :], ps[:, 1, NE * t:NE * t + NE], ALU.add))
            step(tt(r["pos"][:, :, :], r["cr"][:, 0:T, :], ps[:, 0, 0:NE * T].rearrange("p (t e) -> p t e", e=NE), ALU.add))
            total = r["cr"][:, T, :]
            step(tt(r["cmp"][:, :, :], bc(total, PARTS - 1), bc1(r["thr"][:, :], NE), ALU.is_gt))
            step(red(r["nov"][:, :], r["cmp"][:, :, :], AX.X, ALU.add))
            step(V.tensor_tensor_scan(r["incl"][:, :], r["nov"][:, :], r["zero"][:, :], 0.0, ALU.add, ALU.add))
            step(tt(r["first"][:, :], r["incl"][:, :], r["nov"][:, :], ALU.subtract))

            def chosen(vals, dst):
                for k, o in enumerate((r["o1"], r["o2"])):
                    step(tt(r["tmp"][:, :, :], o[:, :, :, :].rearrange("p t g e -> p t (g e)"), vals, ALU.mult))
                    step(red(dst[:, k, :], r["tmp"][:, :, :], AX.X, ALU.add))

            chosen(r["pos"][:, :, :], r["rank"])
            step(tt(r["part_cmp"][:, :, :, :], bc(r["rank"][:, :, :], PARTS - 1),
                    r["thr"][:, :].unsqueeze(1).unsqueeze(1).broadcast_to([P, 2, T, PARTS - 1]), ALU.is_ge))
            step(red(r["part"][:, :, :], r["part_cmp"][:, :, :, :], AX.X, ALU.add))
            step(stt(r["cpos"][:, :, :], r["part"][:, :, :], float(-C), r["rank"][:, :, :], ALU.mult, ALU.add))
            step(tt(r["in_slot"][:, :, :], bc(r["cpos"][:, :, :].rearrange("p k t -> p (k t)"), C),
                    bc1(r["ic"][:, :], 2 * T), ALU.is_equal))
            chosen(bc1(r["ie"][:, :], T), r["eid"])
            chosen(bc1(r["first"][:, :], T), r["base"])
            step(stt(r["base"][:, :, :], r["base"][:, :, :], float(NE - 1), r["part"][:, :, :], ALU.add, ALU.add))
            step(tt(r["base"][:, :, :], r["base"][:, :, :], r["eid"][:, :, :], ALU.subtract))
            step(ts(r["isov"][:, :, :], r["rank"][:, :, :], float(C), None, ALU.is_ge))
            step(tt(r["base"][:, :, :], r["base"][:, :, :], r["isov"][:, :, :], ALU.mult))
            step(tt(r["eid"][:, :, :], r["eid"][:, :, :], r["base"][:, :, :], ALU.add))
            step(ts(r["bad"][:, :], b.valid[:, :], -1.0e5, 1.0e5, ALU.mult, ALU.add))
            step(tt(r["eid"][:, :, :], r["eid"][:, :, :], bc1(r["bad"][:, :], 2), ALU.add))
            step(tt(r["in_block"][:, :, :], bc(r["eid"][:, :, :].rearrange("p k t -> p (k t)"), NB),
                    bc1(r["ib"][:, :], 2 * T), ALU.is_equal))
            assert n == BLOCK_STEP, n
            for v in (0, 2):
                step(tt(spread[:, :, v, :], r["in_block"][:, :, :],
                        bc(r["vals"][:, v, :, :].rearrange("p k t -> p (k t)"), NB), ALU.mult))
            assert n == SPREAD_STEP, n
            step(tt(r["le_"][:, :, :], bc1(r["incl"][:, :], OV), bc(r["ib"][:, 0:OV], NE), ALU.is_le))
            step(red(r["ovf"][:, 0:OV], r["le_"][:, :, :], AX.X, ALU.add))
            step(V.tensor_copy(r["ovf"][:, OV:OV + 1], r["incl"][:, NE - 1:NE]))
            step(V.tensor_copy(b.ove[:, :], r["ovf"][:, :]))
            dve.wait_ge(tabled, 1)
            table = ps[0:C, 2, 0:3 * NB].rearrange("p (v b) -> p v b", v=3)
            step(ts(rows_f[:, :, :], table[:, 0:2, :], -1.0, float(NOWHERE), ALU.mult, ALU.add))
            step(V.tensor_copy(b.slot_rows[:, :, :], rows_f[:, :, :]))
            V.tensor_copy(b.slot_w[:, :], table[:, 2, :])

        @block.tensor
        def _(pe):
            mm = nc.tensor.matmul

            def turn_and_route(t):
                n = rows(t)
                pe.wait_ge(h2_ok, t + 1)
                if t >= 1:
                    pe.wait_ge(turned_c, 2 * t)
                for g in range(2):
                    for k in range(4):
                        kk = 4 * g + k
                        ins = nc.tensor.transpose(ps[:, 4 + g, k * P:k * P + n],
                                                  h2[t % 2][0:n, kk * P:kk * P + P], b.ident[0:n, 0:n])
                    ins.then_inc(turned, 1)
                pe.wait_ge(turned_c, 2 * t + 2)
                if t >= 1:
                    pe.wait_ge(lg_ok, t)
                for kk in range(KD):
                    ins = mm(ps[0:n, 6, 0:GRP + NE], h2t[:, kk, 0:n], b.rw[:, kk, :], start=(kk == 0),
                             stop=(kk == KD - 1))
                ins.then_inc(logits, 1)

            for t in range(TILES):
                n = rows(t)
                if t >= 2:
                    pe.wait_ge(x1_ok, t - 1)
                pe.wait_ge(y_lo_ok, t + 1)
                cols = slice(t * P, t * P + n)
                for kk in range(KD):
                    if t == 0:
                        pe.wait_ge(w_lo_ok, kk + 1)
                    lo_w, lo_y = wo_lo[:, kk, :], yt_lo[:, kk, cols]
                    for q, (y, w) in enumerate(((yt_hi[:, kk, cols], w_hi(kk)), (yt_hi[:, kk, cols], lo_w),
                                                (lo_y, w_hi(kk)))):
                        for c in range(2):
                            ins = mm(ps[0:n, 2 * (t % 2) + c, :], y, w[:, c * 512:c * 512 + 512],
                                     start=(kk == 0 and q == 0), stop=(kk == KD - 1 and q == 2))
                ins.then_inc(prod, 1)
                if t >= 1:
                    turn_and_route(t - 1)
            turn_and_route(TILES - 1)
            pe.wait_ge(vr, 30)
            rhs = r["os"][:, :, :, :].rearrange("p t g e -> p (t g e)")
            pe.wait_ge(x1_ok, TILES)
            mm(ps[:, 0, 0:NE * TILES], b.before[:, :], rhs, start=True, stop=True)
            mm(ps[:, 1, 0:NE * TILES], b.ones[:, :], rhs, start=True, stop=True).then_inc(counted, 1)
            pe.wait_ge(vr, SPREAD_STEP)
            pe.wait_ge(spread_1, 1)
            for j in range(2 * T):
                ins = mm(ps[0:C, 2, 0:3 * NB], r["in_slot"][:, j, :],
                         spread[:, j, :, :].rearrange("p v b -> p (v b)"), start=(j == 0), stop=(j == 2 * T - 1))
            ins.then_inc(tabled, 1)


BLOCK_STEP = 69
SPREAD_STEP = 71


def expert_slots(m, b):
    slots = []
    for k, at in enumerate((b.R2, b.R2 + 24576, b.R1, b.R1 + 24576)):
        slots.append((m.place(f"wg{k}", [P, KD, FF], at=at), m.place(f"wu{k}", [P, KD, FF], at=at + 8192),
                      m.place(f"wd{k}", [P, KF, D], at=at + 16384)))
    return slots


def load_expert(eng, b, io, e, k, sem=None):
    wg, wu, wd = b.slots[k]
    sem = b.w_landed[k] if sem is None else sem
    e1 = bass.ds(e, 1)
    eng.dma_start(wg[:, :, :], io.w_gate[e1].rearrange("a (p k) f -> (a p) k f", k=KD)).then_inc(sem, 16)
    eng.dma_start(wu[:, :, :], io.w_up[e1].rearrange("a (p k) f -> (a p) k f", k=KD)).then_inc(sem, 16)
    eng.dma_start(wd[:, :, :], io.w_down[e1].rearrange("a (f p) d -> (a p) f d", p=P)).then_inc(sem, 16)


class StepSems:

    def __init__(self, q):
        self.turned, self.xt_ok, self.gu_ok, self.tanh_ok = q["turned"], q["xt_ok"], q["gu_ok"], q["tanh_ok"]
        self.ge_ok, self.he_ok, self.down_ok = q["ge_ok"], q["he_ok"], q["down_ok"]
        self.outa_ok, self.outb_ok, self.scattered = q["outa_ok"], q["outb_ok"], q["scattered"]


def expert_stage(nc, m, s, b, io):
    ps = b.psum
    xg = b.xg
    m.at = b.R3 + 4 * 4096
    xt = [m.place(f"xgt{k}", [P, KD, C]) for k in range(2)]
    th = [m.place(f"thx{k}", [P, KF, C]) for k in range(2)]
    ge = [m.place(f"ge{k}", [P, KF, C]) for k in range(2)]
    he = [m.place(f"he{k}", [P, KF, C]) for k in range(2)]
    m.at = b.R5
    out = [m.place(f"out{k}", [C, D]) for k in range(2)]
    assert m.at <= b.R2
    names = "turned xt_ok gu_ok tanh_ok ge_ok he_ok down_ok outa_ok outb_ok scattered".split()
    q = {n: s.pair("e_" + n) for n in names}
    gathered = s.pair("e_gathered", 4)
    main = [StepSems({n: q[n][p] for n in names}) for p in range(2)]
    qm = {n: s.pair("v_" + n) for n in names}
    more = [StepSems({n: qm[n][p] for n in names}) for p in range(2)]
    more_w, more_gathered = s.pair("v_w"), s.pair("v_gathered")



    def gather(pool, k, e, done):
        pool.indirect_dma_start(xg[k][:, :], None, b.h2_dram,
                                bass.IndirectOffsetOnAxis(ap=b.slot_rows[:, 0, e:e + 1].bitcast(U32), axis=0),
                                bounds_check=TOK - 1, oob_is_err=False).then_inc(done, 16)

    def scatter(pool, q, p, n, e):
        pool.wait_ge(q.outa_ok, n + 1)
        pool.wait_ge(q.outb_ok, n + 1)
        pool.indirect_dma_start(b.ye, bass.IndirectOffsetOnAxis(ap=b.slot_rows[:, 1, e:e + 1].bitcast(U32), axis=0),
                                out[p][:, :], None, bounds_check=2 * TOK - 1, oob_is_err=False
                                ).then_inc(q.scattered, 16)

    def turn(pe, q, k):
        for g in range(2):
            for j in range(4):
                kk = 4 * g + j
                ins = nc.tensor.transpose(ps[:, 2 + g, j * P:j * P + C], xg[k][:, kk:kk + KD * (P - 1) + 1:KD],
                                          b.ident[0:C, 0:C])
        ins.then_inc(q.turned, 1)

    def copy_turned(act, q, p, n):
        act.wait_ge(q.turned, n + 1)
        if later(n):
            act.wait_ge(q.gu_ok, n)
        for g in range(2):
            nc.scalar.activation(xt[p][:, 4 * g:4 * g + 4, :], bank4(ps, 2 + g, P, C), ACT.Copy
                                 ).then_inc(q.xt_ok, 1)

    def gate_up(pe, q, p, n, k):
        pe.wait_ge(q.xt_ok, 2 * n + 2)
        for g in range(2):
            for f in range(KF):
                o = (g * KF + f) * P
                for kk in range(KD):
                    ins = nc.tensor.matmul(ps[:, p, o:o + C], b.slots[k][g][:, kk, f * P:f * P + P],
                                           xt[p][:, kk, :], start=(kk == 0), stop=(kk == KD - 1))
        ins.then_inc(q.gu_ok, 1)

    def tanh(act, q, p, n):
        act.wait_ge(q.gu_ok, n + 1)
        nc.scalar.activation(th[p][:, :, :], bank4(ps, p, P, C)[:, 0:KF], ACT.Tanh, scale=0.5).then_inc(q.tanh_ok, 1)

    def swiglu(dve, q, p, n):
        dve.wait_ge(q.tanh_ok, n + 1)
        g = bank4(ps, p, P, C)
        nc.vector.scalar_tensor_tensor(ge[p][:, :, :], th[p][:, :, :], 1.0, g[:, 0:KF], ALU.add, ALU.mult
                                       ).then_inc(q.ge_ok, 1)
        dve.wait_ge(q.ge_ok, n + 1)
        nc.vector.scalar_tensor_tensor(he[p][:, :, :], ge[p][:, :, :], 0.5, g[:, KF:2 * KF], ALU.mult, ALU.mult
                                       ).then_inc(q.he_ok, 1)

    def down(pe, q, p, n, k):
        pe.wait_ge(q.he_ok, n + 1)
        if later(n):
            pe.wait_ge(q.outa_ok, n)
            pe.wait_ge(q.outb_ok, n)
        for c in range(2):
            for f in range(KF):
                ins = nc.tensor.matmul(ps[0:C, 4 + 2 * p + c, :], he[p][:, f, :],
                                       b.slots[k][2][:, f, c * 512:c * 512 + 512], start=(f == 0), stop=(f == KF - 1))
        ins.then_inc(q.down_ok, 1)

    def weight(e):
        return b.slot_w[:, bass.ds(e, 1)]

    def weigh_a(act, q, p, n, e):
        act.wait_ge(q.down_ok, n + 1)
        if later(n):
            act.wait_ge(q.scattered, 16 * n)
        nc.scalar.activation(out[p][:, 0:512], ps[0:C, 4 + 2 * p, :], ACT.Copy, scale=weight(e)
                             ).then_inc(q.outa_ok, 1)

    def weigh_b(dve, q, p, n, e):
        dve.wait_ge(q.down_ok, n + 1)
        if later(n):
            dve.wait_ge(q.scattered, 16 * n)
        nc.vector.tensor_scalar(out[p][:, 512:D], ps[0:C, 5 + 2 * p, :], weight(e), None, ALU.mult
                                ).then_inc(q.outb_ok, 1)

    def block_of(j, i=0):
        x = Shared()
        x.e, x.p, x.n, x.k, x.r, x.q = 4 * i + j, j % 2, 2 * i + j // 2, j % 4, i + j // 4, main[j % 2]
        x.last, x.last_n = main[1 - j % 2], 2 * i + (j + 1) // 2
        return x

    def staggered(eng, front, mid, back):
        front(block_of(0))
        front(block_of(1))
        mid(block_of(0))
        for j in range(4):
            front(block_of(j + 2))
            mid(block_of(j + 1))
            back(block_of(j))
        with eng.Fori(1, 7) as i:
            for j in range(4):
                front(block_of(j + 2, i))
                mid(block_of(j + 1, i))
                back(block_of(j, i))
        for e in (30, 31):
            front(block_of(e))
            mid(block_of(e - 1))
            back(block_of(e - 2))
        mid(block_of(31))
        back(block_of(30))
        back(block_of(31))

    def further(eng, body):
        count = eng.to_reg(eng.value_load(b.ove[0:1, OV:OV + 1], min_val=0, max_val=OV))

        def both(n):
            for p in range(2):
                with eng.If_lt(eng.to_reg(2 * n + p), count):
                    body(2 * n + p, p, n)

        both(0)
        with eng.Fori(1, OV // 2) as n:
            both(n)
        with eng.If_lt(eng.to_reg(OV - 1), count):
            body(OV - 1, 0, OV // 2)

    def nothing(x):
        pass

    with nc.Block() as block:
        @block.sync
        def _(sp):
            with sp.Fori(0, 7) as i:
                for k in range(4):
                    sp.wait_ge(main[k % 2].down_ok, 2 * i + k // 2 + 1)
                    load_expert(sp, b, io, 4 * i + 4 + k, k)

            def body(v, p, n):
                if later(n):
                    sp.wait_ge(more[p].down_ok, n)
                else:
                    sp.wait_ge(main[p].down_ok, NE // 2 - 1)
                e = sp.value_load(b.ove[0:1, bass.ds(v, 1)], min_val=0, max_val=NE - 1)
                load_expert(sp, b, io, e, p, more_w[p])
            further(sp, body)

        @block.gpsimd
        def _(pool):
            for k in range(4):
                gather(pool, k, k, gathered[k])
            count = pool.to_reg(pool.value_load(b.ove[0:1, OV:OV + 1], min_val=0, max_val=OV))
            for e in range(NE):
                x = block_of(e)
                if e < NE - 2:
                    pool.wait_ge(x.q.turned, x.n + 1)
                if e + 4 < NE:
                    gather(pool, x.k, e + 4, gathered[x.k])
                elif e < NE - 2:
                    with pool.If_lt(pool.to_reg(x.k), count):
                        gather(pool, x.k, e + 4, more_gathered[x.k])
                scatter(pool, x.q, x.p, x.n, e)
            for p in range(2):
                pool.wait_ge(main[p].scattered, 16 * (NE // 2))
            for v in range(OV):
                p, n = v % 2, v // 2
                if v + 2 < OV:
                    with pool.If_lt(pool.to_reg(v + 2), count):
                        pool.wait_ge(more[p].turned, n + 1)
                        gather(pool, p, NE + v + 2, more_gathered[p])
                with pool.If_lt(pool.to_reg(v), count):
                    scatter(pool, more[p], p, n, NE + v)
                    pool.wait_ge(more[p].scattered, 16 * (n + 1))

        @block.scalar
        def _(act):
            def back(x):
                weigh_a(act, x.q, x.p, x.n, x.e)
            staggered(act, lambda x: copy_turned(act, x.q, x.p, x.n), lambda x: tanh(act, x.q, x.p, x.n), back)

            for p in range(2):
                act.wait_ge(main[p].gu_ok, NE // 2)
                act.wait_ge(main[p].scattered, 16 * (NE // 2))

            def body(v, p, n):
                copy_turned(act, more[p], p, n)
                tanh(act, more[p], p, n)
                weigh_a(act, more[p], p, n, NE + v)
            further(act, body)

        @block.vector
        def _(dve):
            staggered(dve, nothing, lambda x: swiglu(dve, x.q, x.p, x.n),
                      lambda x: weigh_b(dve, x.q, x.p, x.n, x.e))

            for p in range(2):
                dve.wait_ge(main[p].scattered, 16 * (NE // 2))

            def body(v, p, n):
                swiglu(dve, more[p], p, n)
                weigh_b(dve, more[p], p, n, NE + v)
            further(dve, body)

        @block.tensor
        def _(pe):
            def front(x):
                if later(x.last_n):
                    pe.wait_ge(x.last.xt_ok, 2 * x.last_n)
                pe.wait_ge(gathered[x.k], 16 * (x.r + 1))
                turn(pe, x.q, x.k)

            def mid(x):
                pe.wait_ge(b.w_landed[x.k], 48 * (x.r + 1))
                gate_up(pe, x.q, x.p, x.n, x.k)

            staggered(pe, front, mid, lambda x: down(pe, x.q, x.p, x.n, x.k))
            for p in range(2):
                pe.wait_ge(main[p].outa_ok, NE // 2)
                pe.wait_ge(main[p].outb_ok, NE // 2)

            def body(v, p, n):
                pe.wait_ge(more_gathered[p], 16 * (n + 1))
                turn(pe, more[p], p)
                pe.wait_ge(more_w[p], 48 * (n + 1))
                gate_up(pe, more[p], p, n, p)
                down(pe, more[p], p, n, p)
            further(pe, body)


def final_stage(nc, m, s, b, io):
    m.at = b.R2
    y0 = [m.place(f"y0_{t}", [P, D]) for t in range(TILES)]
    y1 = [m.place(f"y1_{t}", [P, D]) for t in range(TILES)]
    wn = m.place("wn", [P, D])
    w_in, e_in, add0, x2_ok, sq, ln, rs, o_ok, left = (
        s("wn_in"), s.pair("ye_in", TILES), s("f_add"), s("x2_ok"), s("f_sq"), s("f_ln"), s("f_rs"), s("f_ok"),
        s("y_out"))

    def rows(t):
        return P if t < 8 else LAST

    with nc.Block() as block:
        @block.sync
        def _(sp):
            sp.dma_start(wn[:, :], io.norm_final.partition_broadcast(P)).then_inc(w_in, 16)
            for t in range(TILES):
                n = rows(t)
                sp.dma_start(y0[t][0:n, :], b.ye[t * P:t * P + n, :]).then_inc(e_in[t], 16)
                sp.dma_start(y1[t][0:n, :], b.ye[TOK + t * P:TOK + t * P + n, :]).then_inc(e_in[t], 16)

        @block.gpsimd
        def _(pool):
            for t in range(TILES):
                n = rows(t)
                pool.wait_ge(e_in[t], 32)
                nc.gpsimd.tensor_tensor(y0[t][0:n, :], y0[t][0:n, :], y1[t][0:n, :], ALU.add).then_inc(add0, 1)

        @block.scalar
        def _(act):
            nc.scalar.preload_act_table_set("natural_log_exp_and_others")

            def send(t):
                n = rows(t)
                act.wait_ge(o_ok, t + 1)
                act.dma_start(io.y[t * P:t * P + n, :], y1[t][0:n, :]).then_inc(left, 16)

            for t in range(TILES):
                n = rows(t)
                act.wait_ge(x2_ok, t + 1)
                nc.scalar.activation(y0[t][0:n, :], b.x1[0:n, t, :], ACT.Square, accum_out=b.stat[0:n, t, 0:1]
                                     ).then_inc(sq, 1)
                act.wait_ge(sq, t + 1)
                nc.scalar.activation(b.stat[0:n, t, 1:2], b.stat[0:n, t, 0:1], ACT.Ln, scale=1.0 / D,
                                     bias=b.eps[0:n, :]).then_inc(ln, 1)
                act.wait_ge(ln, t + 1)
                nc.scalar.activation(b.stat[0:n, t, 2:3], b.stat[0:n, t, 1:2], ACT.Exp, scale=-0.5).then_inc(rs, 1)
                if t >= 1:
                    send(t - 1)
            send(TILES - 1)
            act.wait_ge(left, 16 * TILES)

        @block.vector
        def _(dve):
            dve.wait_ge(w_in, 16)

            def scale(t):
                n = rows(t)
                dve.wait_ge(rs, t + 1)
                nc.vector.scalar_tensor_tensor(y1[t][0:n, :], b.x1[0:n, t, :], b.stat[0:n, t, 2:3], wn[0:n, :],
                                               ALU.mult, ALU.mult).then_inc(o_ok, 1)

            for t in range(TILES):
                n = rows(t)
                dve.wait_ge(add0, t + 1)
                nc.vector.tensor_tensor(b.x1[0:n, t, :], b.x1[0:n, t, :], y0[t][0:n, :], ALU.add).then_inc(x2_ok, 1)
                if t >= 1:
                    scale(t - 1)
            scale(TILES - 1)


def laid_out(inputs):
    import numpy as np

    a = {k: np.asarray(v) for k, v in inputs.items()}
    f = np.ascontiguousarray
    w_in = a["w_in"][0]
    blocks = w_in[:, :NBLK * P].reshape(KD, P, NBLK, P)
    order = [q for g in range(CA) for q in (CA + g, 2 * CA + g, g)] + list(range(3 * CA, NBLK))
    return {
        "x": f(np.concatenate([a["meta_tokens"], a["x_prompt"][0], a["x_sample"][:, 0]], axis=0)),
        "w_in": f(blocks[:, :, order].transpose(2, 1, 0, 3)),
        "w_ab": f(w_in[:, NBLK * P:].reshape(KD, P, 8).transpose(1, 0, 2)),
        "conv_a": f(a["conv_a_w"][0].reshape(KA, CA, P).transpose(2, 1, 0)),
        "conv_q": f(a["conv_qkv_w"][0].reshape(KQ, QKV, P).transpose(2, 1, 0)),
        "hist_a": f(a["state_conv_a"][0].reshape(SAMPLES, KA - 1, CA, P).transpose(3, 2, 0, 1)),
        "hist_q": f(a["state_conv_qkv"][0].reshape(SAMPLES, KQ - 1, QKV, P).transpose(3, 2, 0, 1)),
        "ssm": f(a["state_ssm"][0]),
        "a_log": f(a["a_log"][0]),
        "dt_bias": f(a["dt_bias"][0]),
        "o_norm": f(a["o_norm"][0].reshape(P, 1)),
        "norm_mix": f(a["norm_mix"][0]),
        "norm_ffn": f(a["norm_ffn"][0]),
        "norm_final": f(a["norm_final"]),
        "w_out": f(a["w_out"][0].reshape(KD, P, D).transpose(1, 0, 2)),
        "r_w": f(np.concatenate([a["router_group_w"][0], a["router_expert_w"][0]], axis=1)
                 .reshape(KD, P, GRP + NE).transpose(1, 0, 2)),
        "r_b": f(np.concatenate([a["router_group_b"][0], a["router_expert_b"][0]])),
        "w_gate": f(a["w_gate"][0]),
        "w_up": f(a["w_up"][0]),
        "w_down": f(a["w_down"][0]),
    }


OUTPUTS = {
    "y": (TOK, D),
    "new_hist": (P, CA + QKV, RLEN - PROMPT),
    "new_ssm_prompt": (H, P, P),
    "new_ssm_sample": (SAMPLES, H, P, P),
}


def kernel(**inputs):
    import concourse.bacc as bacc
    import numpy as np
    from concourse.bass_utils import run_bass_kernel_spmd

    arrays = laid_out(inputs)
    nc = bacc.Bacc("TRN2", target_bir_lowering=False, num_devices=1)
    args = {}
    for name, a in arrays.items():
        args[name] = nc.dram_tensor(name, a.shape, mybir.dt.from_np(a.dtype), kind="ExternalInput").ap()
    for name, shape in OUTPUTS.items():
        args[name] = nc.dram_tensor(name, shape, F32, kind="ExternalOutput").ap()
    build(nc, **args)
    r = run_bass_kernel_spmd(nc, [arrays], core_ids=[0]).results[0]
    y, hist = r["y"], r["new_hist"]
    ch = hist.transpose(2, 1, 0)
    ha = ch[:, :CA].reshape(-1, CA * P)
    hq = ch[:, CA:].reshape(-1, QKV * P)
    conv_a_sample = np.stack([ha[2 + KA * k + 1:2 + KA * k + KA] for k in range(SAMPLES)])
    conv_q_sample = np.stack([hq[3 + KQ * k + 1:3 + KQ * k + KQ] for k in range(SAMPLES)])
    return (y[None, META:PROMPT], y[PROMPT:, None], ha[None, None, 0:KA - 1], hq[None, None, 0:KQ - 1],
            r["new_ssm_prompt"][None, None], conv_a_sample[None], conv_q_sample[None], r["new_ssm_sample"][None])
```
